# Optimizing a Trainium2 kernel written in Bass

```python
import math
import jax, jax.numpy as jnp
from jax import lax
import numpy as np

D_MODEL = 1024
BATCH = 1
SEQ = 256
DEPTH = 2

PLE_DIM = 256
EPS = 1e-6
ROPE_THETA = 10000.0

CONV_WIDTH = D_MODEL // 2
CONV_K = 3
ATT_HEADS = 8
ATT_HEAD_DIM = 64
ATT_WIDTH = ATT_HEADS * ATT_HEAD_DIM
IDX_HEADS = 8
IDX_DIM = 64
IDX_ROPE_DIM = 32
TOPK_MAX = 256
Q_BLOCK = 128
DN_HEADS = 8
DN_DK = 128
DN_DV = 128
DN_CONV_K = 4
DN_CHUNK = 64
D_FF = -(-8 * D_MODEL // (3 * 256)) * 256

EVEN_SPLITS = (CONV_WIDTH, CONV_WIDTH, CONV_WIDTH, ATT_WIDTH, ATT_WIDTH, ATT_WIDTH, IDX_HEADS * IDX_DIM, IDX_DIM, IDX_HEADS)
EVEN_IN = sum(EVEN_SPLITS)
EVEN_MIX = CONV_WIDTH + ATT_WIDTH
DN_QKV = 2 * DN_HEADS * DN_DK + DN_HEADS * DN_DV
ODD_SPLITS = (DN_QKV, DN_HEADS * DN_DV, DN_HEADS, DN_HEADS)
ODD_IN = sum(ODD_SPLITS)
ODD_MIX = DN_HEADS * DN_DV
N_EVEN = (DEPTH + 1) // 2
N_ODD = DEPTH // 2


def split_cols(z, sizes):
    return jnp.split(z, [int(c) for c in np.cumsum(sizes)[:-1]], axis=-1)

def rmsnorm(x, g):
    xf = x.astype(jnp.float32)
    y = xf * lax.rsqrt(jnp.mean(xf * xf, axis=-1, keepdims=True) + EPS)
    return (y * g.astype(jnp.float32)).astype(x.dtype)

def layernorm(x, g, b):
    xf = x.astype(jnp.float32)
    mu = jnp.mean(xf, axis=-1, keepdims=True)
    var = jnp.mean(jnp.square(xf - mu), axis=-1, keepdims=True)
    y = (xf - mu) * lax.rsqrt(var + EPS)
    return (y * g.astype(jnp.float32) + b.astype(jnp.float32)).astype(x.dtype)

def l2norm(x):
    return x * lax.rsqrt(jnp.sum(x * x, axis=-1, keepdims=True) + EPS)

def rope_tables(positions, dim):
    inv_freq = 1.0 / (ROPE_THETA ** (jnp.arange(0, dim, 2, dtype=jnp.float32) / dim))
    ang = positions.astype(jnp.float32)[..., None] * inv_freq
    return jnp.cos(ang), jnp.sin(ang)

def apply_rope(x, cos, sin):
    x1, x2 = jnp.split(x.astype(jnp.float32), 2, axis=-1)
    c = cos[:, :, None, :]
    s = sin[:, :, None, :]
    return jnp.concatenate([x1 * c - x2 * s, x1 * s + x2 * c], axis=-1).astype(x.dtype)

def partial_rope(x, cos, sin):
    return jnp.concatenate([apply_rope(x[..., :IDX_ROPE_DIM], cos, sin), x[..., IDX_ROPE_DIM:]], axis=-1)

def causal_dwconv(u, w):
    k, s = w.shape[0], u.shape[1]
    up = jnp.pad(u, ((0, 0), (k - 1, 0), (0, 0)))
    y = up[:, 0:s] * w[0]
    for j in range(1, k):
        y = y + up[:, j:j + s] * w[j]
    return y

def dsa_attention(q, k, v, qi, ki, wi):
    b_, s_, _, dh = q.shape
    topk = min(TOPK_MAX, s_ // 4)
    nb = s_ // Q_BLOCK
    key_pos = jnp.arange(s_)
    wi = wi * (IDX_HEADS ** -0.5 * IDX_DIM ** -0.5)

    def to_blocks(t):
        return jnp.swapaxes(t.reshape(b_, nb, Q_BLOCK, *t.shape[2:]), 0, 1)

    def block(args):
        qb, qib, wib, start = args
        qpos = start + jnp.arange(Q_BLOCK)
        causal = key_pos[None, :] <= qpos[:, None]
        rel = jax.nn.relu(jnp.einsum('bqhd,bkd->bqhk', qib, ki).astype(jnp.float32))
        score = jnp.einsum('bqhk,bqh->bqk', rel, wib.astype(jnp.float32))
        score = jnp.where(causal[None], score, -jnp.inf)
        _, idx = lax.top_k(score, topk)
        valid = idx <= qpos[None, :, None]
        kg = jax.vmap(lambda kk, ii: kk[ii])(k, idx)
        vg = jax.vmap(lambda vv, ii: vv[ii])(v, idx)
        logits = jnp.einsum('bqhd,bqnhd->bhqn', qb, kg).astype(jnp.float32) * (dh ** -0.5)
        logits = jnp.where(valid[:, None], logits, -jnp.inf)
        prob = jax.nn.softmax(logits, axis=-1)
        return jnp.einsum('bhqn,bqnhd->bqhd', prob.astype(vg.dtype), vg)

    starts = jnp.arange(nb, dtype=jnp.int32) * Q_BLOCK
    out = lax.map(block, (to_blocks(q), to_blocks(qi), to_blocks(wi), starts))
    return jnp.swapaxes(out, 0, 1).reshape(b_, s_, q.shape[2], dh)

def conv_dsa_mixer(h, cos_a, sin_a, cos_i, sin_i, w_in, conv_w, q_norm_g, k_norm_g, ik_ln_g, ik_ln_b, w_out):
    b_, s_, _ = h.shape
    zb, zc, zh, q, k, v, qi, ki, wi = split_cols(h @ w_in, EVEN_SPLITS)
    y_a = zb * causal_dwconv(zc * zh, conv_w)
    heads = lambda t: t.reshape(b_, s_, ATT_HEADS, ATT_HEAD_DIM)
    q = apply_rope(rmsnorm(heads(q), q_norm_g), cos_a, sin_a)
    k = apply_rope(rmsnorm(heads(k), k_norm_g), cos_a, sin_a)
    v = heads(v)
    qi = partial_rope(qi.reshape(b_, s_, IDX_HEADS, IDX_DIM), cos_i, sin_i)
    ki = partial_rope(layernorm(ki, ik_ln_g, ik_ln_b)[:, :, None, :], cos_i, sin_i)[:, :, 0, :]
    y_b = dsa_attention(q, k, v, qi, ki, wi).reshape(b_, s_, ATT_WIDTH)
    return jnp.concatenate([y_a, y_b], axis=-1) @ w_out

def gated_delta_rule(q, k, v, g, beta):
    b_, s_, h_, dk = q.shape
    dv = v.shape[-1]
    c = DN_CHUNK
    n = s_ // c
    q = l2norm(q) * (dk ** -0.5)
    k = l2norm(k)

    def chunks(t):
        t = jnp.moveaxis(t, 2, 1)
        return t.reshape(b_, h_, n, c, *t.shape[3:])

    q, k, v, g, beta = chunks(q), chunks(k), chunks(v), chunks(g), chunks(beta)
    g = jnp.cumsum(g, axis=-1)
    tril = jnp.tril(jnp.ones((c, c), bool))
    strict = jnp.tril(jnp.ones((c, c), bool), -1)
    decay = jnp.exp(jnp.where(tril, g[..., :, None] - g[..., None, :], -jnp.inf))
    kb = k * beta[..., None]
    vb = v * beta[..., None]
    m = jnp.where(strict, jnp.einsum('bhncd,bhnsd->bhncs', kb, k) * decay, 0.0)
    eye = jnp.eye(c, dtype=q.dtype)
    t_inv = lax.linalg.triangular_solve(eye + m, jnp.broadcast_to(eye, m.shape), left_side=True, lower=True, unit_diagonal=True)
    u = t_inv @ vb
    w = t_inv @ (kb * jnp.exp(g)[..., None])
    qk = jnp.where(tril, jnp.einsum('bhncd,bhnsd->bhncs', q, k) * decay, 0.0)

    def step(state, xs):
        q_c, k_c, u_c, w_c, g_c, qk_c = xs
        v_new = u_c - w_c @ state
        o = (q_c * jnp.exp(g_c)[..., None]) @ state + qk_c @ v_new
        g_last = g_c[..., -1]
        k_dec = k_c * jnp.exp(g_last[..., None] - g_c)[..., None]
        state = state * jnp.exp(g_last)[..., None, None] + jnp.einsum('bhcd,bhce->bhde', k_dec, v_new)
        return state, o

    xs = tuple(jnp.moveaxis(t, 2, 0) for t in (q, k, u, w, g, qk))
    state0 = jnp.zeros((b_, h_, dk, dv), q.dtype)
    _, o = lax.scan(step, state0, xs)
    o = jnp.moveaxis(o, 0, 2).reshape(b_, h_, s_, dv)
    return jnp.moveaxis(o, 1, 2)

def gated_deltanet_mixer(h, w_in, conv_w, a_log, dt_bias, o_norm_g, w_out):
    b_, s_, _ = h.shape
    qkv, z, a, bt = split_cols(h @ w_in, ODD_SPLITS)
    qkv = jax.nn.silu(causal_dwconv(qkv, conv_w))
    q, k, v = split_cols(qkv, (DN_HEADS * DN_DK, DN_HEADS * DN_DK, DN_HEADS * DN_DV))
    f32 = jnp.float32
    q = q.reshape(b_, s_, DN_HEADS, DN_DK).astype(f32)
    k = k.reshape(b_, s_, DN_HEADS, DN_DK).astype(f32)
    v = v.reshape(b_, s_, DN_HEADS, DN_DV).astype(f32)
    g = -jnp.exp(a_log.astype(f32)) * jax.nn.softplus(a.astype(f32) + dt_bias.astype(f32))
    beta = jax.nn.sigmoid(bt.astype(f32))
    o = gated_delta_rule(q, k, v, g, beta)
    o = rmsnorm(o, o_norm_g) * jax.nn.silu(z.reshape(b_, s_, DN_HEADS, DN_DV).astype(f32))
    return o.reshape(b_, s_, ODD_MIX).astype(h.dtype) @ w_out

def swiglu(h, w_gate, w_up, w_down):
    return (jax.nn.silu(h @ w_gate) * (h @ w_up)) @ w_down

def first_inputs(seed: int = 0) -> dict:
    key = jax.random.key(seed)
    k = jax.random.split(key, 25)
    f32 = jnp.float32
    nrm = lambda kk, shape, scale: jax.random.normal(kk, shape, f32) * scale
    gain = lambda kk, shape: 1.0 + 0.02 * jax.random.normal(kk, shape, f32)
    x = nrm(k[0], (BATCH, SEQ, D_MODEL), 1.0)
    p = nrm(k[1], (DEPTH, BATCH, SEQ, PLE_DIM), 1.0)
    offset = jax.random.randint(k[2], (BATCH, 1), 0, 4096, dtype=jnp.int32)
    positions = offset + jnp.arange(SEQ, dtype=jnp.int32)[None, :]
    norm_mix_g = gain(k[3], (DEPTH, D_MODEL))
    norm_ffn_g = gain(k[4], (DEPTH, D_MODEL))
    ev_w_in = nrm(k[5], (N_EVEN, D_MODEL, EVEN_IN), D_MODEL ** -0.5)
    ev_conv_w = nrm(k[6], (N_EVEN, CONV_K, CONV_WIDTH), CONV_K ** -0.5)
    ev_q_norm_g = gain(k[7], (N_EVEN, ATT_HEAD_DIM))
    ev_k_norm_g = gain(k[8], (N_EVEN, ATT_HEAD_DIM))
    ev_ik_ln_g = gain(k[9], (N_EVEN, IDX_DIM))
    ev_ik_ln_b = nrm(k[10], (N_EVEN, IDX_DIM), 0.02)
    ev_w_out = nrm(k[11], (N_EVEN, EVEN_MIX, D_MODEL), 0.5 * EVEN_MIX ** -0.5)
    od_w_in = nrm(k[12], (N_ODD, D_MODEL, ODD_IN), D_MODEL ** -0.5)
    od_conv_w = nrm(k[13], (N_ODD, DN_CONV_K, DN_QKV), 0.5)
    dt = jnp.exp(jax.random.uniform(k[14], (N_ODD, DN_HEADS), f32, math.log(1e-3), math.log(1e-1)))
    od_dt_bias = dt + jnp.log(-jnp.expm1(-dt))
    od_a_log = jnp.log(jax.random.uniform(k[15], (N_ODD, DN_HEADS), f32, 1.0, 16.0))
    od_o_norm_g = gain(k[16], (N_ODD, DN_DV))
    od_w_out = nrm(k[17], (N_ODD, ODD_MIX, D_MODEL), 0.5 * ODD_MIX ** -0.5)
    ffn_w_gate = nrm(k[18], (DEPTH, D_MODEL, D_FF), D_MODEL ** -0.5)
    ffn_w_up = nrm(k[19], (DEPTH, D_MODEL, D_FF), D_MODEL ** -0.5)
    ffn_w_down = nrm(k[20], (DEPTH, D_FF, D_MODEL), 0.5 * D_FF ** -0.5)
    ple_w_proj = nrm(k[21], (DEPTH, PLE_DIM, D_MODEL), PLE_DIM ** -0.5)
    ple_post_norm_g = gain(k[22], (DEPTH, D_MODEL))
    ple_norm_g = gain(k[23], (DEPTH, D_MODEL))
    ple_w_gate = nrm(k[24], (DEPTH, D_MODEL, D_MODEL), D_MODEL ** -0.5)
    return {'x': x, 'p': p, 'positions': positions, 'norm_mix_g': norm_mix_g, 'norm_ffn_g': norm_ffn_g,
            'ev_w_in': ev_w_in, 'ev_conv_w': ev_conv_w, 'ev_q_norm_g': ev_q_norm_g, 'ev_k_norm_g': ev_k_norm_g,
            'ev_ik_ln_g': ev_ik_ln_g, 'ev_ik_ln_b': ev_ik_ln_b, 'ev_w_out': ev_w_out,
            'od_w_in': od_w_in, 'od_conv_w': od_conv_w, 'od_a_log': od_a_log, 'od_dt_bias': od_dt_bias,
            'od_o_norm_g': od_o_norm_g, 'od_w_out': od_w_out,
            'ffn_w_gate': ffn_w_gate, 'ffn_w_up': ffn_w_up, 'ffn_w_down': ffn_w_down,
            'ple_w_proj': ple_w_proj, 'ple_post_norm_g': ple_post_norm_g, 'ple_norm_g': ple_norm_g, 'ple_w_gate': ple_w_gate}

def first_block(x, p, positions, norm_mix_g, norm_ffn_g, ev_w_in, ev_conv_w, ev_q_norm_g, ev_k_norm_g, ev_ik_ln_g, ev_ik_ln_b, ev_w_out, od_w_in, od_conv_w, od_a_log, od_dt_bias, od_o_norm_g, od_w_out, ffn_w_gate, ffn_w_up, ffn_w_down, ple_w_proj, ple_post_norm_g, ple_norm_g, ple_w_gate):
    cos_a, sin_a = rope_tables(positions, ATT_HEAD_DIM)
    cos_i, sin_i = rope_tables(positions, IDX_ROPE_DIM)
    h = x
    for i in range(DEPTH):
        j = i // 2
        hn = rmsnorm(h, norm_mix_g[i])
        if i % 2 == 0:
            h = h + conv_dsa_mixer(hn, cos_a, sin_a, cos_i, sin_i, ev_w_in[j], ev_conv_w[j], ev_q_norm_g[j],
                                   ev_k_norm_g[j], ev_ik_ln_g[j], ev_ik_ln_b[j], ev_w_out[j])
        else:
            h = h + gated_deltanet_mixer(hn, od_w_in[j], od_conv_w[j], od_a_log[j], od_dt_bias[j],
                                         od_o_norm_g[j], od_w_out[j])
        h = h + swiglu(rmsnorm(h, norm_ffn_g[i]), ffn_w_gate[i], ffn_w_up[i], ffn_w_down[i])
        e = rmsnorm(p[i] @ ple_w_proj[i], ple_post_norm_g[i])
        h = h + e * jax.nn.sigmoid(rmsnorm(h, ple_norm_g[i]) @ ple_w_gate[i])
    return h


GRID_W = 64
CTX_LEN = 256

MIX_WIDTH = D_MODEL
FOURIER_WIDTH = MIX_WIDTH // 4
N_FOURIER_HEADS = 4
FOURIER_HEAD_DIM = FOURIER_WIDTH // N_FOURIER_HEADS
POOL_WIDTH = MIX_WIDTH // 4
POOL_WINDOWS = (2, 4, 8, 16)
POOL_GROUP_DIM = POOL_WIDTH // len(POOL_WINDOWS)
ATTN_WIDTH = MIX_WIDTH // 2
HEAD_DIM = 128
N_Q_HEADS = ATTN_WIDTH // HEAD_DIM
N_KV_HEADS = 2
Q_PER_KV = N_Q_HEADS // N_KV_HEADS
KV_WIDTH = N_KV_HEADS * HEAD_DIM
ROPE_HALF = HEAD_DIM // 2

F_OFF = 0
P_OFF = F_OFF + FOURIER_WIDTH
Q_OFF = P_OFF + POOL_WIDTH
K_OFF = Q_OFF + ATTN_WIDTH
V_OFF = K_OFF + KV_WIDTH
IN_WIDTH = V_OFF + KV_WIDTH

N_EXPERTS = 16
EC_CAPACITY_FACTOR = 2
EXPERT_FF = D_MODEL


def rms_norm(x, g):
    xf = x.astype(jnp.float32)
    y = xf * lax.rsqrt(jnp.mean(xf * xf, axis=-1, keepdims=True) + EPS)
    return (y * g.astype(jnp.float32)).astype(x.dtype)

def modulate(x, g, shift, scale):
    xf = x.astype(jnp.float32)
    y = xf * lax.rsqrt(jnp.mean(xf * xf, axis=-1, keepdims=True) + EPS) * g.astype(jnp.float32)
    y = y * (1.0 + scale.astype(jnp.float32)) + shift.astype(jnp.float32)
    return y.astype(x.dtype)

def axial_angles(n):
    rows = n // GRID_W
    row = jnp.repeat(jnp.arange(rows, dtype=jnp.float32), GRID_W)
    col = jnp.tile(jnp.arange(GRID_W, dtype=jnp.float32), rows)
    inv = ROPE_THETA ** (-jnp.arange(0, ROPE_HALF, 2, dtype=jnp.float32) / ROPE_HALF)
    return row[:, None] * inv[None, :], col[:, None] * inv[None, :]

def rope_half(x, ang):
    cos = jnp.cos(ang)[None, :, None, :]
    sin = jnp.sin(ang)[None, :, None, :]
    xf = x.astype(jnp.float32)
    x1, x2 = xf[..., : ROPE_HALF // 2], xf[..., ROPE_HALF // 2:]
    return jnp.concatenate([x1 * cos - x2 * sin, x2 * cos + x1 * sin], axis=-1).astype(x.dtype)

def axial_rope(x, ang_row, ang_col):
    return jnp.concatenate([rope_half(x[..., :ROPE_HALF], ang_row),
                            rope_half(x[..., ROPE_HALF:], ang_col)], axis=-1)

def attend(q, k, v):
    s = jnp.einsum('bqhgd,bkhd->bhgqk', q, k).astype(jnp.float32) * (HEAD_DIM ** -0.5)
    p = jax.nn.softmax(s, axis=-1).astype(v.dtype)
    return jnp.einsum('bhgqk,bkhd->bqhgd', p, v)

def blocked_attention(q, k, v):
    B, L = q.shape[0], q.shape[1]
    nb = L // Q_BLOCK
    qb = q.reshape(B, nb, Q_BLOCK, N_KV_HEADS, Q_PER_KV, HEAD_DIM).transpose(1, 0, 2, 3, 4, 5)
    ob = lax.map(lambda qi: attend(qi, k, v), qb)
    return ob.transpose(1, 0, 2, 3, 4, 5).reshape(B, L, ATTN_WIDTH)

def fourier_mix(f, w):
    B, n, _ = f.shape
    fh = f.astype(jnp.float32).reshape(B, n, N_FOURIER_HEADS, FOURIER_HEAD_DIM).transpose(0, 2, 1, 3)
    fr = jnp.real(jnp.fft.fft2(fh, axes=(-2, -1), norm="ortho"))
    fr = fr.transpose(0, 2, 1, 3).reshape(B, n, FOURIER_WIDTH).astype(f.dtype)
    return fr @ w

def pool_mix(p, w, scale):
    B, n, _ = p.shape
    pf = p.astype(jnp.float32)
    cs = jnp.concatenate([jnp.zeros((B, 1, POOL_WIDTH), jnp.float32), jnp.cumsum(pf, axis=1)], axis=1)
    t = jnp.arange(n)
    outs = []
    for gi, win in enumerate(POOL_WINDOWS):
        lo = jnp.clip(t - win // 2, 0, n)
        hi = jnp.clip(t + win // 2, 0, n)
        sl = slice(gi * POOL_GROUP_DIM, (gi + 1) * POOL_GROUP_DIM)
        csg = cs[..., sl]
        s = jnp.take(csg, hi, axis=1) - jnp.take(csg, lo, axis=1)
        cnt = (hi - lo).astype(jnp.float32)[None, :, None]
        outs.append(s / cnt - pf[..., sl])
    d = jnp.stack(outs, axis=2).astype(p.dtype)
    y = jnp.einsum('bngc,gcd->bngd', d, w).reshape(B, n, POOL_WIDTH)
    return y * scale

def expert_choice_ffn(h, w_router, w_gate, w_up, w_down):
    B, n, D = h.shape
    cap = EC_CAPACITY_FACTOR * n // N_EXPERTS
    logits = jnp.einsum('bnd,de->bne', h, w_router).astype(jnp.float32)
    aff = jax.nn.softmax(logits, axis=-1)
    g, idx = lax.top_k(aff.transpose(0, 2, 1), cap)
    xs = jax.vmap(lambda hb, ib: hb[ib])(h, idx)
    a = jnp.einsum('becd,edf->becf', xs, w_gate)
    u = jnp.einsum('becd,edf->becf', xs, w_up)
    y = jnp.einsum('becf,efd->becd', jax.nn.silu(a) * u, w_down)
    y = y * g[..., None].astype(y.dtype)
    return jax.vmap(lambda yb, ib: jnp.zeros((n, D), yb.dtype).at[ib.reshape(-1)].add(yb.reshape(-1, D)))(y, idx)

def second_inputs(seed: int = 0) -> dict:
    key = jax.random.key(seed)
    ks = jax.random.split(key, 20)
    nrm = jax.random.normal
    f32 = jnp.float32
    D = D_MODEL
    return {
        "x": nrm(ks[0], (BATCH, SEQ, D), f32),
        "c": nrm(ks[1], (BATCH, D), f32),
        "ctx": nrm(ks[2], (BATCH, CTX_LEN, D), f32),
        "c_ctx": nrm(ks[3], (D,), f32),
        "ada_w": nrm(ks[4], (DEPTH, D, 6 * D), f32) * (0.5 * D ** -0.5),
        "ada_b": nrm(ks[5], (DEPTH, 6 * D), f32) * 0.02,
        "norm1_g": 1.0 + 0.02 * nrm(ks[6], (DEPTH, D), f32),
        "norm2_g": 1.0 + 0.02 * nrm(ks[7], (DEPTH, D), f32),
        "w_in": nrm(ks[8], (DEPTH, D, IN_WIDTH), f32) * D ** -0.5,
        "w_fourier": nrm(ks[9], (DEPTH, FOURIER_WIDTH, FOURIER_WIDTH), f32) * FOURIER_WIDTH ** -0.5,
        "w_pool": nrm(ks[10], (DEPTH, len(POOL_WINDOWS), POOL_GROUP_DIM, POOL_GROUP_DIM), f32) * POOL_GROUP_DIM ** -0.5,
        "pool_scale": 1.0 + 0.1 * nrm(ks[11], (DEPTH, POOL_WIDTH), f32),
        "q_norm_g": 1.0 + 0.02 * nrm(ks[12], (DEPTH, HEAD_DIM), f32),
        "k_norm_g": 1.0 + 0.02 * nrm(ks[13], (DEPTH, HEAD_DIM), f32),
        "w_out": nrm(ks[14], (DEPTH, MIX_WIDTH, D), f32) * MIX_WIDTH ** -0.5,
        "w_router": nrm(ks[15], (DEPTH, D, N_EXPERTS), f32) * D ** -0.5,
        "w_gate": nrm(ks[16], (DEPTH, N_EXPERTS, D, EXPERT_FF), f32) * D ** -0.5,
        "w_up": nrm(ks[17], (DEPTH, N_EXPERTS, D, EXPERT_FF), f32) * D ** -0.5,
        "w_down": nrm(ks[18], (DEPTH, N_EXPERTS, EXPERT_FF, D), f32) * EXPERT_FF ** -0.5,
    }

def second_block(x, c, ctx, c_ctx, ada_w, ada_b, norm1_g, norm2_g, w_in, w_fourier, w_pool, pool_scale,
              q_norm_g, k_norm_g, w_out, w_router, w_gate, w_up, w_down):
    B, L, D = x.shape
    Lc = ctx.shape[1]
    ang_row, ang_col = axial_angles(L)
    sc = jax.nn.silu(c)
    scc = jax.nn.silu(c_ctx)
    for i in range(DEPTH):
        last = i == DEPTH - 1
        sh1, sc1, g1, sh2, sc2, g2 = jnp.split((sc @ ada_w[i] + ada_b[i])[:, None, :], 6, axis=-1)
        csh1, csc1, cg1, csh2, csc2, cg2 = jnp.split((scc @ ada_w[i] + ada_b[i])[None, None, :], 6, axis=-1)

        hx = modulate(x, norm1_g[i], sh1, sc1)
        hc = modulate(ctx, norm1_g[i], csh1, csc1)
        px_all = hx @ w_in[i]
        kvc = hc @ w_in[i][:, K_OFF:]
        kc = rms_norm(kvc[..., :KV_WIDTH].reshape(B, Lc, N_KV_HEADS, HEAD_DIM), k_norm_g[i])
        vc = kvc[..., KV_WIDTH:].reshape(B, Lc, N_KV_HEADS, HEAD_DIM)

        qx = rms_norm(px_all[..., Q_OFF:K_OFF].reshape(B, L, N_Q_HEADS, HEAD_DIM), q_norm_g[i])
        kx = rms_norm(px_all[..., K_OFF:V_OFF].reshape(B, L, N_KV_HEADS, HEAD_DIM), k_norm_g[i])
        vx = px_all[..., V_OFF:].reshape(B, L, N_KV_HEADS, HEAD_DIM)
        qx = axial_rope(qx, ang_row, ang_col)
        kx = axial_rope(kx, ang_row, ang_col)
        k_all = jnp.concatenate([kx, kc], axis=1)
        v_all = jnp.concatenate([vx, vc], axis=1)
        ax = blocked_attention(qx, k_all, v_all)
        ox = jnp.concatenate([fourier_mix(px_all[..., F_OFF:P_OFF], w_fourier[i]),
                              pool_mix(px_all[..., P_OFF:Q_OFF], w_pool[i], pool_scale[i]),
                              ax], axis=-1) @ w_out[i]
        x_new = x + g1 * ox

        x_new = x_new + g2 * expert_choice_ffn(modulate(x_new, norm2_g[i], sh2, sc2),
                                               w_router[i], w_gate[i], w_up[i], w_down[i])

        if not last:
            pc_all = hc @ w_in[i][:, :K_OFF]
            qc = rms_norm(pc_all[..., Q_OFF:K_OFF].reshape(B, Lc, N_KV_HEADS, Q_PER_KV, HEAD_DIM), q_norm_g[i])
            ac = attend(qc, kc, vc).reshape(B, Lc, ATTN_WIDTH)
            oc = jnp.concatenate([fourier_mix(pc_all[..., F_OFF:P_OFF], w_fourier[i]),
                                  pool_mix(pc_all[..., P_OFF:Q_OFF], w_pool[i], pool_scale[i]),
                                  ac], axis=-1) @ w_out[i]
            ctx = ctx + cg1 * oc
            ctx = ctx + cg2 * expert_choice_ffn(modulate(ctx, norm2_g[i], csh2, csc2),
                                                w_router[i], w_gate[i], w_up[i], w_down[i])
        x = x_new
    return x


def setup_inputs(seed=0):
    out = dict(first_inputs(seed))
    for name, value in second_inputs(seed + 1).items():
        if name != "x":
            out[name + "_2"] = value
    return out


def reference(
    x, p, positions, norm_mix_g, norm_ffn_g, ev_w_in, ev_conv_w, ev_q_norm_g, ev_k_norm_g,
    ev_ik_ln_g, ev_ik_ln_b, ev_w_out, od_w_in, od_conv_w, od_a_log, od_dt_bias, od_o_norm_g,
    od_w_out, ffn_w_gate, ffn_w_up, ffn_w_down, ple_w_proj, ple_post_norm_g, ple_norm_g,
    ple_w_gate, c_2, ctx_2, c_ctx_2, ada_w_2, ada_b_2, norm1_g_2, norm2_g_2, w_in_2,
    w_fourier_2, w_pool_2, pool_scale_2, q_norm_g_2, k_norm_g_2, w_out_2, w_router_2, w_gate_2,
    w_up_2, w_down_2,
):
    x = first_block(
        x, p, positions, norm_mix_g, norm_ffn_g, ev_w_in, ev_conv_w, ev_q_norm_g, ev_k_norm_g,
        ev_ik_ln_g, ev_ik_ln_b, ev_w_out, od_w_in, od_conv_w, od_a_log, od_dt_bias, od_o_norm_g,
        od_w_out, ffn_w_gate, ffn_w_up, ffn_w_down, ple_w_proj, ple_post_norm_g, ple_norm_g,
        ple_w_gate,
    )
    return second_block(
        x, c_2, ctx_2, c_ctx_2, ada_w_2, ada_b_2, norm1_g_2, norm2_g_2, w_in_2, w_fourier_2,
        w_pool_2, pool_scale_2, q_norm_g_2, k_norm_g_2, w_out_2, w_router_2, w_gate_2, w_up_2,
        w_down_2,
    )


_drawn_inputs = setup_inputs


def setup_inputs(seed=0):
    import zlib

    import numpy as np

    out = dict(_drawn_inputs(seed))
    spreads = {}
    factors = {'norm_mix_g': 3.418,
     'norm_ffn_g': 5.142,
     'ev_q_norm_g': 8.0,
     'ev_k_norm_g': 8.0,
     'ev_ik_ln_g': 7.858,
     'ev_ik_ln_b': 8.0,
     'od_a_log': 2.848,
     'od_o_norm_g': 8.0,
     'ple_post_norm_g': 4.436,
     'ple_norm_g': 8.0,
     'ctx_2': 4.733,
     'ada_b_2': 3.318,
     'norm1_g_2': 8.0,
     'norm2_g_2': 8.0,
     'pool_scale_2': 3.663,
     'q_norm_g_2': 8.0,
     'k_norm_g_2': 8.0}
    for name, (base, spread) in spreads.items():
        noise = np.random.default_rng([zlib.crc32(name.encode()), seed]).standard_normal(out[name].shape)
        drawn = base * np.exp(spread * noise) if base else spread * noise
        out[name] = __import__('jax').numpy.asarray(drawn.astype(out[name].dtype))
    for name, factor in factors.items():
        out[name] = (out[name] * factor).astype(out[name].dtype)
    return out
```

```python
from contextlib import ExitStack

import numpy as np
import concourse.bass as bass
from concourse import mybir

F32 = mybir.dt.float32
I32 = mybir.dt.int32
ALU = mybir.AluOpType
ACT = mybir.ActivationFunctionType
AX = mybir.AxisListType

D = 1024
EPS = 1e-6
BIG = 1e30
TAKEN = -3e38
RING = 5
SLOT = 4096
NE = 16
CAP = 32
MAGIC = 12582912.0
TWO_PI_A = 6.28125
TWO_PI_B = 0.00193500518798828125
TWO_PI_C = float(2 * np.pi - 6.28125 - 0.00193500518798828125)

SMALL = [
    ("xtiny", 2), ("norm_mix", 16), ("norm_ffn", 16), ("ple_post", 16), ("ple_norm", 16),
    ("ev_conv", 12), ("od_conv", 96), ("ev_qg", 64), ("ev_kg", 64), ("ln_g", 64), ("ln_b", 64),
    ("o_g", 128), ("a_log", 8), ("dt_bias", 8),
    ("c2", 16), ("ada_b", 96), ("n1", 16), ("n2", 16), ("pool_scale", 4),
    ("qg", 256), ("kg", 256), ("w_pool", 256), ("w_router", 256),
    ("ident", 128), ("ones", 128), ("invf", 48), ("tri", 128), ("iota", 32),
    ("rcos", 128), ("rsin", 128), ("levels", 768), ("cumT", 128), ("lastT", 128),
    ("sel", 256), ("dmask", 128),
]
OFF = {}
_at = 0
for _n, _w in SMALL:
    OFF[_n] = (_at, _w)
    _at += _w
NSMALL = _at


class Queues:

    def __init__(self, nc, ctx):
        self.nc, self.ctx = nc, ctx
        self.eng = {"pe": nc.tensor, "act": nc.scalar, "dve": nc.vector, "pool": nc.gpsimd, "sp": nc.sync}
        self.sem = {n: ctx.enter_context(nc.semaphore("s_" + n)) for n in self.eng}
        self.count = {n: 0 for n in self.sem}
        self.seen = {n: {} for n in self.eng}
        self.mm_last = None

    def new_sem(self, name):
        self.sem[name] = self.ctx.enter_context(self.nc.semaphore(name))
        self.count[name] = 0
        return name

    def put(self, eng, fn, after=(), inc=None, by=1):
        e = self.eng[eng]
        for t in after:
            if t is None:
                continue
            name, value = t
            if self.seen[eng].get(name, 0) < value:
                self.seen[eng][name] = value
                e.wait_ge(self.sem[name], value)
        ins = fn(e)
        if inc:
            ins.then_inc(self.sem[inc], by)
            self.count[inc] += by
            return inc, self.count[inc]
        self.mm_last = ins
        return None

    def mm(self, out, lhsT, rhs, start, stop, after=(), skip=False):
        self.put("pe", lambda e: e.matmul(out, lhsT, rhs, start=start, stop=stop, skip_group_check=skip), after)

    def tr(self, out, in_, ident, after=()):
        self.put("pe", lambda e: e.transpose(out, in_, ident), after)

    def pe_done(self):
        if self.mm_last is not None:
            self.mm_last.then_inc(self.sem["pe"], 1)
            self.mm_last = None
            self.count["pe"] += 1
        return "pe", self.count["pe"]

    def _one(self, eng, fn, after):
        prev = (eng, self.count[eng])
        return self.put(eng, fn, (prev,) + tuple(after), eng)

    def v(self, fn, *after):
        return self._one("dve", fn, after)

    def a(self, fn, *after):
        return self._one("act", fn, after)

    def g(self, fn, *after):
        return self._one("pool", fn, after)

    def last(self, eng):
        return (eng, self.count[eng])

    def dma(self, eng, out, in_, sem, after=()):
        return self.put(eng, lambda e: e.dma_start(out, in_), after, sem, 16)


class Banks:

    def __init__(self, nc, ctx):
        self.bank = [ctx.enter_context(nc.psum_tensor(f"ps{i}", [128, 512], F32)) for i in range(8)]
        self.idle = [(i, None) for i in range(8)]

    def take(self):
        i, tok = self.idle.pop(0)
        return i, self.bank[i], tok

    def free(self, i, tok):
        self.idle.append((i, tok))


class Chunk:
    def __init__(self, ring, i, ap, tok):
        self.ring, self.i, self.ap, self.tok = ring, i, ap, tok

    def done(self, tok):
        self.ring.released[self.i] = tok


class Ring:

    def __init__(self, nc, ctx, Q):
        self.Q = Q
        self.buf = ctx.enter_context(nc.sbuf_tensor("ring", [128, RING, SLOT], F32))
        for i in range(RING):
            Q.new_sem(f"ring{i}")
        self.n = 0
        self.released = {}

    def load(self, srcs):
        i = self.n
        self.n += 1
        s = i % RING
        after = (self.released[i - RING],) if i >= RING else ()
        for src, off, width, m in srcs:
            dst = self.buf[:, s, off:off + width]
            if m > 1:
                dst = dst.rearrange("p (j f) -> p j f", j=m)
            tok = self.Q.dma("sp", dst, src, f"ring{s}", after)
        return Chunk(self, i, self.buf[:, s, :], tok)


def bc(ap, shape):
    return ap.to_broadcast(shape)


def program(nc, dr, out_dram, upto=99, dump=None):
    with ExitStack() as ctx:
        Q = Queues(nc, ctx)
        B = Banks(nc, ctx)
        R = Ring(nc, ctx, Q)

        def sb(name, n):
            return ctx.enter_context(nc.sbuf_tensor("m_" + name, [128, n], F32))

        small = sb("small", NSMALL)
        xT = sb("xT", 2048)
        cT = sb("cT", 2048)
        nT = sb("nT", 4096)
        wk = sb("wk", 2048)
        misc = sb("misc", 1152)
        SC = sb("scratch", 17280)
        posi = ctx.enter_context(nc.sbuf_tensor("posi", [128, 2], I32))

        def sm(name, a=0, b=None):
            o, w = OFF[name]
            return small[:, o + a:o + (w if b is None else b)]

        def sc(off, n):
            assert off + n <= 17280
            return SC[:, off:off + n]

        x8 = xT[:, :].rearrange("p (k t) -> p k t", k=8)
        c8 = cT[:, :].rearrange("p (k t) -> p k t", k=8)
        n8 = nT[:, 0:2048].rearrange("p (k t) -> p k t", k=8)
        n2 = nT[:, :].rearrange("p (k s t) -> p k s t", k=8, s=2)
        wk8 = wk[:, :].rearrange("p (k t) -> p k t", k=8)
        ident = sm("ident")
        ones = sm("ones")

        mo = [0]

        def mi(n):
            mo[0] += n
            assert mo[0] <= 1152
            return misc[:, mo[0] - n:mo[0]]

        dumps = []

        def dbg(name, ap, tok):
            if dump is not None:
                t = nc.dram_tensor("dbg_" + name, list(ap.shape), F32, kind="ExternalOutput").ap()
                w = Q.dma("pool", t, ap, Q.new_sem("dbg_" + name), tok)
                dump.append("dbg_" + name)
                Q.v(lambda e: e.memset(dummy, 0.0), w)
                Q.a(lambda e: e.activation(dummy[:, 0:1], dummy[:, 1:2], ACT.Copy), Q.last("dve"))
                Q.v(lambda e: e.memset(dummy, 0.0), Q.last("act"))

        s_out = Q.new_sem("s_out")
        dummy = misc[:, 1150:1152]

        s_in = Q.new_sem("s_in")
        half = (NSMALL // 2)
        Q.dma("act", xT[:, :], dr["xT"], s_in)
        Q.dma("act", small[:, 0:half], dr["small"][:, 0:half], s_in)
        Q.dma("act", small[:, half:NSMALL], dr["small"][:, half:NSMALL], s_in)
        t_in = Q.dma("act", posi[:, :], dr["posT"], s_in)

        def chunk(W, j0, m, kt):
            f = kt * 128
            if m == 1:
                return R.load([(W[j0], 0, f, 1)])
            return R.load([(W[j0:j0 + m].rearrange("j p f -> p j f"), 0, m * f, m)])

        def dense(W, tiles, kt, rhs, tok, consume, width=256, per=2):
            m = max(1, SLOT // (kt * 128))
            if m > per:
                m -= m % per
            i = 0
            held = None
            while i < len(tiles):
                k = min(m, len(tiles) - i)
                c = chunk(W, tiles[i], k, kt)
                for j in range(k):
                    g = (i + j) % per
                    if g == 0:
                        b, ps, bt = B.take()
                        held = (b, ps)
                    b, ps = held
                    for q in range(kt):
                        w = c.ap[:, (j * kt + q) * 128:(j * kt + q + 1) * 128]
                        Q.mm(ps[:, g * width:(g + 1) * width], w, rhs(q), q == 0, q == kt - 1,
                             (c.tok, bt) + tok if q == 0 else ())
                    if g == per - 1 or i + j == len(tiles) - 1:
                        pt = Q.pe_done()
                        rt = consume(ps, i + j - g, g + 1, pt)
                        B.free(b, rt)
                c.done(Q.pe_done())
                i += k

        def tokens(cap, kt, j0, m, lhs, tok, consume):
            b, ps, bt = B.take()
            f = kt * 128
            v = cap[:, j0 * f:(j0 + m) * f].rearrange("p (j k n) -> p j k n", j=m, k=kt)
            for q in range(kt):
                Q.mm(ps[:, 0:m * 128].rearrange("p (j n) -> p j n", j=m), lhs(q), v[:, :, q, :],
                     q == 0, q == kt - 1, (bt,) + tok if q == 0 else ())
            rt = consume(ps, Q.pe_done())
            B.free(b, rt)

        rr = mi(256)

        def power(ap):
            t = Q.v(lambda e: e.reciprocal(ap, ap))
            return Q.a(lambda e: e.activation(ap, ap, ACT.Sqrt), t)

        def rstd(ps, n, dim, eps, tok):
            Q.v(lambda e: e.tensor_scalar(rr[:, 0:n], ps, 1.0 / dim, eps, ALU.mult, ALU.add), tok)
            return power(rr[:, 0:n])

        def norm(src, out, gain, shift, tok):
            b, ps, bt = B.take()
            for h in range(2):
                sl = slice(4 * h, 4 * h + 4)
                t = Q.a(lambda e, sl=sl: e.activation(wk8[:, sl, :], src[:, sl, :], ACT.Square), *tok)
                for k in range(4 * h, 4 * h + 4):
                    Q.mm(ps[:, 0:256], ones, wk8[:, k, :], k == 0, k == 7, (t, bt))
            tp = rstd(ps[:, 0:256], 256, D, EPS, Q.pe_done())
            B.free(b, Q.last("dve"))
            for k in range(8):
                t = Q.v(lambda e, k=k: e.scalar_tensor_tensor(out(k), src[:, k, :], gain[:, k:k + 1], rr[:, 0:256],
                                                               ALU.mult, ALU.mult), tp, *tok)
                if shift is not None:
                    ta = Q.a(lambda e, k=k: e.activation(out(k), out(k), ACT.Identity, bias=shift[:, k:k + 1]), t)
            return (t, ta) if shift is not None else (t,)

        def transpose4(parts, dst, tok, eng="act"):
            b, ps, bt = B.take()
            for i, p in enumerate(parts):
                Q.tr(ps[:, i * 128:(i + 1) * 128], p, ident, (bt,) + tok)
            pt = Q.pe_done()
            n = len(parts)
            src = ps[:, 0:n * 128].rearrange("p (i t) -> p i t", i=n)
            if eng == "act":
                t = Q.a(lambda e: e.activation(dst, src, ACT.Copy), pt)
            else:
                t = Q.v(lambda e: e.tensor_copy(dst, src), pt)
            B.free(b, t)
            return t

        def head_norm(z, tmp, heads, dim, scale_to=None, tok=()):
            Q.v(lambda e: e.tensor_tensor(tmp, z, z, ALU.mult), *tok)
            Q.v(lambda e: e.tensor_reduce(rr[:, 0:heads], tmp, AX.X, ALU.add))
            Q.v(lambda e: e.tensor_scalar(rr[:, 0:heads], rr[:, 0:heads], 1.0 / (scale_to or dim), EPS, ALU.mult, ALU.add))
            tp = power(rr[:, 0:heads])
            return Q.v(lambda e: e.tensor_tensor(z, z, bc(rr[:, 0:heads].unsqueeze(2), [128, heads, dim]), ALU.mult), tp)

        def rope(o1, o2, x1, x2, c, s, t1, t2):
            Q.v(lambda e: e.tensor_tensor(t1, x1, c, ALU.mult))
            Q.v(lambda e: e.tensor_tensor(t2, x2, s, ALU.mult))
            Q.v(lambda e: e.tensor_tensor(t1, t1, t2, ALU.subtract))
            Q.v(lambda e: e.tensor_tensor(t2, x1, s, ALU.mult))
            Q.v(lambda e: e.tensor_tensor(o2, x2, c, ALU.mult))
            Q.v(lambda e: e.tensor_tensor(o2, o2, t2, ALU.add))
            return Q.v(lambda e: e.tensor_copy(o1, t1))

        def add_x(ps, j, n, pt):
            return Q.v(lambda e: e.tensor_tensor(x8[:, j:j + n, :], x8[:, j:j + n, :],
                                                 ps[:, 0:n * 256].rearrange("p (k t) -> p k t", k=n), ALU.add), pt)

        def even():
            mix = sc(0, 2048).rearrange("p (k t) -> p k t", k=8)
            qk = [sc(2048, 1024), sc(3072, 1024)]
            vv = sc(4096, 1024)
            qi = sc(5120, 1024)
            kid = sc(6144, 256)
            qTt = sc(6400, 1024).rearrange("p (k t) -> p k t", k=4)
            kTt = sc(7424, 1024).rearrange("p (k t) -> p k t", k=4)
            qiT = sc(8448, 1024).rearrange("p (k t) -> p k t", k=4)
            kiT = sc(9472, 256)
            score = sc(9728, 512)
            bias = sc(10240, 512)
            P = sc(10752, 512)
            PT = [sc(11264, 512), sc(11776, 512)]
            tmp = sc(12288, 1024)
            zc = sc(13312, 1024)
            u = sc(14336, 1032).rearrange("p (k t) -> p k t", k=4)
            zz = sc(15368, 1024)
            cs = mi(192)
            cosA, sinA = cs[:, 0:64], cs[:, 64:128]
            cosI, sinI = cs[:, 128:160], cs[:, 160:192]
            wi = mi(16)
            posf = mi(2)
            mx = mi(16)
            sm8 = mi(8)

            Q.v(lambda e: e.tensor_copy(posf, posi[:, :]), t_in)
            ang = tmp[:, 0:96]
            r1 = tmp[:, 96:192]
            r2 = tmp[:, 192:288]
            for t in range(2):
                Q.v(lambda e, t=t: e.tensor_scalar(ang[:, 48 * t:48 * t + 48], sm("invf"), posf[:, t:t + 1], None, ALU.mult))
            for quarter in (0.25, 0.0):
                Q.v(lambda e: e.tensor_scalar(r1, ang, float(1 / (2 * np.pi)), quarter, ALU.mult, ALU.add))
                Q.v(lambda e: e.tensor_scalar(r1, r1, MAGIC, None, ALU.add))
                Q.v(lambda e: e.tensor_scalar(r1, r1, -MAGIC, None, ALU.add))
                Q.v(lambda e: e.scalar_tensor_tensor(r2, r1, -TWO_PI_A, ang, ALU.mult, ALU.add))
                Q.v(lambda e: e.scalar_tensor_tensor(r2, r1, -TWO_PI_B, r2, ALU.mult, ALU.add))
                Q.v(lambda e: e.scalar_tensor_tensor(r2, r1, -TWO_PI_C, r2, ALU.mult, ALU.add))
                if quarter:
                    Q.v(lambda e: e.tensor_scalar(r2, r2, float(np.pi / 2), None, ALU.add))
                Q.v(lambda e: e.tensor_scalar(r2, r2, 3.1415925, None, ALU.min))
                t_r = Q.v(lambda e: e.tensor_scalar(r2, r2, -3.1415925, None, ALU.max))
                v2 = r2.rearrange("p (t f) -> p t f", t=2)
                A_, I_ = (cosA, cosI) if quarter else (sinA, sinI)
                Q.a(lambda e, A_=A_, v2=v2: e.activation(A_.rearrange("p (t f) -> p t f", t=2), v2[:, :, 0:32], ACT.Sin), t_r)
                t_cs = Q.a(lambda e, I_=I_, v2=v2: e.activation(I_.rearrange("p (t f) -> p t f", t=2), v2[:, :, 32:48], ACT.Sin), t_r)
                Q.v(lambda e: e.memset(dummy, 0.0), t_cs)

            tn = norm(x8, lambda k: n8[:, k, :], sm("norm_mix", 0, 8), None, (t_in,))
            lhs = lambda t: (lambda q: n8[:, q, t * 128:(t + 1) * 128])

            c = chunk(dr["ev_in"], 24, 4, 8)
            for t in range(2):
                dst = qi[:, t * 512:(t + 1) * 512]

                def take_qi(ps, pt, t=t, dst=dst):
                    return Q.a(lambda e: e.activation(dst, ps[:, :], ACT.Copy), pt)
                tokens(c.ap, 8, 0, 4, lhs(t), (c.tok,) + tn, take_qi)
            c.done(Q.pe_done())
            c = R.load([(dr["ev_tail"], 0, 576, 1)])
            ctail = c.ap[:, 0:576].rearrange("p (k n) -> p k n", k=8)
            for t in range(2):
                b, ps, bt = B.take()
                for q in range(8):
                    Q.mm(ps[:, 0:72], lhs(t)(q), ctail[:, q, :], q == 0, q == 7, (bt, c.tok) + tn)
                pt = Q.pe_done()
                kd = kid[:, t * 128:t * 128 + 64]
                Q.v(lambda e, ps=ps, kd=kd: e.tensor_copy(kd, ps[:, 0:64]), pt)
                tw = Q.v(lambda e, ps=ps, t=t: e.tensor_scalar(wi[:, t * 8:t * 8 + 8], ps[:, 64:72], float(8 ** -0.5 * 64 ** -0.5), None, ALU.mult), pt)
                B.free(b, tw)
                Q.v(lambda e, kd=kd: e.tensor_reduce(mx[:, 0:1], kd, AX.X, ALU.add))
                Q.v(lambda e: e.tensor_scalar(mx[:, 0:1], mx[:, 0:1], -1.0 / 64, None, ALU.mult))
                Q.v(lambda e, kd=kd: e.tensor_scalar(kd, kd, mx[:, 0:1], None, ALU.add))
                Q.v(lambda e, kd=kd: e.tensor_tensor(tmp[:, 512:576], kd, kd, ALU.mult))
                Q.v(lambda e: e.tensor_reduce(rr[:, 0:1], tmp[:, 512:576], AX.X, ALU.add))
                Q.v(lambda e: e.tensor_scalar(rr[:, 0:1], rr[:, 0:1], 1.0 / 64, EPS, ALU.mult, ALU.add))
                tp = power(rr[:, 0:1])
                Q.v(lambda e, kd=kd: e.scalar_tensor_tensor(kd, kd, rr[:, 0:1], sm("ln_g"), ALU.mult, ALU.mult), tp)
                Q.v(lambda e, kd=kd: e.tensor_tensor(kd, kd, sm("ln_b"), ALU.add))
                rope(kd[:, 0:16], kd[:, 16:32], kd[:, 0:16], kd[:, 16:32], cosI[:, t * 16:t * 16 + 16],
                     sinI[:, t * 16:t * 16 + 16], tmp[:, 0:16], tmp[:, 16:32])
                tk = Q.v(lambda e, kd=kd, t=t: e.tensor_copy(kid[:, t * 128 + 64:t * 128 + 128], kd))
            c.done(Q.pe_done())
            transpose4([kid[:, 0:128], kid[:, 128:256]], kiT.rearrange("p (i t) -> p i t", i=2), (tk,))
            t_ki = Q.last("act")
            for t in range(2):
                z = qi[:, t * 512:(t + 1) * 512].rearrange("p (h d) -> p h d", h=8)
                cb = bc(cosI[:, t * 16:t * 16 + 16].unsqueeze(1), [128, 8, 16])
                sb_ = bc(sinI[:, t * 16:t * 16 + 16].unsqueeze(1), [128, 8, 16])
                t1 = tmp[:, 0:128].rearrange("p (h d) -> p h d", h=8)
                t2 = tmp[:, 128:256].rearrange("p (h d) -> p h d", h=8)
                Q.v(lambda e: e.memset(dummy, 0.0), Q.last("act"))
                tr_ = rope(z[:, :, 0:16], z[:, :, 16:32], z[:, :, 0:16], z[:, :, 16:32], cb, sb_, t1, t2)
                t_qi = transpose4([qi[:, t * 512 + i * 128:t * 512 + (i + 1) * 128] for i in range(4)],
                                  qiT[:, :, t * 128:(t + 1) * 128], (tr_,))

            if dump is not None:
                Q.v(lambda e: e.memset(sc(9728, 1024), 0.0))
            for t in range(2):
                nk = 128 * (t + 1)
                s = score[:, t * 256:t * 256 + nk]
                Q.v(lambda e, s=s: e.memset(s, 0.0))
                relt = [None, None]
                for h in range(8):
                    b, ps, bt = B.take()
                    o = (h % 2) * 64
                    Q.mm(ps[:, 0:nk], qiT[o:o + 64, h // 2, t * 128:(t + 1) * 128], kiT[o:o + 64, 0:nk], True, True,
                         (bt, t_qi, t_ki))
                    rel = tmp[:, 512 + (h % 2) * 256:512 + (h % 2) * 256 + nk]
                    ta = Q.a(lambda e, ps=ps, nk=nk, rel=rel: e.activation(rel, ps[:, 0:nk], ACT.Relu), Q.pe_done(), relt[h % 2],
                             Q.last("dve") if h == 0 else None)
                    B.free(b, ta)
                    relt[h % 2] = Q.v(lambda e, s=s, rel=rel, t=t, h=h: e.scalar_tensor_tensor(
                        s, rel, wi[:, t * 8 + h:t * 8 + h + 1], s, ALU.mult, ALU.add), ta)
                Q.v(lambda e, s=s, nk=nk: e.tensor_tensor(s[:, nk - 128:nk], s[:, nk - 128:nk], sm("tri"), ALU.add))
            if dump is not None:
                dbg("score", score, (Q.last("dve"),))

            for which, j0 in ((0, 12), (1, 16)):
                c = chunk(dr["ev_in"], j0, 4, 8)
                for t in range(2):
                    dst = qk[which][:, t * 512:(t + 1) * 512]
                    tokens(c.ap, 8, 0, 4, lhs(t), (c.tok,) + tn,
                           lambda ps, pt, dst=dst: Q.a(lambda e: e.activation(dst, ps[:, :], ACT.Copy), pt))
                c.done(Q.pe_done())
            t_qk = Q.last("act")
            c = chunk(dr["ev_in"], 20, 4, 8)
            for t in range(2):
                dst = vv[:, t * 512:(t + 1) * 512]
                tokens(c.ap, 8, 0, 4, lhs(t), (c.tok,) + tn,
                       lambda ps, pt, dst=dst: Q.a(lambda e: e.activation(dst, ps[:, :], ACT.Copy), pt))
            c.done(Q.pe_done())
            t_v = Q.last("act")

            for which, dst, g in ((0, qTt, "ev_qg"), (1, kTt, "ev_kg")):
                for t in range(2):
                    z = qk[which][:, t * 512:(t + 1) * 512].rearrange("p (h d) -> p h d", h=8)
                    t3 = tmp[:, 0:512].rearrange("p (h d) -> p h d", h=8)
                    head_norm(z, t3, 8, 64, tok=(t_qk,))
                    Q.v(lambda e, z=z, g=g: e.tensor_tensor(z, z, bc(sm(g).unsqueeze(1), [128, 8, 64]), ALU.mult))
                    cb = bc(cosA[:, t * 32:t * 32 + 32].unsqueeze(1), [128, 8, 32])
                    sb_ = bc(sinA[:, t * 32:t * 32 + 32].unsqueeze(1), [128, 8, 32])
                    t1 = tmp[:, 0:256].rearrange("p (h d) -> p h d", h=8)
                    t2 = tmp[:, 256:512].rearrange("p (h d) -> p h d", h=8)
                    tr_ = rope(z[:, :, 0:32], z[:, :, 32:64], z[:, :, 0:32], z[:, :, 32:64], cb, sb_, t1, t2)
                    t_T = transpose4([qk[which][:, t * 512 + i * 128:t * 512 + (i + 1) * 128] for i in range(4)],
                                     dst[:, :, t * 128:(t + 1) * 128], (tr_,))

            for t in range(2):
                nk = 128 * (t + 1)
                s = score[:, t * 256:t * 256 + nk]
                for _ in range(8):
                    Q.v(lambda e, s=s: e.max(sm8, s))
                    Q.v(lambda e, s=s: e.match_replace(s, sm8, s, TAKEN))
                bb = bias[:, t * 256:t * 256 + nk]
                Q.v(lambda e, s=s, bb=bb: e.tensor_scalar(bb, s, TAKEN, 1.0, ALU.is_equal, ALU.subtract))
                Q.v(lambda e, bb=bb: e.tensor_scalar(bb, bb, BIG, None, ALU.mult))
                Q.v(lambda e, bb=bb, nk=nk: e.tensor_tensor(bb[:, nk - 128:nk], bb[:, nk - 128:nk], sm("tri"), ALU.add))
            if dump is not None:
                dbg("bias", bias, (Q.last("dve"),))

            Q.v(lambda e: e.memset(u[:, :, 0:2], 0.0))

            def take_zc(ps, j, n, pt):
                return Q.a(lambda e: e.activation(zc[:, j * 256:(j + n) * 256], ps[:, 0:n * 256], ACT.Copy), pt)
            dense(dr["ev_in"], [4, 5, 6, 7], 8, lambda q: n8[:, q, :], tn, take_zc)
            t_zc = Q.last("act")

            def take_zh(ps, j, n, pt):
                t = Q.v(lambda e: e.tensor_tensor(u[:, j:j + n, 2:258], ps[:, 0:n * 256].rearrange("p (k t) -> p k t", k=n),
                                                  zc[:, j * 256:(j + n) * 256].rearrange("p (k t) -> p k t", k=n), ALU.mult), pt, t_zc)
                for i in range(j, j + n):
                    y = zz[:, i * 256:(i + 1) * 256]
                    w = sm("ev_conv", 3 * i, 3 * i + 3)
                    Q.v(lambda e, i=i, y=y, w=w: e.tensor_scalar(y, u[:, i, 0:256], w[:, 0:1], None, ALU.mult))
                    Q.v(lambda e, i=i, y=y, w=w: e.scalar_tensor_tensor(y, u[:, i, 1:257], w[:, 1:2], y, ALU.mult, ALU.add))
                    Q.v(lambda e, i=i, y=y, w=w: e.scalar_tensor_tensor(y, u[:, i, 2:258], w[:, 2:3], y, ALU.mult, ALU.add))
                return t
            dense(dr["ev_in"], [8, 9, 10, 11], 8, lambda q: n8[:, q, :], tn, take_zh)

            def take_zb(ps, j, n, pt):
                return Q.v(lambda e: e.tensor_tensor(mix[:, j:j + n, :], ps[:, 0:n * 256].rearrange("p (k t) -> p k t", k=n),
                                                     zz[:, j * 256:(j + n) * 256].rearrange("p (k t) -> p k t", k=n), ALU.mult), pt)
            dense(dr["ev_in"], [0, 1, 2, 3], 8, lambda q: n8[:, q, :], tn, take_zb)

            for i in range(2):
                Q.v(lambda e, i=i: e.memset(PT[i][:, 256:384], 0.0))
            t_z = Q.last("dve")
            ptfree = [t_z, t_z]
            for h in range(8):
                o = (h % 2) * 64
                pt_ = PT[h % 2].rearrange("p (k t) -> p k t", k=2)
                if h % 2 == 0:
                    ob, ops, obt = B.take()
                for t in range(2):
                    nk = 128 * (t + 1)
                    b, ps, bt = B.take()
                    Q.mm(ps[:, 0:nk], qTt[o:o + 64, h // 2, t * 128:(t + 1) * 128], kTt[o:o + 64, h // 2, 0:nk], True, True,
                         (bt, t_T))
                    p = P[:, t * 256:t * 256 + nk]
                    bb = bias[:, t * 256:t * 256 + nk]
                    tv = Q.v(lambda e, ps=ps, p=p, bb=bb, nk=nk: e.scalar_tensor_tensor(p, ps[:, 0:nk], 0.125, bb, ALU.mult, ALU.add), Q.pe_done())
                    B.free(b, tv)
                    m_ = mx[:, 2 * t:2 * t + 1]
                    z_ = mx[:, 2 * t + 1:2 * t + 2]
                    Q.v(lambda e, p=p, m_=m_: e.tensor_reduce(m_, p, AX.X, ALU.max))
                    tv = Q.v(lambda e, m_=m_: e.tensor_scalar(m_, m_, -1.0, None, ALU.mult))
                    ta = Q.a(lambda e, p=p, m_=m_, z_=z_: e.activation(p, p, ACT.Exp, bias=m_, accum_out=z_), tv)
                    Q.v(lambda e, z_=z_: e.reciprocal(z_, z_), ta)
                    tv = Q.v(lambda e, p=p, z_=z_: e.tensor_scalar(p, p, z_, None, ALU.mult))
                    b, ps, bt = B.take()
                    for k in range(t + 1):
                        Q.tr(ps[:, k * 128:(k + 1) * 128], p[:, k * 128:(k + 1) * 128], ident, (bt, tv))
                    ta = Q.a(lambda e, ps=ps, nk=nk, t=t, pt_=pt_: e.activation(
                        pt_[:, 0:t + 1, t * 128:(t + 1) * 128], ps[:, 0:nk].rearrange("p (k t) -> p k t", k=t + 1), ACT.Copy),
                        Q.pe_done(), ptfree[h % 2])
                    B.free(b, ta)
                for k in range(2):
                    Q.mm(ops[o:o + 64, 0:256], vv[:, k * 512 + h * 64:k * 512 + (h + 1) * 64], pt_[:, k, :], k == 0, k == 1,
                         (obt, ta, t_v, t_z))
                ptfree[h % 2] = Q.pe_done()
                if h % 2 == 1:
                    ta = Q.a(lambda e, ops=ops, h=h: e.activation(mix[:, 4 + h // 2, :], ops[:, 0:256], ACT.Copy), Q.pe_done())
                    B.free(ob, ta)
            if dump is not None:
                dbg("mix", sc(0, 2048), (Q.last("dve"), Q.last("act")))
            dense(dr["ev_out"], list(range(8)), 8, lambda q: mix[:, q, :], (Q.last("act"), Q.last("dve")), add_x)

        def ffn(l):
            act = sc(0, 5632).rearrange("p (k t) -> p k t", k=22)
            sg = [sc(5632, 512), sc(6144, 512), sc(6656, 512), sc(7168, 512)]
            tn = norm(x8, lambda k: n8[:, k, :], sm("norm_ffn", 8 * l, 8 * l + 8), None, (Q.last("dve"),))
            n = [0, 0]
            utok = {}

            def gate(ps, j, k, pt):
                s = sg[n[0] % 4]
                t = Q.a(lambda e: e.activation(s[:, 0:k * 256], ps[:, 0:k * 256], ACT.Silu), pt, utok.get(n[0] - 4))
                gtok[n[0]] = t
                n[0] += 1
                return t

            gtok = {}
            for j0 in range(0, 22, 4):
                js = list(range(j0, min(j0 + 4, 22)))
                dense(dr["ffn_gate"][l], js, 8, lambda q: n8[:, q, :], tn, gate)

                def up(ps, j, k, pt, j0=j0):
                    s = sg[n[1] % 4]
                    t = Q.v(lambda e: e.tensor_tensor(act[:, j0 + j:j0 + j + k, :], ps[:, 0:k * 256].rearrange("p (k t) -> p k t", k=k),
                                                      s[:, 0:k * 256].rearrange("p (k t) -> p k t", k=k), ALU.mult), pt, gtok[n[1]])
                    utok[n[1]] = t
                    n[1] += 1
                    return t
                dense(dr["ffn_up"][l], js, 8, lambda q: n8[:, q, :], tn, up)
            dense(dr["ffn_down"][l], list(range(8)), 22, lambda q: act[:, q, :], (Q.last("dve"),), add_x)

        s_p = Q.new_sem("s_p")

        def ple(l):
            er = sc(8192, 2048).rearrange("p (k t) -> p k t", k=8)
            pT = sc(10240, 512).rearrange("p (k t) -> p k t", k=2)
            sg = [sc(10752, 512), sc(11264, 512)]
            tp = Q.dma("pool", sc(10240, 512), dr["pT"][l], s_p, (Q.last("dve"), Q.last("act"), Q.pe_done()))

            def take(ps, j, n, pt):
                return Q.a(lambda e: e.activation(er[:, j:j + n, :], ps[:, 0:n * 256].rearrange("p (k t) -> p k t", k=n), ACT.Copy), pt)
            dense(dr["ple_proj"][l], list(range(8)), 2, lambda q: pT[:, q, :], (tp,), take)
            norm(er, lambda k: er[:, k, :], sm("ple_post", 8 * l, 8 * l + 8), None, (Q.last("act"),))
            tn = norm(x8, lambda k: n8[:, k, :], sm("ple_norm", 8 * l, 8 * l + 8), None, (Q.last("dve"), Q.pe_done()))
            i = [0]
            free = [None, None]

            def take2(ps, j, n, pt):
                s = sg[i[0] % 2]
                k = i[0] % 2
                i[0] += 1
                ta = Q.a(lambda e: e.activation(s, ps[:, 0:n * 256], ACT.Sigmoid), pt, free[k])
                sv = s.rearrange("p (k t) -> p k t", k=n)
                Q.v(lambda e: e.tensor_tensor(sv, sv, er[:, j:j + n, :], ALU.mult), ta)
                free[k] = Q.v(lambda e: e.tensor_tensor(x8[:, j:j + n, :], x8[:, j:j + n, :], sv, ALU.add))
                return ta
            dense(dr["ple_gate"][l], list(range(8)), 8, lambda q: n8[:, q, :], tn, take2)

        def odd():
            S = lambda i: sc(i * 1024, 1024)
            gb = mi(16 * 3)
            gcu, beta, eg = gb[:, 0:16], gb[:, 16:32], gb[:, 32:48]
            gk = mi(32)
            glast, kd = gk[:, 0:16], gk[:, 16:32]
            EL = mi(32)
            ea = mi(8)
            gt = mi(32)
            rq = mi(8)
            rq2 = mi(8)
            oT = cT[:, :].rearrange("p (k t) -> p k t", k=8)
            tn = norm(x8, lambda k: n8[:, k, :], sm("norm_mix", 8, 16), None, (Q.last("dve"),))
            lhs = lambda t: (lambda q: n8[:, q, t * 128:(t + 1) * 128])

            c = R.load([(dr["od_tail"], 0, 128, 1)])
            ctail = c.ap[:, 0:128].rearrange("p (k n) -> p k n", k=8)
            t_ea = Q.a(lambda e: e.activation(ea, sm("a_log"), ACT.Exp))
            for t in range(2):
                b, ps, bt = B.take()
                for q in range(8):
                    Q.mm(ps[:, 0:16], lhs(t)(q), ctail[:, q, :], q == 0, q == 7, (bt, c.tok) + tn)
                g = gt[:, 0:8]
                a1 = gt[:, 8:16]
                a2 = gt[:, 16:24]
                Q.v(lambda e, ps=ps: e.tensor_tensor(g, ps[:, 0:8], sm("dt_bias"), ALU.add), Q.pe_done())
                tb = Q.v(lambda e, ps=ps: e.tensor_copy(a2, ps[:, 8:16]))
                B.free(b, tb)
                Q.v(lambda e: e.tensor_scalar(a1, g, -1.0, None, ALU.mult))
                tv = Q.v(lambda e: e.tensor_tensor(a1, a1, g, ALU.min))
                Q.a(lambda e, t=t: e.activation(beta[:, 8 * t:8 * t + 8], a2, ACT.Sigmoid), tv)
                Q.a(lambda e: e.activation(a1, a1, ACT.Exp), tv)
                ta = Q.a(lambda e: e.activation(a1, a1, ACT.Ln, bias=1.0))
                Q.v(lambda e: e.tensor_scalar(g, g, 0.0, None, ALU.max))
                Q.v(lambda e: e.tensor_tensor(g, g, a1, ALU.add), ta)
                Q.v(lambda e: e.tensor_scalar(g, g, -1.0, None, ALU.mult))
                t_g = Q.v(lambda e, t=t: e.tensor_tensor(gcu[:, 8 * t:8 * t + 8], g, ea, ALU.mult), t_ea)
            c.done(Q.pe_done())
            b, ps, bt = B.take()
            Q.mm(ps[:, 0:16], sm("cumT"), gcu, True, True, (bt, t_g))
            t_g = Q.v(lambda e, ps=ps: e.tensor_copy(gcu, ps[:, 0:16]), Q.pe_done())
            B.free(b, t_g)
            b, ps, bt = B.take()
            Q.mm(ps[:, 0:16], sm("lastT"), gcu, True, True, (bt, t_g))
            Q.mm(ps[:, 16:32], sm("sel", 0, 128), gcu, True, True)
            Q.mm(ps[:, 32:48], sm("sel", 128, 256), gcu, True, True)
            pt = Q.pe_done()
            t1 = Q.v(lambda e, ps=ps: e.tensor_tensor(kd, ps[:, 0:16], gcu, ALU.subtract), pt)
            Q.a(lambda e: e.activation(kd, kd, ACT.Exp), t1)
            ta = Q.a(lambda e, ps=ps: e.activation(EL, ps[:, 16:48], ACT.Exp), pt)
            B.free(b, ta)
            t_gates = Q.a(lambda e: e.activation(eg, gcu, ACT.Exp), t_g)

            if dump is not None:
                dbg("gcu", gcu, (Q.last("dve"),))
            u = wk[:, 0:1036].rearrange("p (k t) -> p k t", k=4)
            Q.v(lambda e: e.memset(u[:, :, 0:3], 0.0), Q.pe_done())
            for H in range(2):
                qT, z, kT, vT, K, kbg, V, knT, MT, qkT, T, TT, Y, BT, wT = (S(i) for i in range(15))
                St = sc(15360, 512)
                d4 = lambda a: a.rearrange("p (k t) -> p k t", k=4)
                t4 = lambda a: a.rearrange("p (t f) -> p t f", t=2)
                for base, dst in ((0, qT), (8, kT), (16, vT)):
                    ufree = [Q.last("dve")]

                    def take(ps, j, n, pt, dst=dst, base=base):
                        ta = Q.a(lambda e: e.activation(u[:, j:j + n, 3:259], ps[:, 0:n * 256].rearrange("p (k t) -> p k t", k=n),
                                                        ACT.Copy), pt, ufree[0])
                        for i in range(j, j + n):
                            w = sm("od_conv", 4 * (base + 4 * H + i), 4 * (base + 4 * H + i) + 4)
                            y = d4(dst)[:, i, :]
                            Q.v(lambda e, i=i, y=y, w=w: e.tensor_scalar(y, u[:, i, 0:256], w[:, 0:1], None, ALU.mult), ta, Q.last("pe"))
                            for s in range(1, 4):
                                tv = Q.v(lambda e, i=i, y=y, w=w, s=s: e.scalar_tensor_tensor(
                                    y, u[:, i, s:s + 256], w[:, s:s + 1], y, ALU.mult, ALU.add))
                        Q.a(lambda e, dst=dst, j=j, n=n: e.activation(d4(dst)[:, j:j + n, :], d4(dst)[:, j:j + n, :], ACT.Silu), tv)
                        return ta
                    dense(dr["od_in"], [base + 4 * H + i for i in range(4)], 8, lambda q: n8[:, q, :], tn, take)
                c = chunk(dr["od_in"], 24 + 4 * H, 4, 8)
                for t in range(2):
                    tokens(c.ap, 8, 0, 4, lhs(t), (c.tok,) + tn,
                           lambda ps, pt, t=t: Q.a(lambda e: e.activation(z[:, t * 512:(t + 1) * 512], ps[:, :], ACT.Silu), pt))
                c.done(Q.pe_done())
                t_c = Q.last("act")
                if dump is not None and H == 0:
                    dbg("oqT", qT, (Q.last("act"),)); dbg("ovT", vT, (Q.last("act"),))
                for t in range(2):
                    transpose4([d4(kT)[:, h, t * 128:(t + 1) * 128] for h in range(4)],
                               K[:, t * 512:(t + 1) * 512].rearrange("p (k t) -> p k t", k=4), (t_c,))
                    transpose4([d4(vT)[:, h, t * 128:(t + 1) * 128] for h in range(4)],
                               V[:, t * 512:(t + 1) * 512].rearrange("p (k t) -> p k t", k=4), (t_c,))
                t_kv = Q.last("act")
                sq = Y
                tv = Q.v(lambda e: e.tensor_tensor(sq, qT, qT, ALU.mult), t_kv)
                b, ps, bt = B.take()
                for t in range(2):
                    for h in range(4):
                        Q.mm(ps[:, t * 4 + h:t * 4 + h + 1], d4(sq)[:, h, t * 128:(t + 1) * 128], ones[:, 0:1], True, True, (bt, tv))
                Q.v(lambda e, ps=ps: e.tensor_scalar(rq, ps[:, 0:8], EPS, None, ALU.add), Q.pe_done())
                B.free(b, Q.last("dve"))
                tp = power(rq)
                Q.v(lambda e: e.tensor_scalar(rq, rq, float(128 ** -0.5), None, ALU.mult), tp)
                gs = lambda a: a.rearrange("p (t h) -> p t h", t=2)[:, :, 4 * H:4 * H + 4]
                Q.v(lambda e: e.tensor_tensor(rq2.rearrange("p (t h) -> p t h", t=2), rq.rearrange("p (t h) -> p t h", t=2),
                                              gs(eg), ALU.mult), t_gates)
                k3 = K.rearrange("p (h d) -> p h d", h=8)
                head_norm(k3, BT.rearrange("p (h d) -> p h d", h=8), 8, 128, 1.0)
                t_kn = Q.last("dve")
                for t in range(2):
                    transpose4([K[:, t * 512 + h * 128:t * 512 + (h + 1) * 128] for h in range(4)],
                               d4(knT)[:, :, t * 128:(t + 1) * 128], (t_kn,))
                t_knT = Q.last("act")
                for t in range(2):
                    col = lambda a, t=t: bc(a[:, 8 * t + 4 * H:8 * t + 4 * H + 4].unsqueeze(2), [128, 4, 128])
                    hv = lambda a, t=t: a[:, t * 512:(t + 1) * 512].rearrange("p (h d) -> p h d", h=4)
                    Q.v(lambda e, col=col, hv=hv: e.tensor_tensor(hv(V), hv(V), col(beta), ALU.mult))
                    Q.v(lambda e, col=col, hv=hv: e.tensor_tensor(hv(kbg), hv(K), col(beta), ALU.mult))
                    Q.v(lambda e, col=col, hv=hv: e.tensor_tensor(hv(kbg), hv(kbg), col(eg), ALU.mult))
                    for h in range(4):
                        tv = Q.v(lambda e, t=t, h=h: e.tensor_scalar(Y[:, h * 128:(h + 1) * 128], ident,
                                                                     gcu[:, 8 * t + 4 * H + h:8 * t + 4 * H + h + 1], None, ALU.mult),
                                 Q.last("pe"))
                    b, ps, bt = B.take()
                    Q.mm(ps[:, :], ones, Y[:, 0:512], True, False, (bt, tv))
                    Q.mm(ps[:, :].rearrange("p (h t) -> p h t", h=4), ident, bc(sm("dmask").unsqueeze(1), [128, 4, 128]), False, True)
                    pt = Q.pe_done()
                    for h in range(4):
                        ta = Q.a(lambda e, ps=ps, h=h, t=t: e.activation(
                            kT[:, t * 512 + h * 128:t * 512 + (h + 1) * 128], ps[:, h * 128:(h + 1) * 128], ACT.Exp,
                            bias=gcu[:, 8 * t + 4 * H + h:8 * t + 4 * H + h + 1], scale=-1.0), pt)
                    B.free(b, ta)
                    for kind in range(2):
                        b, ps, bt = B.take()
                        L = knT if kind == 0 else qT
                        for h in range(4):
                            Q.mm(ps[:, h * 128:(h + 1) * 128], d4(L)[:, h, t * 128:(t + 1) * 128],
                                 d4(knT)[:, h, t * 128:(t + 1) * 128], True, True, (bt, t_knT))
                        pt = Q.pe_done()
                        for h in range(4):
                            s_ = (beta[:, 8 * t + 4 * H + h:8 * t + 4 * H + h + 1] if kind == 0 else rq[:, 4 * t + h:4 * t + h + 1])
                            tv = Q.v(lambda e, ps=ps, h=h, t=t, s_=s_: e.scalar_tensor_tensor(
                                vT[:, h * 128:(h + 1) * 128], ps[:, h * 128:(h + 1) * 128], s_,
                                kT[:, t * 512 + h * 128:t * 512 + (h + 1) * 128], ALU.mult, ALU.mult), pt, ta, Q.last("pe"))
                        B.free(b, tv)
                        dst = MT if kind == 0 else qkT
                        transpose4([vT[:, h * 128:(h + 1) * 128] for h in range(4)],
                                   dst[:, t * 512:(t + 1) * 512].rearrange("p (k t) -> p k t", k=4), (tv,))
                    Q.v(lambda e, col=col, hv=hv: e.tensor_tensor(hv(K), hv(K), col(kd), ALU.mult), t_knT)
                t_MT = Q.last("act")
                if dump is not None and H == 0:
                    dbg("MT", MT, (Q.last("act"), Q.last("dve"))); dbg("knT", knT, (Q.last("act"), Q.last("dve")))
                    dbg("qkT", qkT, (Q.last("act"), Q.last("dve")))
                p8 = lambda a: a.rearrange("p (i t) -> p i t", i=8)
                lv = lambda l: bc(sm("levels", 128 * l, 128 * l + 128).unsqueeze(1), [128, 8, 128])
                Q.v(lambda e: e.tensor_tensor(p8(BT), p8(MT), lv(0), ALU.mult), t_MT)
                tv = Q.v(lambda e: e.tensor_tensor(p8(TT), bc(ident.unsqueeze(1), [128, 8, 128]), p8(BT), ALU.subtract))
                for t in range(2):
                    transpose4([TT[:, t * 512 + h * 128:t * 512 + (h + 1) * 128] for h in range(4)],
                               T[:, t * 512:(t + 1) * 512].rearrange("p (k t) -> p k t", k=4), (tv,))
                t_T = Q.last("act")
                for l in range(1, 6):
                    tb = Q.v(lambda e, l=l: e.tensor_tensor(p8(BT), p8(MT), lv(l), ALU.mult), Q.last("pe"))
                    for t in range(2):
                        b, ps, bt = B.take()
                        for h in range(4):
                            i = t * 4 + h
                            Q.mm(ps[:, h * 128:(h + 1) * 128], p8(BT)[:, i, :], p8(T)[:, i, :], True, True, (bt, tb, t_T))
                        ta = Q.a(lambda e, ps=ps, t=t: e.activation(Y[:, t * 512:(t + 1) * 512], ps[:, :], ACT.Copy), Q.pe_done())
                        B.free(b, ta)
                    for t in range(2):
                        for kind in range(2):
                            if kind == 0 and l == 5:
                                continue
                            b, ps, bt = B.take()
                            for h in range(4):
                                i = t * 4 + h
                                if kind == 0:
                                    Q.mm(ps[:, h * 128:(h + 1) * 128], p8(TT)[:, i, :], p8(Y)[:, i, :], True, True, (bt, ta))
                                else:
                                    Q.mm(ps[:, h * 128:(h + 1) * 128], p8(Y)[:, i, :], p8(TT)[:, i, :], True, True, (bt, ta))
                            dst = (T if kind == 0 else TT)[:, t * 512:(t + 1) * 512]
                            tv = Q.v(lambda e, ps=ps, dst=dst: e.tensor_tensor(dst, dst, ps[:, :], ALU.subtract), Q.pe_done())
                            B.free(b, tv)
                    t_T = tv
                if dump is not None and H == 0:
                    dbg("TT", TT, (Q.last("act"), Q.last("dve")))
                U = vT
                for t in range(2):
                    b, ps, bt = B.take()
                    for h in range(4):
                        i = t * 4 + h
                        Q.mm(ps[:, h * 128:(h + 1) * 128], p8(TT)[:, i, :], p8(V)[:, i, :], True, True, (bt, t_T))
                    ta = Q.a(lambda e, ps=ps, t=t: e.activation(U[:, t * 512:(t + 1) * 512], ps[:, :], ACT.Copy), Q.pe_done())
                    B.free(b, ta)
                    b, ps, bt = B.take()
                    for h in range(4):
                        i = t * 4 + h
                        Q.mm(ps[:, h * 128:(h + 1) * 128], p8(kbg)[:, i, :], p8(TT)[:, i, :], True, True, (bt, t_T))
                    ta = Q.a(lambda e, ps=ps, t=t: e.activation(wT[:, t * 512:(t + 1) * 512], ps[:, :], ACT.Copy), Q.pe_done())
                    B.free(b, ta)
                t_uw = ta
                O = T
                vn = Y
                t_s = None
                for n in range(4):
                    t, o = n // 2, 64 * (n % 2)
                    r = slice(o, o + 64)
                    vs = vn[r, t * 512:(t + 1) * 512]
                    us = U[r, t * 512:(t + 1) * 512]
                    if n == 0:
                        tvn = Q.v(lambda e, vs=vs, us=us: e.tensor_copy(vs, us), t_uw, Q.last("pe"))
                    else:
                        b, ps, bt = B.take()
                        for h in range(4):
                            i = t * 4 + h
                            Q.mm(ps[r, h * 128:(h + 1) * 128], p8(wT)[:, i, o:o + 64], St[:, h * 128:(h + 1) * 128], True, True,
                                 (bt, t_s, t_uw))
                        tvn = Q.v(lambda e, vs=vs, us=us, ps=ps, r=r: e.tensor_tensor(vs, us, ps[r, :], ALU.subtract), Q.pe_done())
                        B.free(b, tvn)
                    b, ps, bt = B.take()
                    for h in range(4):
                        i = t * 4 + h
                        Q.mm(ps[r, h * 128:(h + 1) * 128], p8(qkT)[r, i, o:o + 64], vn[r, t * 512 + h * 128:t * 512 + (h + 1) * 128],
                             True, True, (bt, tvn))
                    Os = O[r, t * 512:(t + 1) * 512]
                    ta = Q.a(lambda e, ps=ps, r=r, Os=Os: e.activation(Os, ps[r, :], ACT.Copy), Q.pe_done())
                    B.free(b, ta)
                    if n:
                        b, ps, bt = B.take()
                        for h in range(4):
                            Q.mm(ps[r, h * 128:(h + 1) * 128], d4(qT)[:, h, t * 128 + o:t * 128 + o + 64],
                                 St[:, h * 128:(h + 1) * 128], True, True, (bt, t_s))
                        pt = Q.pe_done()
                        for h in range(4):
                            tv = Q.v(lambda e, ps=ps, r=r, h=h, t=t: e.scalar_tensor_tensor(
                                O[r, t * 512 + h * 128:t * 512 + (h + 1) * 128], ps[r, h * 128:(h + 1) * 128],
                                rq2[r, 4 * t + h:4 * t + h + 1], O[r, t * 512 + h * 128:t * 512 + (h + 1) * 128],
                                ALU.mult, ALU.add), pt, ta)
                        B.free(b, tv)
                    if n < 3:
                        b, ps, bt = B.take()
                        for h in range(4):
                            i = t * 4 + h
                            Q.mm(ps[:, h * 128:(h + 1) * 128], p8(K)[r, i, :], vn[r, t * 512 + h * 128:t * 512 + (h + 1) * 128],
                                 True, True, (bt, tvn))
                        pt = Q.pe_done()
                        if n == 0:
                            t_s = Q.v(lambda e, ps=ps: e.tensor_copy(St, ps[:, :]), pt)
                        else:
                            for h in range(4):
                                el = EL[:, 16 * (n % 2) + 8 * t + 4 * H + h:16 * (n % 2) + 8 * t + 4 * H + h + 1]
                                t_s = Q.v(lambda e, ps=ps, h=h, el=el: e.scalar_tensor_tensor(
                                    St[:, h * 128:(h + 1) * 128], St[:, h * 128:(h + 1) * 128], el,
                                    ps[:, h * 128:(h + 1) * 128], ALU.mult, ALU.add), pt)
                        B.free(b, t_s)
                if dump is not None and H == 0:
                    dbg("O", O, (Q.last("act"), Q.last("dve")))
                o3 = O.rearrange("p (h d) -> p h d", h=8)
                head_norm(o3, BT.rearrange("p (h d) -> p h d", h=8), 8, 128, tok=(Q.last("act"),))
                Q.v(lambda e: e.tensor_tensor(o3, o3, bc(sm("o_g").unsqueeze(1), [128, 8, 128]), ALU.mult))
                tv = Q.v(lambda e: e.tensor_tensor(O, O, z, ALU.mult))
                for t in range(2):
                    t_o = transpose4([O[:, t * 512 + h * 128:t * 512 + (h + 1) * 128] for h in range(4)],
                                     oT[:, 4 * H:4 * H + 4, t * 128:(t + 1) * 128], (tv,))
            dense(dr["od_out"], list(range(8)), 8, lambda q: oT[:, q, :], (t_o,), add_x)

        mods = [mi(96), mi(96)]
        s1 = mi(32)

        def ada(l):
            c2 = mi(16) if l == 0 else c2s[0]
            if l == 0:
                c2s.append(c2)
                t_c2[0] = Q.a(lambda e: e.activation(c2, sm("c2"), ACT.Silu))
            c2v = c2.rearrange("p (k s) -> p k s", k=8)

            def take(ps, j, n, pt):
                return Q.v(lambda e: e.tensor_tensor(
                    mods[l].rearrange("p (j s) -> p j s", j=48)[:, j:j + n, :],
                    ps[:, 0:2 * n].rearrange("p (j s) -> p j s", j=n),
                    bc(sm("ada_b", 48 * l + j, 48 * l + j + n).unsqueeze(2), [128, n, 2]), ALU.add), pt)
            dense(dr["ada"][l], list(range(48)), 8, lambda q: c2v[:, q, :], (t_c2[0],), take, width=2, per=4)
        c2s = []
        t_c2 = [None]

        def mod(l, which, side):
            return mods[l].rearrange("p (w k s) -> p w s k", w=6, k=8)[:, which, side, :]

        s_c = Q.new_sem("s_c")
        s_k = Q.new_sem("s_k")

        def load_consts():
            after = (Q.last("dve"), Q.last("act"), Q.pe_done())
            Q.dma("pool", sc(0, 1280), dr["dft"], s_c, after)
            return Q.dma("pool", cT[:, :], dr["ctxT"], s_c, after)

        def scales(l, which_g, which_m, side):
            g = sm(which_g, 8 * l, 8 * l + 8)
            dst = s1[:, 8 * side:8 * side + 8]
            Q.v(lambda e: e.tensor_scalar(dst, mod(l, which_m, side), 1.0, None, ALU.add))
            Q.v(lambda e: e.tensor_tensor(dst, dst, g, ALU.mult))
            return dst

        def mixer2(l):
            CS = sc(0, 1024).rearrange("p (k t) -> p k t", k=2)
            BD = sc(1024, 256)
            fp = sc(1280, 2048).rearrange("p (s t f) -> p s t f", s=2, t=2)
            kv = sc(3328, 2048).rearrange("p (s t f) -> p s t f", s=2, t=2)
            q_ = sc(5376, 1024)
            qTt = sc(6400, 1024).rearrange("p (h t) -> p h t", h=4)
            kTt = sc(7424, 1024).rearrange("p (h t) -> p h t", h=2)
            PT = [sc(8448, 1024), sc(9472, 1024)]
            P = [sc(10496, 512), sc(11008, 512)]
            mix = sc(11520, 4096).rearrange("p (k s t) -> p k s t", k=8, s=2)
            tmp = sc(15616, 1536)
            src = [x8, c8]
            nside = 2 if l == 0 else 1
            for side in range(2):
                dst = scales(l, "n1", 1, side)
                tn = norm(src[side], lambda k, side=side: n2[:, k, side, :], dst, mod(l, 0, side), (Q.last("dve"), t_const) + tuple(lasts()))
            tn = tn + (Q.last("act"), Q.last("dve"))
            t_pool = Q.dma("pool", wk[:, :], dr["poolA"], s_k, tn + (Q.pe_done(),))
            PA = wk[:, :].rearrange("p (g k t) -> p g k t", g=4, k=2)
            lhs = lambda s, t: (lambda q: n2[:, q, s, t * 128:(t + 1) * 128])
            c = chunk(dr["w_in"][l], 0, 4, 8)
            for s in range(nside):
                for t in range(2):
                    tokens(c.ap, 8, 0, 4, lhs(s, t), (c.tok,) + tn,
                           lambda ps, pt, s=s, t=t: Q.a(lambda e: e.activation(fp[:, s, t, :], ps[:, :], ACT.Copy), pt))
            c.done(Q.pe_done())
            t_fp = Q.last("act")
            c = chunk(dr["w_in"][l], 8, 4, 8)
            for s in range(2):
                for t in range(2):
                    tokens(c.ap, 8, 0, 4, lhs(s, t), (c.tok,) + tn,
                           lambda ps, pt, s=s, t=t: Q.a(lambda e: e.activation(kv[:, s, t, :], ps[:, :], ACT.Copy), pt))
            c.done(Q.pe_done())
            t_kv = Q.last("act")
            cq = chunk(dr["w_in"][l], 4, 4, 8)

            def rope2(z, t, heads):
                zz = z.rearrange("p (h a x f) -> p h a x f", h=heads, a=2, x=2)
                n = heads * 64
                t1 = tmp[:, 0:n].rearrange("p (h a f) -> p h a f", h=heads, a=2)
                t2 = tmp[:, n:2 * n].rearrange("p (h a f) -> p h a f", h=heads, a=2)
                cb = bc(sm("rcos", 64 * t, 64 * t + 64).rearrange("p (a f) -> p a f", a=2).unsqueeze(1), [128, heads, 2, 32])
                sb_ = bc(sm("rsin", 64 * t, 64 * t + 64).rearrange("p (a f) -> p a f", a=2).unsqueeze(1), [128, heads, 2, 32])
                return rope(zz[:, :, :, 0, :], zz[:, :, :, 1, :], zz[:, :, :, 0, :], zz[:, :, :, 1, :], cb, sb_, t1, t2)

            for s in range(2):
                for t in range(2):
                    z = kv[:, s, t, 0:256]
                    z3 = z.rearrange("p (h d) -> p h d", h=2)
                    head_norm(z3, tmp[:, 0:256].rearrange("p (h d) -> p h d", h=2), 2, 128, tok=(t_kv,))
                    tv = Q.v(lambda e, z3=z3: e.tensor_tensor(z3, z3, bc(sm("kg", 128 * l, 128 * l + 128).unsqueeze(1), [128, 2, 128]), ALU.mult))
                    if s == 0:
                        tv = rope2(z, t, 2)
                    t_kT = transpose4([z[:, h * 128:(h + 1) * 128] for h in range(2)],
                                      kTt[:, :, s * 256 + t * 128:s * 256 + (t + 1) * 128], (tv,))
            for s in range(nside):
                for f in range(2):
                    b, ps, bt = B.take()
                    for t in range(2):
                        Q.mm(ps[:, :], fp[:, s, t, f * 128:(f + 1) * 128], CS[:, t, :], t == 0, t == 1, (bt, t_fp, t_const))
                    pq = P[f]
                    ta = Q.a(lambda e, ps=ps, pq=pq: e.activation(pq, ps[:, :], ACT.Copy), Q.pe_done())
                    B.free(b, ta)
                fr = tmp[:, 0:512].rearrange("p (k t) -> p k t", k=2)
                b, ps, bt = B.take()
                for f in range(2):
                    for k in range(2):
                        Q.mm(ps[:, f * 256:(f + 1) * 256], BD[:, k * 128:(k + 1) * 128], P[f][:, k * 256:(k + 1) * 256], k == 0, k == 1,
                             (bt, ta))
                t_fr = Q.v(lambda e, ps=ps: e.tensor_copy(tmp[:, 0:512], ps[:, :]), Q.pe_done(), Q.last("act"))
                B.free(b, t_fr)
                b, ps, bt = B.take()
                for g in range(4):
                    o = 64 * (g % 2)
                    for t in range(2):
                        Q.mm(ps[o:o + 64, (g // 2) * 256:(g // 2 + 1) * 256], fp[:, s, t, 256 + g * 64:256 + (g + 1) * 64],
                             PA[:, g, t, :], t == 0, t == 1, (bt, t_pool, t_fp))
                dp = tmp[:, 512:1024]
                tv = Q.v(lambda e, ps=ps, dp=dp: e.tensor_copy(dp, ps[:, :]), Q.pe_done())
                B.free(b, tv)
                b, ps, bt = B.take()
                for g in range(4):
                    o = 64 * (g % 2)
                    wp = sm("w_pool", 128 * l + 64 * (g // 2), 128 * l + 64 * (g // 2) + 64)
                    Q.mm(ps[o:o + 64, (g // 2) * 256:(g // 2 + 1) * 256], wp[o:o + 64, :], dp[o:o + 64, (g // 2) * 256:(g // 2 + 1) * 256],
                         True, True, (bt, tv))
                pt = Q.pe_done()
                for k in range(2):
                    tv = Q.v(lambda e, ps=ps, k=k, s=s: e.tensor_scalar(mix[:, 2 + k, s, :], ps[:, k * 256:(k + 1) * 256],
                                                                        sm("pool_scale", 2 * l + k, 2 * l + k + 1), None, ALU.mult), pt)
                B.free(b, tv)
                if s == 0:
                    cf = R.load([(dr["w_four"][l].rearrange("j p f -> p j f"), 0, 512, 2)])
                b, ps, bt = B.take()
                for j in range(2):
                    for k in range(2):
                        Q.mm(ps[:, j * 256:(j + 1) * 256], cf.ap[:, (j * 2 + k) * 128:(j * 2 + k + 1) * 128], fr[:, k, :], k == 0, k == 1,
                             (bt, cf.tok, t_fr))
                ta = Q.a(lambda e, ps=ps, s=s: e.activation(mix[:, 0:2, s, :], ps[:, :].rearrange("p (k t) -> p k t", k=2), ACT.Copy), Q.pe_done())
                B.free(b, ta)
                t_fr = Q.pe_done()
                Q.v(lambda e: e.memset(dummy, 0.0), t_fr, ta)
                for t in range(2):
                    z = q_[:, t * 512:(t + 1) * 512]
                    tokens(cq.ap, 8, 0, 4, lhs(s, t), (cq.tok,) + tn,
                           lambda ps, pt, z=z: Q.a(lambda e: e.activation(z, ps[:, :], ACT.Copy), pt, Q.last("dve"), Q.last("pe")))
                    z3 = z.rearrange("p (h d) -> p h d", h=4)
                    head_norm(z3, tmp[:, 0:512].rearrange("p (h d) -> p h d", h=4), 4, 128, tok=(Q.last("act"),))
                    tv = Q.v(lambda e, z3=z3: e.tensor_tensor(z3, z3, bc(sm("qg", 128 * l, 128 * l + 128).unsqueeze(1), [128, 4, 128]), ALU.mult))
                    if s == 0:
                        tv = rope2(z, t, 4)
                    t_qT = transpose4([z[:, h * 128:(h + 1) * 128] for h in range(4)],
                                      qTt[:, :, t * 128:(t + 1) * 128], (tv,))
                if s == nside - 1:
                    cq.done(Q.pe_done())
                    cf.done(Q.pe_done())
                k0, nk = (0, 512) if s == 0 else (256, 256)
                kn = nk // 128
                free = [None, None]
                for h in range(4):
                    pt_ = PT[h % 2].rearrange("p (k t) -> p k t", k=4)
                    for t in range(2):
                        b, ps, bt = B.take()
                        Q.mm(ps[:, 0:nk], qTt[:, h, t * 128:(t + 1) * 128], kTt[:, h // 2, k0:k0 + nk], True, True, (bt, t_qT, t_kT))
                        pt = Q.pe_done()
                        m_ = rr[:, 8 + t:9 + t]
                        z_ = rr[:, 10 + t:11 + t]
                        Q.v(lambda e, ps=ps, m_=m_, nk=nk: e.tensor_reduce(m_, ps[:, 0:nk], AX.X, ALU.max), pt)
                        tv = Q.v(lambda e, m_=m_: e.tensor_scalar(m_, m_, -float(128 ** -0.5), None, ALU.mult))
                        p = P[t][:, 0:nk]
                        ta = Q.a(lambda e, p=p, ps=ps, nk=nk, m_=m_, z_=z_: e.activation(p, ps[:, 0:nk], ACT.Exp, bias=m_,
                                                                                         scale=float(128 ** -0.5), accum_out=z_), tv, pt, Q.last("pe"))
                        B.free(b, ta)
                        Q.v(lambda e, z_=z_: e.reciprocal(z_, z_), ta)
                        tv = Q.v(lambda e, p=p, z_=z_: e.tensor_scalar(p, p, z_, None, ALU.mult))
                        b, ps, bt = B.take()
                        for k in range(kn):
                            Q.tr(ps[:, k * 128:(k + 1) * 128], p[:, k * 128:(k + 1) * 128], ident, (bt, tv))
                        ta = Q.a(lambda e, ps=ps, t=t, pt_=pt_, nk=nk, kn=kn: e.activation(
                            pt_[:, 0:kn, t * 128:(t + 1) * 128], ps[:, 0:nk].rearrange("p (k t) -> p k t", k=kn), ACT.Copy),
                            Q.pe_done(), free[h % 2])
                        B.free(b, ta)
                    b, ps, bt = B.take()
                    g = h // 2
                    for k in range(kn):
                        kt = k0 // 128 + k
                        Q.mm(ps[:, 0:256], kv[:, kt // 2, kt % 2, 256 + g * 128:256 + (g + 1) * 128], pt_[:, k, :], k == 0, k == kn - 1,
                             (bt, ta, t_kv))
                    free[h % 2] = Q.pe_done()
                    ta = Q.a(lambda e, ps=ps, h=h, s=s: e.activation(mix[:, 4 + h, s, :], ps[:, 0:256], ACT.Copy), Q.pe_done())
                    B.free(b, ta)
            if dump is not None:
                dbg(f"mix2_{l}", sc(11520, 4096), tuple(lasts()))

            def take(ps, j, n, pt):
                for s in range(nside):
                    t = Q.v(lambda e, s=s: e.scalar_tensor_tensor(src[s][:, j, :], ps[:, s * 256:(s + 1) * 256], mod(l, 2, s)[:, j:j + 1],
                                                                  src[s][:, j, :], ALU.mult, ALU.add), pt)
                return t
            if nside == 2:
                dense(dr["w_out"][l], list(range(8)), 8, lambda q: mix[:, q, :, :], tuple(lasts()), take, width=512, per=1)
            else:
                dense(dr["w_out"][l], list(range(8)), 8, lambda q: mix[:, q, 0, :], tuple(lasts()), take, width=256, per=1)

        def lasts():
            return [Q.last("dve"), Q.last("act"), Q.pe_done()]

        def moe(l):
            nside = 2 if l == 0 else 1
            src = [x8, c8]
            xs = sc(0, 8192).rearrange("p (k s n) -> p k s n", k=8, s=2)
            PgT = sc(8192, 2048).rearrange("p (s i t) -> p s i t", s=2, i=4)
            P = sc(10240, 1024)
            Pg = sc(11264, 1024)
            yT = sc(10240, 2048).rearrange("p (k s n) -> p k s n", k=8, s=2)
            aff = sc(12288, 32)
            affT = sc(12320, 256)
            msk = sc(12576, 256)
            cs = sc(12832, 256)
            sl = sc(13088, 32)
            lg = sc(13120, 32)
            st = sc(13152, 16)
            y = nT[:, 0:2048].rearrange("p (s f) -> p s f", s=2)
            gs = [nT[:, 2048:2560], nT[:, 2560:3072]]
            aT = [nT[:, 3072:3584], nT[:, 3584:4096]]
            for side in range(nside):
                dst = scales(l, "n2", 4, side)
                tn = norm(src[side], lambda k, side=side: n2[:, k, side, :], dst, mod(l, 3, side), tuple(lasts()))
                tn = tn + (Q.last("act"), Q.last("dve"))
                wr = sm("w_router", 128 * l, 128 * l + 128).rearrange("p (k n) -> p k n", k=8)
                for t in range(2):
                    b, ps, bt = B.take()
                    for q in range(8):
                        Q.mm(ps[:, 0:16], n2[:, q, side, t * 128:(t + 1) * 128], wr[:, q, :], q == 0, q == 7, (bt,) + tn)
                    L = lg[:, 16 * t:16 * t + 16]
                    A = aff[:, 16 * t:16 * t + 16]
                    Q.v(lambda e, ps=ps, L=L: e.tensor_copy(L, ps[:, 0:16]), Q.pe_done())
                    B.free(b, Q.last("dve"))
                    Q.v(lambda e, L=L, t=t: e.tensor_reduce(st[:, t:t + 1], L, AX.X, ALU.max))
                    tv = Q.v(lambda e, t=t: e.tensor_scalar(st[:, t:t + 1], st[:, t:t + 1], -1.0, None, ALU.mult))
                    ta = Q.a(lambda e, A=A, L=L, t=t: e.activation(A, L, ACT.Exp, bias=st[:, t:t + 1], accum_out=st[:, 2 + t:3 + t]), tv)
                    Q.v(lambda e, t=t: e.reciprocal(st[:, 2 + t:3 + t], st[:, 2 + t:3 + t]), ta)
                    tv = Q.v(lambda e, A=A, t=t: e.tensor_scalar(A, A, st[:, 2 + t:3 + t], None, ALU.mult))
                if dump is not None:
                    dbg(f"aff{l}{side}", aff, tuple(lasts()))
                b, ps, bt = B.take()
                for t in range(2):
                    Q.tr(ps[0:16, t * 128:(t + 1) * 128], aff[:, 16 * t:16 * t + 16], ident, (bt, tv))
                Q.v(lambda e, ps=ps: e.tensor_copy(affT[0:16, :], ps[0:16, 0:256]), Q.pe_done())
                B.free(b, Q.last("dve"))
                for _ in range(CAP // 8):
                    Q.v(lambda e: e.max(st[0:16, 8:16], affT[0:16, :]))
                    Q.v(lambda e: e.match_replace(affT[0:16, :], st[0:16, 8:16], affT[0:16, :], -1.0))
                Q.v(lambda e: e.tensor_scalar(msk[0:16, :], affT[0:16, :], -1.0, None, ALU.is_equal))
                Q.v(lambda e: e.tensor_tensor_scan(cs[0:16, :], bc(ones[0:16, 0:1], [16, 256]), msk[0:16, :], 0.0, ALU.mult, ALU.add))
                Q.v(lambda e: e.tensor_tensor(cs[0:16, :], cs[0:16, :], msk[0:16, :], ALU.mult))
                tv = Q.v(lambda e: e.tensor_scalar(cs[0:16, :], cs[0:16, :], -1.0, None, ALU.add))
                b, ps, bt = B.take()
                for t in range(2):
                    Q.tr(ps[:, t * 16:(t + 1) * 16], cs[0:16, t * 128:(t + 1) * 128], ident[0:16, 0:16], (bt, tv))
                Q.v(lambda e, ps=ps: e.tensor_copy(sl, ps[:, 0:32]), Q.pe_done())
                B.free(b, Q.last("dve"))
                for t in range(2):
                    pv = P[:, t * 512:(t + 1) * 512].rearrange("p (e j) -> p e j", e=16)
                    pg = Pg[:, t * 512:(t + 1) * 512].rearrange("p (e j) -> p e j", e=16)
                    Q.v(lambda e, pv=pv, t=t: e.tensor_tensor(pv, bc(sm("iota").unsqueeze(1), [128, 16, 32]),
                                                              bc(sl[:, 16 * t:16 * t + 16].unsqueeze(2), [128, 16, 32]), ALU.is_equal), Q.last("pe"))
                    tv = Q.v(lambda e, pv=pv, pg=pg, t=t: e.tensor_tensor(pg, pv, bc(aff[:, 16 * t:16 * t + 16].unsqueeze(2), [128, 16, 32]), ALU.mult))
                for t in range(2):
                    transpose4([Pg[:, t * 512 + i * 128:t * 512 + (i + 1) * 128] for i in range(4)],
                               PgT[:, side, :, t * 128:(t + 1) * 128], (tv,))
                hk = wk[:, :].rearrange("p (t f) -> p t f", t=2)
                for t in range(2):
                    for hf in range(2):
                        t_h = transpose4([n2[:, hf * 4 + i, side, t * 128:(t + 1) * 128] for i in range(4)],
                                         hk[:, t, hf * 512:(hf + 1) * 512].rearrange("p (i t) -> p i t", i=4), tn + (tv,))
                for k in range(8):
                    b, ps, bt = B.take()
                    for t in range(2):
                        Q.mm(ps[:, :], hk[:, t, k * 128:(k + 1) * 128], P[:, t * 512:(t + 1) * 512], t == 0, t == 1, (bt, t_h, tv))
                    if k % 2:
                        tx = Q.a(lambda e, ps=ps, k=k, side=side: e.activation(xs[:, k, side, :], ps[:, :], ACT.Copy), Q.pe_done())
                    else:
                        tx = Q.v(lambda e, ps=ps, k=k, side=side: e.tensor_copy(xs[:, k, side, :], ps[:, :]), Q.pe_done())
                    B.free(b, tx)
            tx = tuple(lasts())
            w = 32 * nside
            afree = [None, None]
            for e_ in range(NE):
                rhs = lambda q, e_=e_: xs[:, q, 0:nside, e_ * 32:(e_ + 1) * 32]
                A = aT[e_ % 2]
                G = gs[e_ % 2]
                ta = None

                def gate(ps, j, n, pt, G=G, e_=e_):
                    return Q.a(lambda e: e.activation(G[:, 0:8 * w], ps[:, 0:8 * w], ACT.Silu), pt, afree[e_ % 2])
                dense(dr["moe_gate"][l][e_], list(range(8)), 8, rhs, tx, gate, width=w, per=8)
                tg = Q.last("act")

                def up(ps, j, n, pt, G=G, A=A, e_=e_, tg=tg):
                    return Q.v(lambda e: e.tensor_tensor(A[:, 0:8 * w], ps[:, 0:8 * w], G[:, 0:8 * w], ALU.mult), pt, tg, afree[e_ % 2])
                dense(dr["moe_up"][l][e_], list(range(8)), 8, rhs, tx, up, width=w, per=8)
                tu = Q.last("dve")
                i4 = e_ % 4

                def down(ps, j, n, pt, i4=i4):
                    return Q.v(lambda e: e.tensor_copy(yT[:, :, 0:nside, i4 * 32:(i4 + 1) * 32],
                                                       ps[:, 0:8 * w].rearrange("p (k s n) -> p k s n", k=8, s=nside)), pt)
                dense(dr["moe_down"][l][e_], list(range(8)), 8, lambda q, A=A: A[:, q * w:(q + 1) * w], (tu,), down, width=w, per=8)
                afree[e_ % 2] = Q.pe_done()
                if i4 == 3:
                    tq = Q.last("dve")
                    eg = e_ // 4
                    for s in range(nside):
                        for hf in range(2):
                            t_y = transpose4([yT[:, hf * 4 + i, s, :] for i in range(4)],
                                             y[:, s, hf * 512:(hf + 1) * 512].rearrange("p (i t) -> p i t", i=4), (tq,))
                        for k in range(8):
                            if k % 2 == 0:
                                b, ps, bt = B.take()
                            o = (k % 2) * 256
                            Q.mm(ps[:, o:o + 256], y[:, s, k * 128:(k + 1) * 128], PgT[:, s, eg, :], True, True, (bt, t_y))
                            if k % 2:
                                pt = Q.pe_done()
                                for kk in (k - 1, k):
                                    tv = Q.v(lambda e, ps=ps, kk=kk, s=s: e.scalar_tensor_tensor(
                                        src[s][:, kk, :], ps[:, (kk % 2) * 256:(kk % 2) * 256 + 256], mod(l, 5, s)[:, kk:kk + 1],
                                        src[s][:, kk, :], ALU.mult, ALU.add), pt)
                                B.free(b, tv)
                    Q.v(lambda e: e.memset(dummy, 0.0), Q.pe_done())

        steps = [even, lambda: ffn(0), lambda: ple(0), odd, lambda: ffn(1), lambda: ple(1)]
        for i, st_ in enumerate(steps):
            if i < upto:
                st_()
                if dump is not None:
                    dbg(f"x{i}", xT[:, :], (Q.last("dve"),))
        if upto > 6:
            ada(0)
            t_const = load_consts()
            mixer2(0)
            if dump is not None:
                dbg("x6", xT[:, :], (Q.last("dve"),))
                dbg("c6", cT[:, :], (Q.last("dve"),))
            moe(0)
            if dump is not None:
                dbg("x7", xT[:, :], (Q.last("dve"),))
                dbg("c7", cT[:, :], (Q.last("dve"),))
        if upto > 8:
            ada(1)
            Q.dma("pool", sc(0, 1280), dr["dft"], s_c, tuple(lasts()))
            t_const = ("s_c", Q.count["s_c"])
            mixer2(1)
            moe(1)

        t_o = Q.dma("sp", out_dram, xT[:, :], s_out, (Q.last("dve"),))
        nc.sync.wait_ge(Q.sem[t_o[0]], t_o[1])


def constants():
    f = np.float32
    i = np.arange(128)
    c = {}
    c["ident"] = np.eye(128, dtype=f)
    c["ones"] = np.ones((128, 128), f)
    inv = []
    for dim in (64, 32):
        e = np.arange(0, dim, 2, dtype=f) / f(dim)
        inv.append((1.0 / np.power(f(10000.0), e)).astype(f))
    c["invf"] = np.tile(np.concatenate(inv)[None, :], (128, 1))
    c["tri"] = np.where(i[None, :] <= i[:, None], 0.0, -BIG).astype(f)
    c["iota"] = np.tile(np.arange(32, dtype=f)[None, :], (128, 1))
    t = np.arange(256)
    inv2 = 10000.0 ** (-np.arange(0, 64, 2, dtype=np.float64) / 64)
    ang = np.stack([(t // 64)[:, None] * inv2, (t % 64)[:, None] * inv2], 1).reshape(2, 128, 64)
    c["rcos"] = np.cos(ang).transpose(1, 0, 2).reshape(128, 128).astype(f)
    c["rsin"] = np.sin(ang).transpose(1, 0, 2).reshape(128, 128).astype(f)
    lv = []
    for l in range(6):
        b = 1 << l
        same = (i[:, None] // (2 * b)) == (i[None, :] // (2 * b))
        lv.append((same & ((i[:, None] // b) % 2 == 0) & ((i[None, :] // b) % 2 == 1)).astype(f))
    c["levels"] = np.concatenate(lv, 1)
    same = (i[:, None] // 64) == (i[None, :] // 64)
    c["cumT"] = (same & (i[:, None] <= i[None, :])).astype(f)
    c["lastT"] = (same & (i[:, None] % 64 == 63)).astype(f)
    c["sel"] = np.concatenate([np.tile((i == 63 + 64 * j).astype(f)[:, None], (1, 128)) for j in range(2)], 1)
    c["dmask"] = np.where(same & (i[None, :] <= i[:, None]), 0.0, BIG).astype(f)
    n = np.arange(256)
    a = 2 * np.pi * ((n[:, None] * n[None, :]) % 256) / 256
    cs = np.concatenate([np.cos(a), np.sin(a)], 1) / 16.0
    cs = cs.reshape(2, 128, 512).transpose(1, 0, 2).reshape(128, 1024)
    d = np.arange(64)
    b = 2 * np.pi * ((d[:, None] * d[None, :]) % 64) / 64
    bd = np.zeros((128, 256))
    for k in range(2):
        bd[64 * k:64 * k + 64, 64 * k:64 * k + 64] = np.cos(b) / 8.0
        bd[64 * k:64 * k + 64, 128 + 64 * k:128 + 64 * k + 64] = -np.sin(b) / 8.0
    dft = np.concatenate([cs, bd], 1).astype(f)
    pa = []
    for win in (2, 4, 8, 16):
        lo = np.clip(n - win // 2, 0, 256)
        hi = np.clip(n + win // 2, 0, 256)
        s = n[:, None]
        m = ((s >= lo[None, :]) & (s < hi[None, :])) / (hi - lo)[None, :].astype(np.float64) - np.eye(256)
        pa.append(m.reshape(2, 128, 256).transpose(1, 0, 2).reshape(128, 512))
    return c, dft, np.concatenate(pa, 1).astype(f)


def layout(a):
    cat, asc = np.concatenate, np.ascontiguousarray

    def blocks(w):
        lead = w.shape[:-2]
        k, n = w.shape[-2:]
        w = w.reshape(*lead, k // 128, 128, n // 128, 128)
        r = len(lead)
        w = w.transpose(*range(r), r + 2, r + 1, r, r + 3)
        return asc(w.reshape(*lead, n // 128, 128, k))

    def tail(w):
        k, n = w.shape
        return asc(w.reshape(k // 128, 128, n).transpose(1, 0, 2).reshape(128, -1))

    def featT(x):
        t, k = x.shape
        return asc(x.T.reshape(k // 128, 128, t).transpose(1, 0, 2).reshape(128, -1))

    def cols(v):
        v = v.reshape(-1, 128)
        return v.T

    def rows(v):
        return np.broadcast_to(v.reshape(1, -1), (128, v.size))

    const, dft, poolA = constants()
    s = dict(const)
    s["xtiny"] = rows(a["od_a_log"][0][0:2])
    s["norm_mix"] = cols(a["norm_mix_g"])
    s["norm_ffn"] = cols(a["norm_ffn_g"])
    s["ple_post"] = cols(a["ple_post_norm_g"])
    s["ple_norm"] = cols(a["ple_norm_g"])
    s["ev_conv"] = a["ev_conv_w"][0].reshape(3, 4, 128).transpose(2, 1, 0).reshape(128, 12)
    s["od_conv"] = a["od_conv_w"][0].reshape(4, 24, 128).transpose(2, 1, 0).reshape(128, 96)
    s["ev_qg"] = rows(a["ev_q_norm_g"])
    s["ev_kg"] = rows(a["ev_k_norm_g"])
    s["ln_g"] = rows(a["ev_ik_ln_g"])
    s["ln_b"] = rows(a["ev_ik_ln_b"])
    s["o_g"] = rows(a["od_o_norm_g"])
    s["a_log"] = rows(a["od_a_log"])
    s["dt_bias"] = rows(a["od_dt_bias"])
    s["c2"] = np.stack([cols(a["c_2"]), cols(a["c_ctx_2"])], 2).reshape(128, 16)
    s["ada_b"] = cols(a["ada_b_2"])
    s["n1"] = cols(a["norm1_g_2"])
    s["n2"] = cols(a["norm2_g_2"])
    s["pool_scale"] = cols(a["pool_scale_2"])
    s["qg"] = rows(a["q_norm_g_2"])
    s["kg"] = rows(a["k_norm_g_2"])
    s["w_pool"] = a["w_pool_2"].reshape(2, 2, 128, 64).transpose(2, 0, 1, 3).reshape(128, 256)
    s["w_router"] = a["w_router_2"].reshape(2, 8, 128, 16).transpose(2, 0, 1, 3).reshape(128, 256)
    small = cat([np.asarray(s[n]).reshape(128, w) for n, w in SMALL], 1)
    ev, od = a["ev_w_in"][0], a["od_w_in"][0]
    return {
        "small": asc(small), "xT": featT(a["x"][0]), "ctxT": featT(a["ctx_2"][0]),
        "posT": asc(a["positions"].reshape(2, 128).T), "dft": dft, "poolA": poolA,
        "pT": asc(np.stack([featT(a["p"][l, 0]) for l in range(2)])),
        "ev_in": blocks(ev[:, :3584]), "ev_tail": tail(ev[:, 3584:]), "ev_out": blocks(a["ev_w_out"][0]),
        "od_in": blocks(od[:, :4096]), "od_tail": tail(od[:, 4096:]), "od_out": blocks(a["od_w_out"][0]),
        "ffn_gate": blocks(a["ffn_w_gate"]), "ffn_up": blocks(a["ffn_w_up"]), "ffn_down": blocks(a["ffn_w_down"]),
        "ple_proj": blocks(a["ple_w_proj"]), "ple_gate": blocks(a["ple_w_gate"]),
        "ada": blocks(a["ada_w_2"]), "w_in": blocks(a["w_in_2"]), "w_out": blocks(a["w_out_2"]),
        "w_four": blocks(a["w_fourier_2"]),
        "moe_gate": blocks(a["w_gate_2"]), "moe_up": blocks(a["w_up_2"]), "moe_down": blocks(a["w_down_2"]),
    }


def kernel(**inputs):
    import numpy as _np
    import concourse.bacc as _bacc
    from concourse import mybir as _mybir
    from concourse.bass_utils import run_bass_kernel_spmd as _run

    nc = _bacc.Bacc("TRN2", target_bir_lowering=False, num_devices=1)
    arrays = layout({k: _np.asarray(v) for k, v in inputs.items()})
    dr = {n: nc.dram_tensor(n, v.shape, _mybir.dt.from_np(v.dtype), kind="ExternalInput").ap() for n, v in arrays.items()}
    out = nc.dram_tensor("out", (128, 2048), _mybir.dt.float32, kind="ExternalOutput").ap()
    program(nc, dr, out)
    r = _run(nc, [arrays], core_ids=[0])
    o = r.results[0]["out"].reshape(128, 8, 256)
    return _np.ascontiguousarray(o.transpose(2, 1, 0).reshape(1, 256, 1024))
```

```python
from contextlib import ExitStack

import numpy as np
import concourse.bass as bass
from concourse import mybir

F32 = mybir.dt.float32
F32R = mybir.dt.float32r
I32 = mybir.dt.int32
ALU = mybir.AluOpType
ACT = mybir.ActivationFunctionType
AX = mybir.AxisListType

D = 1024
EPS = 1e-6
BIG = 1e30
TAKEN = -3e38
RING = 3
MORE = 3
NB = 3
AHEAD = 2
SLOT = 4096
NE = 16
CAP = 32
MAGIC = 12582912.0
TWO_PI_A = 6.28125
TWO_PI_B = 0.00193500518798828125
TWO_PI_C = float(2 * np.pi - 6.28125 - 0.00193500518798828125)

SMALL = [
    ("xtiny", 2), ("norm_mix", 16), ("norm_ffn", 16), ("ple_post", 16), ("ple_norm", 16),
    ("ev_conv", 12), ("od_conv", 96), ("ev_qg", 64), ("ev_kg", 64), ("ln_g", 64), ("ln_b", 64),
    ("o_g", 128), ("a_log", 8), ("dt_bias", 8),
    ("c2", 16), ("ada_b", 96), ("n1", 16), ("n2", 16), ("pool_scale", 4),
    ("qg", 256), ("kg", 256), ("w_pool", 256), ("w_router", 256),
    ("ident", 128), ("ones", 128), ("invf", 48), ("tri", 128), ("iota", 32),
    ("rcos", 128), ("rsin", 128), ("levels", 768), ("cumT", 128), ("lastT", 128),
    ("sel", 256), ("dmask", 128),
]
OFF = {}
_at = 0
for _n, _w in SMALL:
    OFF[_n] = (_at, _w)
    _at += _w
NSMALL = _at


class Queues:

    def __init__(self, nc, ctx, dry):
        self.nc, self.ctx, self.dry = nc, ctx, dry
        self.eng = {"pe": nc.tensor, "act": nc.scalar, "dve": nc.vector, "pool": nc.gpsimd, "sp": nc.sync}
        self.sem = {n: ctx.enter_context(nc.semaphore("s_" + n)) for n in self.eng}
        self.count = {n: 0 for n in self.sem}
        self.seen = {n: {} for n in self.eng}
        self.mm_last = None
        self.names = 0

    def count_names(self):
        self.names += 1
        return self.names

    def new_sem(self, name):
        self.sem[name] = self.ctx.enter_context(self.nc.semaphore(name))
        self.count[name] = 0
        return name

    def put(self, eng, fn, after=(), inc=None, by=1):
        if self.dry:
            return inc, 0
        e = self.eng[eng]
        flat = list(after)
        for t in flat:
            if t is None:
                continue
            if isinstance(t[0], tuple):
                flat.extend(t)
                continue
            name, value = t
            if self.seen[eng].get(name, 0) < value:
                self.seen[eng][name] = value
                e.wait_ge(self.sem[name], value)
        ins = fn(e)
        if inc:
            ins.then_inc(self.sem[inc], by)
            self.count[inc] += by
            return inc, self.count[inc]
        self.mm_last = ins
        return None

    def mm(self, out, lhsT, rhs, start, stop, after=(), skip=False):
        self.put("pe", lambda e: e.matmul(out, lhsT, rhs, start=start, stop=stop, skip_group_check=skip), after)

    def tr(self, out, in_, ident, after=()):
        self.put("pe", lambda e: e.transpose(out, in_, ident), after)

    def pe_done(self):
        if self.mm_last is not None:
            self.mm_last.then_inc(self.sem["pe"], 1)
            self.mm_last = None
            self.count["pe"] += 1
        return "pe", self.count["pe"]

    def _one(self, eng, fn, after, link):
        prev = (eng, self.count[eng]) if link else None
        return self.put(eng, fn, (prev,) + tuple(after), eng)

    def v(self, fn, *after, link=True):
        return self._one("dve", fn, after, link)

    def a(self, fn, *after, link=True):
        return self._one("act", fn, after, link)

    def g(self, fn, *after, link=True):
        return self._one("pool", fn, after, link)

    def last(self, eng):
        return (eng, self.count[eng])

    def dma(self, eng, out, in_, sem, after=()):
        return self.put(eng, lambda e: e.dma_start(out, in_), after, sem, 16)


class Banks:

    def __init__(self, nc, ctx):
        self.bank = [ctx.enter_context(nc.psum_tensor(f"ps{i}", [128, 512], F32)) for i in range(8)]
        self.idle = [(i, None) for i in range(8)]

    def take(self):
        i, tok = self.idle.pop(0)
        return i, self.bank[i], tok

    def free(self, i, tok):
        self.idle.append((i, tok))


class Slot:

    def __init__(self, ap, sem, free=None):
        self.ap, self.sem, self.free = ap, sem, free


class Chunk:

    def __init__(self, ws, n, key):
        self.ws, self.n, self.key = ws, n, key

    def raw(self):
        return self.ws.load(self.n)

    def piece(self, i):
        return self.ws.split(self.n, i)

    def done(self, tok):
        self.ws.release(self.n, tok)


class Weights:

    def __init__(self, Q, dr, plan):
        self.Q, self.dr, self.plan = Q, dr, plan
        self.asked = []
        self.idle = []
        self.place = {}
        self.parts = {}
        self.used = {}
        self.units = []
        self.at = 0
        self.turn = 0
        self.part_free = [None] * NB
        if plan is not None:
            for n, key in enumerate(plan):
                if key[-1] == "raw":
                    self.units.append((n, None))
                else:
                    self.units += [(n, i) for i in range(self.pieces(key))]

    @staticmethod
    def pieces(key):
        _, _, _, m, kt, mode = key
        return kt // 2 if mode == "tok" else -(-m * kt // 8)

    def ask(self, name, idx, j0, m, kt, mode):
        key = (name, idx, j0, m, kt, mode)
        self.asked.append(key)
        n = len(self.asked) - 1
        assert self.plan is None or self.plan[n] == key
        return Chunk(self, n, key)

    def load(self, n):
        if self.Q.dry:
            return self.slots[0].ap, None
        if n not in self.place:
            assert n == len(self.place)
            slot = self.idle.pop(0)
            name, idx, j0, m, kt, _ = self.plan[n]
            w = self.dr[name]
            for i in idx:
                w = w[i]
            f = kt * 128
            dst = slot.ap[:, 0:m * f]
            tok = self.Q.dma("sp", dst.rearrange("p (j f) -> p j f", j=m), w[j0:j0 + m].rearrange("j p f -> p j f"),
                             slot.sem, (slot.free,))
            self.place[n] = (slot, tok)
        slot, tok = self.place[n]
        return slot.ap, tok

    def release(self, n, tok):
        if self.Q.dry:
            return
        slot = self.place[n][0]
        slot.free = tok
        self.idle.append(slot)

    def emit(self):
        if self.at >= len(self.units):
            return False
        n, i = self.units[self.at]
        if i is None or (n not in self.place and not self.idle):
            return False
        if len(self.parts) + self.held >= NB:
            return False
        ap, tok = self.load(n)
        _, _, _, m, kt, mode = self.plan[n]
        b = self.at_part % NB
        self.at_part += 1
        if mode == "tok":
            src = ap[:, 0:m * kt * 128].rearrange("p (j f) -> p j f", j=m)[:, :, i * 256:(i + 1) * 256]
            width = m * 256
            view = lambda x: x[:, 0:width].rearrange("p (j f) -> p j f", j=m)
        else:
            width = min(1024, m * kt * 128 - i * 1024)
            src = ap[:, i * 1024:i * 1024 + width]
            view = lambda x: x[:, 0:width]
        H, L = self.WH[:, b, :], self.WL[:, b, :]
        free = self.part_free[b]
        tH = self.Q.a(lambda e: e.activation(view(H), src, ACT.Copy), tok, free, link=False)
        tL = self.Q.v(lambda e: e.tensor_tensor(view(L), src, view(H).bitcast(F32), ALU.subtract), tok, tH, free, link=False)
        self.parts[(n, i)] = (H, L, tH, tL, b)
        self.at += 1
        if self.at == len(self.units) or self.units[self.at][0] != n:
            self.release(n, tL)
        return True

    at_part = 0
    held = 0

    def split(self, n, i):
        if self.Q.dry:
            return self.WH[:, 0, :], self.WL[:, 0, :], None, None, 0
        while (n, i) not in self.parts:
            while self.units[self.at][1] is None:
                self.at += 1
            assert self.emit()
        p = self.parts.pop((n, i))
        self.held += 1
        for _ in range(AHEAD - (len(self.parts))):
            if not self.emit():
                break
        return p

    def free_part(self, p, tok):
        self.part_free[p[4]] = tok
        self.held -= not self.Q.dry


def bc(ap, shape):
    return ap.to_broadcast(shape)


def program(nc, dr, out_dram, plan=None, dry=False, upto=99, dump=None):
    with ExitStack() as ctx:
        Q = Queues(nc, ctx, dry)
        B = Banks(nc, ctx)
        W = Weights(Q, dr, plan)

        def sb(name, n):
            return ctx.enter_context(nc.sbuf_tensor("m_" + name, [128, n], F32))

        small = sb("small", NSMALL)
        xT = sb("xT", 2048)
        cT = sb("cT", 2048)
        wk = sb("wk", 2048)
        misc = sb("misc", 1152)
        adaT = sb("adaT", 512)
        ring = ctx.enter_context(nc.sbuf_tensor("ring", [128, RING, SLOT], F32))
        for i in range(RING + MORE):
            Q.new_sem(f"slot{i}")
        W.slots = [Slot(ring[:, i, :], f"slot{i}") for i in range(RING)]
        W.idle = list(W.slots)
        posi = ctx.enter_context(nc.sbuf_tensor("posi", [128, 2], I32))

        def sm(name, a=0, b=None):
            o, w = OFF[name]
            return small[:, o + a:o + (w if b is None else b)]

        area = {}

        def open_area(ph, name, n, dt=F32):
            area[name] = ph.enter_context(nc.sbuf_tensor(f"{name}_{Q.count_names()}", [128, n], dt))
            return area[name]

        def sc(off, n):
            assert off + n <= area["sc"].shape[1]
            return area["sc"][:, off:off + n]

        x8 = xT[:, :].rearrange("p (k t) -> p k t", k=8)
        c8 = cT[:, :].rearrange("p (k t) -> p k t", k=8)
        wk8 = wk[:, :].rearrange("p (k t) -> p k t", k=8)
        ident = sm("ident")
        ones = sm("ones")

        mo = [0]

        def mi(n):
            mo[0] += n
            assert mo[0] <= 1152
            return misc[:, mo[0] - n:mo[0]]

        dumps = []

        def dbg(name, ap, tok):
            if dump is not None:
                t = nc.dram_tensor("dbg_" + name, list(ap.shape), F32, kind="ExternalOutput").ap()
                w = Q.dma("pool", t, ap, Q.new_sem("dbg_" + name), tok)
                dump.append("dbg_" + name)
                Q.v(lambda e: e.memset(dummy, 0.0), w)
                Q.a(lambda e: e.activation(dummy[:, 0:1], dummy[:, 1:2], ACT.Copy), Q.last("dve"))
                Q.v(lambda e: e.memset(dummy, 0.0), Q.last("act"))

        s_out = Q.new_sem("s_out")
        dummy = misc[:, 1150:1152]

        s_in = Q.new_sem("s_in")
        half = (NSMALL // 2)
        Q.dma("sp", xT[:, :], dr["xT"], s_in)
        Q.dma("sp", posi[:, :], dr["posT"], s_in)
        Q.dma("sp", small[:, 0:half], dr["small"][:, 0:half], s_in)
        t_in = Q.dma("sp", small[:, half:NSMALL], dr["small"][:, half:NSMALL], s_in)

        def dense(name, idx, tiles, kt, xH, xL, tok, consume, per=2, width=256):
            m = 4 if kt == 8 else (8 if kt == 2 else 1)
            i = 0
            held = None
            while i < len(tiles):
                k = min(m, len(tiles) - i)
                c = W.ask(name, idx, tiles[i], k, kt, "T")
                nb = k * kt
                for p0 in range(0, nb, 8):
                    part = c.piece(p0 // 8)
                    H, L, tH, tL, _ = part
                    blocks = list(range(p0, min(p0 + 8, nb)))
                    while blocks:
                        j = blocks[0] // kt
                        mine = [n for n in blocks if n // kt == j]
                        blocks = blocks[len(mine):]
                        g = (i + j) % per
                        first, last = mine[0] % kt == 0, mine[-1] % kt == kt - 1
                        if g == 0 and first:
                            held = B.take()
                        b, ps, bt = held
                        o = ps[:, g * width:(g + 1) * width]
                        for n in mine:
                            w = H[:, (n - p0) * 128:(n - p0 + 1) * 128]
                            Q.mm(o, w, xH(n % kt), first and n == mine[0], False, (tH, bt) + tok)
                            Q.mm(o, w, xL(n % kt), False, False)
                        for n in mine:
                            w = L[:, (n - p0) * 128:(n - p0 + 1) * 128]
                            Q.mm(o, w, xH(n % kt), False, last and n == mine[-1], (tL,))
                        if last and (g == per - 1 or i + j == len(tiles) - 1):
                            pt = Q.pe_done()
                            B.free(b, consume(ps, i + j - g, g + 1, pt))
                    W.free_part(part, Q.pe_done())
                i += k

        def by_token(name, idx, j0, xH, xL, which, tok, consume):
            c = W.ask(name, idx, j0, 4, 8, "tok")
            held = [B.take() for _ in which]
            for i in range(4):
                part = c.piece(i)
                H, L, tH, tL, _ = part
                H4 = H.rearrange("p (j k n) -> p j k n", j=4, k=2)
                L4 = L.rearrange("p (j k n) -> p j k n", j=4, k=2)
                for (b, ps, bt), st in zip(held, which):
                    o = ps[:, :].rearrange("p (j n) -> p j n", j=4)
                    for k in range(2):
                        q = 2 * i + k
                        Q.mm(o, xH(q, *st), H4[:, :, k, :], q == 0, False, (tH, bt) + tok)
                        Q.mm(o, xL(q, *st), H4[:, :, k, :], False, False)
                    for k in range(2):
                        q = 2 * i + k
                        Q.mm(o, xH(q, *st), L4[:, :, k, :], False, q == 7, (tL,))
                W.free_part(part, Q.pe_done())
            pt = Q.pe_done()
            for (b, ps, bt), st in zip(held, which):
                B.free(b, consume(ps, pt, *st))

        rr = mi(256)

        def power(ap):
            t = Q.v(lambda e: e.reciprocal(ap, ap))
            return Q.a(lambda e: e.activation(ap, ap, ACT.Sqrt), t)

        def rstd(ps, n, dim, eps, tok):
            Q.v(lambda e: e.tensor_scalar(rr[:, 0:n], ps, 1.0 / dim, eps, ALU.mult, ALU.add), tok)
            return power(rr[:, 0:n])

        def norm(src, gain, shift, tok, outH=None, outL=None, out=None, full=None):
            b, ps, bt = B.take()
            ta = Q.a(lambda e: e.activation(wk8[:, 0:4, :], src[:, 0:4, :], ACT.Square), *tok)
            Q.v(lambda e: e.tensor_tensor(wk8[:, 4:8, :], src[:, 4:8, :], src[:, 4:8, :], ALU.mult), *tok)
            t = Q.v(lambda e: e.tensor_reduce(rr[:, 0:256], wk8.rearrange("p k t -> p t k"), AX.X, ALU.add), ta)
            Q.mm(ps[:, 0:256], ones, rr[:, 0:256], True, True, (t, bt))
            tp = rstd(ps[:, 0:256], 256, D, EPS, Q.pe_done())
            B.free(b, Q.last("dve"))
            first = tuple(tok) + (Q.last("dve"), Q.last("act"), tp)
            for k in range(8):
                y = wk8[:, k, :] if out is None else out(k)
                t = Q.v(lambda e: e.scalar_tensor_tensor(y, src[:, k, :], gain[:, k:k + 1], rr[:, 0:256],
                                                         ALU.mult, ALU.mult), *first, link=False)
                if out is not None:
                    if shift is not None:
                        t = Q.a(lambda e: e.activation(y, y, ACT.Identity, bias=shift[:, k:k + 1]), t, link=False)
                elif shift is None:
                    ta = Q.a(lambda e: e.activation(outH(k), y, ACT.Copy), t, *first, link=False)
                    t = Q.v(lambda e: e.tensor_tensor(outL(k), y, outH(k).bitcast(F32), ALU.subtract), ta, link=False)
                else:
                    ta = Q.a(lambda e: e.activation(outH(k), y, ACT.Identity, bias=shift[:, k:k + 1]), t, *first, link=False)
                    t = Q.v(lambda e: e.scalar_tensor_tensor(outL(k), y, shift[:, k:k + 1], outH(k).bitcast(F32),
                                                             ALU.add, ALU.subtract), ta, link=False)
            return (Q.last("dve"), Q.last("act"))

        def parts(H, L, src, tok, rtok=()):
            ta = Q.a(lambda e: e.activation(H, src, ACT.Copy), *tok, *rtok)
            return ta, Q.v(lambda e: e.tensor_tensor(L, src, H.bitcast(F32), ALU.subtract), ta, *rtok)

        def transpose4(parts, dst, tok, eng="act"):
            b, ps, bt = B.take()
            for i, p in enumerate(parts):
                Q.tr(ps[:, i * 128:(i + 1) * 128], p, ident, (bt,) + tok)
            pt = Q.pe_done()
            n = len(parts)
            src = ps[:, 0:n * 128].rearrange("p (i t) -> p i t", i=n)
            if eng == "act":
                t = Q.a(lambda e: e.activation(dst, src, ACT.Copy), pt)
            else:
                t = Q.v(lambda e: e.tensor_copy(dst, src), pt)
            B.free(b, t)
            return t

        def head_norm(z, tmp, heads, dim, scale_to=None, tok=()):
            Q.v(lambda e: e.tensor_tensor(tmp, z, z, ALU.mult), *tok)
            Q.v(lambda e: e.tensor_reduce(rr[:, 0:heads], tmp, AX.X, ALU.add))
            Q.v(lambda e: e.tensor_scalar(rr[:, 0:heads], rr[:, 0:heads], 1.0 / (scale_to or dim), EPS, ALU.mult, ALU.add))
            tp = power(rr[:, 0:heads])
            return Q.v(lambda e: e.tensor_tensor(z, z, bc(rr[:, 0:heads].unsqueeze(2), [128, heads, dim]), ALU.mult), tp)

        def rope(o1, o2, x1, x2, c, s, t1, t2):
            Q.v(lambda e: e.tensor_tensor(t1, x1, c, ALU.mult))
            Q.v(lambda e: e.tensor_tensor(t2, x2, s, ALU.mult))
            Q.v(lambda e: e.tensor_tensor(t1, t1, t2, ALU.subtract))
            Q.v(lambda e: e.tensor_tensor(t2, x1, s, ALU.mult))
            Q.v(lambda e: e.tensor_tensor(o2, x2, c, ALU.mult))
            Q.v(lambda e: e.tensor_tensor(o2, o2, t2, ALU.add))
            return Q.v(lambda e: e.tensor_copy(o1, t1))

        def hl(ph, k, s=1):
            H = open_area(ph, "H", k * s * 256, F32R)
            L = open_area(ph, "L", k * s * 256, F32R)
            if s == 1:
                return [x[:, :].rearrange("p (k t) -> p k t", k=k) for x in (H, L)]
            return [x[:, :].rearrange("p (k s t) -> p k s t", k=k, s=s) for x in (H, L)]

        def add_x(ps, j, n, pt):
            return Q.v(lambda e: e.tensor_tensor(x8[:, j:j + n, :], x8[:, j:j + n, :],
                                                 ps[:, 0:n * 256].rearrange("p (k t) -> p k t", k=n), ALU.add), pt)

        def even(ph, nH, nL):
            open_area(ph, "sc", 12300)
            mH, mL = hl(ph, 8)
            qk = [sc(0, 1024), sc(1024, 1024)]
            vv = sc(2048, 1024)
            qi = sc(3072, 1024)
            kid = sc(4096, 256)
            qTt = sc(4352, 1024).rearrange("p (k t) -> p k t", k=4)
            kTt = sc(5376, 1024).rearrange("p (k t) -> p k t", k=4)
            qiT = sc(6400, 1024).rearrange("p (k t) -> p k t", k=4)
            kiT = sc(7424, 256)
            score = sc(7680, 512)
            bias = sc(8192, 512)
            P = sc(8704, 512)
            PT = [sc(9216, 512), sc(9728, 512)]
            tmp = sc(10240, 1024)
            zc = cT[:, 0:1024]
            u = sc(11264, 1032).rearrange("p (k t) -> p k t", k=4)
            zz = cT[:, 1024:2048]
            cs = mi(192)
            cosA, sinA = cs[:, 0:64], cs[:, 64:128]
            cosI, sinI = cs[:, 128:160], cs[:, 160:192]
            wi = mi(16)
            posf = mi(2)
            mx = mi(16)
            sm8 = mi(8)

            Q.v(lambda e: e.tensor_copy(posf, posi[:, :]), t_in)
            ang = tmp[:, 0:96]
            r1 = tmp[:, 96:192]
            r2 = tmp[:, 192:288]
            for t in range(2):
                Q.v(lambda e, t=t: e.tensor_scalar(ang[:, 48 * t:48 * t + 48], sm("invf"), posf[:, t:t + 1], None, ALU.mult))
            for quarter in (0.25, 0.0):
                Q.v(lambda e: e.tensor_scalar(r1, ang, float(1 / (2 * np.pi)), quarter, ALU.mult, ALU.add))
                Q.v(lambda e: e.tensor_scalar(r1, r1, MAGIC, None, ALU.add))
                Q.v(lambda e: e.tensor_scalar(r1, r1, -MAGIC, None, ALU.add))
                Q.v(lambda e: e.scalar_tensor_tensor(r2, r1, -TWO_PI_A, ang, ALU.mult, ALU.add))
                Q.v(lambda e: e.scalar_tensor_tensor(r2, r1, -TWO_PI_B, r2, ALU.mult, ALU.add))
                Q.v(lambda e: e.scalar_tensor_tensor(r2, r1, -TWO_PI_C, r2, ALU.mult, ALU.add))
                if quarter:
                    Q.v(lambda e: e.tensor_scalar(r2, r2, float(np.pi / 2), None, ALU.add))
                Q.v(lambda e: e.tensor_scalar(r2, r2, 3.1415925, None, ALU.min))
                t_r = Q.v(lambda e: e.tensor_scalar(r2, r2, -3.1415925, None, ALU.max))
                v2 = r2.rearrange("p (t f) -> p t f", t=2)
                A_, I_ = (cosA, cosI) if quarter else (sinA, sinI)
                Q.a(lambda e, A_=A_, v2=v2: e.activation(A_.rearrange("p (t f) -> p t f", t=2), v2[:, :, 0:32], ACT.Sin), t_r)
                t_cs = Q.a(lambda e, I_=I_, v2=v2: e.activation(I_.rearrange("p (t f) -> p t f", t=2), v2[:, :, 32:48], ACT.Sin), t_r)
                Q.v(lambda e: e.memset(dummy, 0.0), t_cs)

            tn = norm(x8, sm("norm_mix", 0, 8), None, (t_in,), lambda k: nH[:, k, :], lambda k: nL[:, k, :])
            xH = lambda q: nH[:, q, :]
            xL = lambda q: nL[:, q, :]
            yH = lambda q, t: nH[:, q, t * 128:(t + 1) * 128]
            yL = lambda q, t: nL[:, q, t * 128:(t + 1) * 128]

            def copy_to(dst):
                return lambda ps, pt, t: Q.a(lambda e: e.activation(dst[:, t * 512:(t + 1) * 512], ps[:, :], ACT.Copy), pt)

            kw = tmp[:, 256:512]
            dense("ev_in", (), [28], 8, xH, xL, tn,
                  lambda ps, j, n, pt: Q.a(lambda e: e.activation(kw, ps[:, 0:256], ACT.Copy), pt))
            by_token("ev_in", (), 24, yH, yL, [(0,), (1,)], tn, copy_to(qi))
            t_qi0 = Q.last("act")
            for t in range(2):
                b, ps, bt = B.take()
                Q.tr(ps[:, 0:128], kw[:, t * 128:(t + 1) * 128], ident, (bt, t_qi0))
                pt = Q.pe_done()
                kd = kid[:, t * 128:t * 128 + 64]
                Q.v(lambda e: e.tensor_copy(kd, ps[:, 0:64]), pt)
                tw = Q.v(lambda e: e.tensor_scalar(wi[:, t * 8:t * 8 + 8], ps[:, 64:72], float(8 ** -0.5 * 64 ** -0.5), None, ALU.mult), pt)
                B.free(b, tw)
                Q.v(lambda e, kd=kd: e.tensor_reduce(mx[:, 0:1], kd, AX.X, ALU.add))
                Q.v(lambda e: e.tensor_scalar(mx[:, 0:1], mx[:, 0:1], -1.0 / 64, None, ALU.mult))
                Q.v(lambda e, kd=kd: e.tensor_scalar(kd, kd, mx[:, 0:1], None, ALU.add))
                Q.v(lambda e, kd=kd: e.tensor_tensor(tmp[:, 512:576], kd, kd, ALU.mult))
                Q.v(lambda e: e.tensor_reduce(rr[:, 0:1], tmp[:, 512:576], AX.X, ALU.add))
                Q.v(lambda e: e.tensor_scalar(rr[:, 0:1], rr[:, 0:1], 1.0 / 64, EPS, ALU.mult, ALU.add))
                tp = power(rr[:, 0:1])
                Q.v(lambda e, kd=kd: e.scalar_tensor_tensor(kd, kd, rr[:, 0:1], sm("ln_g"), ALU.mult, ALU.mult), tp)
                Q.v(lambda e, kd=kd: e.tensor_tensor(kd, kd, sm("ln_b"), ALU.add))
                rope(kd[:, 0:16], kd[:, 16:32], kd[:, 0:16], kd[:, 16:32], cosI[:, t * 16:t * 16 + 16],
                     sinI[:, t * 16:t * 16 + 16], tmp[:, 0:16], tmp[:, 16:32])
                tk = Q.v(lambda e, kd=kd, t=t: e.tensor_copy(kid[:, t * 128 + 64:t * 128 + 128], kd))
            transpose4([kid[:, 0:128], kid[:, 128:256]], kiT.rearrange("p (i t) -> p i t", i=2), (tk,))
            t_ki = Q.last("act")
            for t in range(2):
                z = qi[:, t * 512:(t + 1) * 512].rearrange("p (h d) -> p h d", h=8)
                cb = bc(cosI[:, t * 16:t * 16 + 16].unsqueeze(1), [128, 8, 16])
                sb_ = bc(sinI[:, t * 16:t * 16 + 16].unsqueeze(1), [128, 8, 16])
                t1 = tmp[:, 0:128].rearrange("p (h d) -> p h d", h=8)
                t2 = tmp[:, 128:256].rearrange("p (h d) -> p h d", h=8)
                Q.v(lambda e: e.memset(dummy, 0.0), Q.last("act"))
                tr_ = rope(z[:, :, 0:16], z[:, :, 16:32], z[:, :, 0:16], z[:, :, 16:32], cb, sb_, t1, t2)
                t_qi = transpose4([qi[:, t * 512 + i * 128:t * 512 + (i + 1) * 128] for i in range(4)],
                                  qiT[:, :, t * 128:(t + 1) * 128], (tr_,))

            if dump is not None:
                Q.v(lambda e: e.memset(sc(7680, 1024), 0.0))
            for t in range(2):
                nk = 128 * (t + 1)
                s = score[:, t * 256:t * 256 + nk]
                Q.v(lambda e, s=s: e.memset(s, 0.0))
                relt = [None, None]
                for h in range(8):
                    b, ps, bt = B.take()
                    o = (h % 2) * 64
                    Q.mm(ps[:, 0:nk], qiT[o:o + 64, h // 2, t * 128:(t + 1) * 128], kiT[o:o + 64, 0:nk], True, True,
                         (bt, t_qi, t_ki))
                    rel = tmp[:, 512 + (h % 2) * 256:512 + (h % 2) * 256 + nk]
                    ta = Q.a(lambda e, ps=ps, nk=nk, rel=rel: e.activation(rel, ps[:, 0:nk], ACT.Relu), Q.pe_done(), relt[h % 2],
                             Q.last("dve") if h == 0 else None)
                    B.free(b, ta)
                    relt[h % 2] = Q.v(lambda e, s=s, rel=rel, t=t, h=h: e.scalar_tensor_tensor(
                        s, rel, wi[:, t * 8 + h:t * 8 + h + 1], s, ALU.mult, ALU.add), ta)
                Q.v(lambda e, s=s, nk=nk: e.tensor_tensor(s[:, nk - 128:nk], s[:, nk - 128:nk], sm("tri"), ALU.add))
            if dump is not None:
                dbg("score", score, (Q.last("dve"),))

            fill(2)
            by_token("ev_in", (), 12, yH, yL, [(0,), (1,)], tn, copy_to(qk[0]))
            by_token("ev_in", (), 16, yH, yL, [(0,), (1,)], tn, copy_to(qk[1]))
            t_qk = Q.last("act")
            by_token("ev_in", (), 20, yH, yL, [(0,), (1,)], tn, copy_to(vv))
            t_v = Q.last("act")

            for which, dst, g in ((0, qTt, "ev_qg"), (1, kTt, "ev_kg")):
                for t in range(2):
                    z = qk[which][:, t * 512:(t + 1) * 512].rearrange("p (h d) -> p h d", h=8)
                    t3 = tmp[:, 0:512].rearrange("p (h d) -> p h d", h=8)
                    head_norm(z, t3, 8, 64, tok=(t_qk,))
                    Q.v(lambda e, z=z, g=g: e.tensor_tensor(z, z, bc(sm(g).unsqueeze(1), [128, 8, 64]), ALU.mult))
                    cb = bc(cosA[:, t * 32:t * 32 + 32].unsqueeze(1), [128, 8, 32])
                    sb_ = bc(sinA[:, t * 32:t * 32 + 32].unsqueeze(1), [128, 8, 32])
                    t1 = tmp[:, 0:256].rearrange("p (h d) -> p h d", h=8)
                    t2 = tmp[:, 256:512].rearrange("p (h d) -> p h d", h=8)
                    tr_ = rope(z[:, :, 0:32], z[:, :, 32:64], z[:, :, 0:32], z[:, :, 32:64], cb, sb_, t1, t2)
                    t_T = transpose4([qk[which][:, t * 512 + i * 128:t * 512 + (i + 1) * 128] for i in range(4)],
                                     dst[:, :, t * 128:(t + 1) * 128], (tr_,))

            for t in range(2):
                nk = 128 * (t + 1)
                s = score[:, t * 256:t * 256 + nk]
                for _ in range(8):
                    Q.v(lambda e, s=s: e.max(sm8, s))
                    Q.v(lambda e, s=s: e.match_replace(s, sm8, s, TAKEN))
                bb = bias[:, t * 256:t * 256 + nk]
                Q.v(lambda e, s=s, bb=bb: e.tensor_scalar(bb, s, TAKEN, 1.0, ALU.is_equal, ALU.subtract))
                Q.v(lambda e, bb=bb: e.tensor_scalar(bb, bb, BIG, None, ALU.mult))
                Q.v(lambda e, bb=bb, nk=nk: e.tensor_tensor(bb[:, nk - 128:nk], bb[:, nk - 128:nk], sm("tri"), ALU.add))
            if dump is not None:
                dbg("bias", bias, (Q.last("dve"),))

            Q.v(lambda e: e.memset(u[:, :, 0:2], 0.0))

            def take_zc(ps, j, n, pt):
                return Q.a(lambda e: e.activation(zc[:, j * 256:(j + n) * 256], ps[:, 0:n * 256], ACT.Copy), pt)
            dense("ev_in", (), [4, 5, 6, 7], 8, xH, xL, tn, take_zc)
            t_zc = Q.last("act")

            def take_zh(ps, j, n, pt):
                t = Q.v(lambda e: e.tensor_tensor(u[:, j:j + n, 2:258], ps[:, 0:n * 256].rearrange("p (k t) -> p k t", k=n),
                                                  zc[:, j * 256:(j + n) * 256].rearrange("p (k t) -> p k t", k=n), ALU.mult), pt, t_zc)
                for i in range(j, j + n):
                    y = zz[:, i * 256:(i + 1) * 256]
                    w = sm("ev_conv", 3 * i, 3 * i + 3)
                    Q.v(lambda e, i=i, y=y, w=w: e.tensor_scalar(y, u[:, i, 0:256], w[:, 0:1], None, ALU.mult))
                    Q.v(lambda e, i=i, y=y, w=w: e.scalar_tensor_tensor(y, u[:, i, 1:257], w[:, 1:2], y, ALU.mult, ALU.add))
                    Q.v(lambda e, i=i, y=y, w=w: e.scalar_tensor_tensor(y, u[:, i, 2:258], w[:, 2:3], y, ALU.mult, ALU.add))
                return t
            dense("ev_in", (), [8, 9, 10, 11], 8, xH, xL, tn, take_zh)

            def take_zb(ps, j, n, pt):
                z = zz[:, j * 256:(j + n) * 256].rearrange("p (k t) -> p k t", k=n)
                t = Q.v(lambda e: e.tensor_tensor(z, ps[:, 0:n * 256].rearrange("p (k t) -> p k t", k=n), z, ALU.mult), pt)
                parts(mH[:, j:j + n, :], mL[:, j:j + n, :], z, (t,))
                return t
            dense("ev_in", (), [0, 1, 2, 3], 8, xH, xL, tn, take_zb)

            for i in range(2):
                Q.v(lambda e, i=i: e.memset(PT[i][:, 256:384], 0.0))
            t_z = Q.last("dve")
            ptfree = [t_z, t_z]
            for h in range(8):
                o = (h % 2) * 64
                pt_ = PT[h % 2].rearrange("p (k t) -> p k t", k=2)
                if h % 2 == 0:
                    ob, ops, obt = B.take()
                for t in range(2):
                    nk = 128 * (t + 1)
                    b, ps, bt = B.take()
                    Q.mm(ps[:, 0:nk], qTt[o:o + 64, h // 2, t * 128:(t + 1) * 128], kTt[o:o + 64, h // 2, 0:nk], True, True,
                         (bt, t_T))
                    p = P[:, t * 256:t * 256 + nk]
                    bb = bias[:, t * 256:t * 256 + nk]
                    tv = Q.v(lambda e, ps=ps, p=p, bb=bb, nk=nk: e.scalar_tensor_tensor(p, ps[:, 0:nk], 0.125, bb, ALU.mult, ALU.add), Q.pe_done())
                    B.free(b, tv)
                    m_ = mx[:, 2 * t:2 * t + 1]
                    z_ = mx[:, 2 * t + 1:2 * t + 2]
                    Q.v(lambda e, p=p, m_=m_: e.tensor_reduce(m_, p, AX.X, ALU.max))
                    tv = Q.v(lambda e, m_=m_: e.tensor_scalar(m_, m_, -1.0, None, ALU.mult))
                    ta = Q.a(lambda e, p=p, m_=m_, z_=z_: e.activation(p, p, ACT.Exp, bias=m_, accum_out=z_), tv)
                    Q.v(lambda e, z_=z_: e.reciprocal(z_, z_), ta)
                    tv = Q.v(lambda e, p=p, z_=z_: e.tensor_scalar(p, p, z_, None, ALU.mult))
                    b, ps, bt = B.take()
                    for k in range(t + 1):
                        Q.tr(ps[:, k * 128:(k + 1) * 128], p[:, k * 128:(k + 1) * 128], ident, (bt, tv))
                    ta = Q.a(lambda e, ps=ps, nk=nk, t=t, pt_=pt_: e.activation(
                        pt_[:, 0:t + 1, t * 128:(t + 1) * 128], ps[:, 0:nk].rearrange("p (k t) -> p k t", k=t + 1), ACT.Copy),
                        Q.pe_done(), ptfree[h % 2])
                    B.free(b, ta)
                for k in range(2):
                    Q.mm(ops[o:o + 64, 0:256], vv[:, k * 512 + h * 64:k * 512 + (h + 1) * 64], pt_[:, k, :], k == 0, k == 1,
                         (obt, ta, t_v, t_z))
                ptfree[h % 2] = Q.pe_done()
                if h % 2 == 1:
                    k = 4 + h // 2
                    _, tv = parts(mH[:, k, :], mL[:, k, :], ops[:, 0:256], (Q.pe_done(),))
                    B.free(ob, tv)
                    fill(1)
            dense("ev_out", (), list(range(8)), 8, lambda q: mH[:, q, :], lambda q: mL[:, q, :],
                  (Q.last("act"), Q.last("dve")), add_x)

        def ffn(ph, nH, nL, l):
            aH, aL = hl(ph, 22)
            sg = [open_area(ph, "sg", 512)[:, :] for _ in range(2)]
            at = [open_area(ph, "at", 512)[:, :] for _ in range(2)]
            tn = norm(x8, sm("norm_ffn", 8 * l, 8 * l + 8), None, tuple(lasts()), lambda k: nH[:, k, :], lambda k: nL[:, k, :])
            xH = lambda q: nH[:, q, :]
            xL = lambda q: nL[:, q, :]
            n = [0, 0]
            gtok, utok = {}, {}

            def gate(ps, j, k, pt):
                s = sg[n[0] % 2]
                gtok[n[0]] = Q.a(lambda e: e.activation(s[:, 0:k * 256], ps[:, 0:k * 256], ACT.Silu), pt, utok.get(n[0] - 2))
                n[0] += 1
                return gtok[n[0] - 1]

            for j0 in range(0, 22, 4):
                js = list(range(j0, min(j0 + 4, 22)))
                dense("ffn_gate", (l,), js, 8, xH, xL, tn, gate)

                def up(ps, j, k, pt):
                    s = sg[n[1] % 2]
                    a = at[n[1] % 2][:, 0:k * 256]
                    t = Q.v(lambda e: e.tensor_tensor(a, ps[:, 0:k * 256], s[:, 0:k * 256], ALU.mult), pt, gtok[n[1]], utok.get(n[1] - 2))
                    a3 = a.rearrange("p (k t) -> p k t", k=k)
                    utok[n[1]] = parts(aH[:, j0 + j:j0 + j + k, :], aL[:, j0 + j:j0 + j + k, :], a3, (t,))[1]
                    n[1] += 1
                    return t
                dense("ffn_up", (l,), js, 8, xH, xL, tn, up)
            dense("ffn_down", (l,), list(range(8)), 22, lambda q: aH[:, q, :], lambda q: aL[:, q, :], tuple(lasts()), add_x)

        s_p = Q.new_sem("s_p")

        def ple(ph, nH, nL, l):
            er = open_area(ph, "er", 2048)[:, :].rearrange("p (k t) -> p k t", k=8)
            praw = open_area(ph, "praw", 512)
            pH, pL = hl(ph, 2)
            sg = [open_area(ph, "sg", 512)[:, :] for _ in range(2)]
            tp = Q.dma("pool", praw[:, :], dr["pT"][l], s_p, lasts())
            tp = parts(pH, pL, praw[:, :].rearrange("p (k t) -> p k t", k=2), (tp,) + tuple(lasts()))

            def take(ps, j, n, pt):
                return Q.a(lambda e: e.activation(er[:, j:j + n, :], ps[:, 0:n * 256].rearrange("p (k t) -> p k t", k=n), ACT.Copy), pt)
            dense("ple_proj", (l,), list(range(8)), 2, lambda q: pH[:, q, :], lambda q: pL[:, q, :], tp, take)
            norm(er, sm("ple_post", 8 * l, 8 * l + 8), None, tuple(lasts()), out=lambda k: er[:, k, :])
            tn = norm(x8, sm("ple_norm", 8 * l, 8 * l + 8), None, tuple(lasts()), lambda k: nH[:, k, :], lambda k: nL[:, k, :])
            i = [0]
            free = [None, None]

            def take2(ps, j, n, pt):
                k = i[0] % 2
                s = sg[k]
                i[0] += 1
                ta = Q.a(lambda e: e.activation(s, ps[:, 0:n * 256], ACT.Sigmoid), pt, free[k])
                sv = s.rearrange("p (k t) -> p k t", k=n)
                Q.v(lambda e: e.tensor_tensor(sv, sv, er[:, j:j + n, :], ALU.mult), ta)
                free[k] = Q.v(lambda e: e.tensor_tensor(x8[:, j:j + n, :], x8[:, j:j + n, :], sv, ALU.add))
                return ta
            dense("ple_gate", (l,), list(range(8)), 8, lambda q: nH[:, q, :], lambda q: nL[:, q, :], tn, take2)

        def odd(ph, nH, nL):
            open_area(ph, "sc", 13 * 1024)
            oH, oL = hl(ph, 8)
            S = lambda i: sc(i * 1024, 1024) if i < 13 else cT[:, (i - 13) * 1024:(i - 12) * 1024]
            gb = mi(16 * 3)
            gcu, beta, eg = gb[:, 0:16], gb[:, 16:32], gb[:, 32:48]
            gk = mi(32)
            glast, kd = gk[:, 0:16], gk[:, 16:32]
            EL = mi(32)
            ea = mi(8)
            gt = mi(32)
            rq = mi(8)
            rq2 = mi(8)
            tn = norm(x8, sm("norm_mix", 8, 16), None, tuple(lasts()), lambda k: nH[:, k, :], lambda k: nL[:, k, :])
            xH = lambda q: nH[:, q, :]
            xL = lambda q: nL[:, q, :]
            yH = lambda q, t: nH[:, q, t * 128:(t + 1) * 128]
            yL = lambda q, t: nL[:, q, t * 128:(t + 1) * 128]

            ab = S(0)[:, 0:256]
            dense("od_in", (), [32], 8, xH, xL, tn,
                  lambda ps, j, n, pt: Q.a(lambda e: e.activation(ab, ps[:, 0:256], ACT.Copy), pt))
            t_ab = Q.last("act")
            t_ea = Q.a(lambda e: e.activation(ea, sm("a_log"), ACT.Exp))
            for t in range(2):
                b, ps, bt = B.take()
                Q.tr(ps[:, 0:128], ab[:, t * 128:(t + 1) * 128], ident, (bt, t_ab))
                g = gt[:, 0:8]
                a1 = gt[:, 8:16]
                a2 = gt[:, 16:24]
                Q.v(lambda e, ps=ps: e.tensor_tensor(g, ps[:, 0:8], sm("dt_bias"), ALU.add), Q.pe_done())
                tb = Q.v(lambda e, ps=ps: e.tensor_copy(a2, ps[:, 8:16]))
                B.free(b, tb)
                Q.v(lambda e: e.tensor_scalar(a1, g, -1.0, None, ALU.mult))
                tv = Q.v(lambda e: e.tensor_tensor(a1, a1, g, ALU.min))
                Q.a(lambda e, t=t: e.activation(beta[:, 8 * t:8 * t + 8], a2, ACT.Sigmoid), tv)
                Q.a(lambda e: e.activation(a1, a1, ACT.Exp), tv)
                ta = Q.a(lambda e: e.activation(a1, a1, ACT.Ln, bias=1.0))
                Q.v(lambda e: e.tensor_scalar(g, g, 0.0, None, ALU.max))
                Q.v(lambda e: e.tensor_tensor(g, g, a1, ALU.add), ta)
                Q.v(lambda e: e.tensor_scalar(g, g, -1.0, None, ALU.mult))
                t_g = Q.v(lambda e, t=t: e.tensor_tensor(gcu[:, 8 * t:8 * t + 8], g, ea, ALU.mult), t_ea)
            b, ps, bt = B.take()
            Q.mm(ps[:, 0:16], sm("cumT"), gcu, True, True, (bt, t_g))
            t_g = Q.v(lambda e, ps=ps: e.tensor_copy(gcu, ps[:, 0:16]), Q.pe_done())
            B.free(b, t_g)
            b, ps, bt = B.take()
            Q.mm(ps[:, 0:16], sm("lastT"), gcu, True, True, (bt, t_g))
            Q.mm(ps[:, 16:32], sm("sel", 0, 128), gcu, True, True)
            Q.mm(ps[:, 32:48], sm("sel", 128, 256), gcu, True, True)
            pt = Q.pe_done()
            t1 = Q.v(lambda e, ps=ps: e.tensor_tensor(kd, ps[:, 0:16], gcu, ALU.subtract), pt)
            Q.a(lambda e: e.activation(kd, kd, ACT.Exp), t1)
            ta = Q.a(lambda e, ps=ps: e.activation(EL, ps[:, 16:48], ACT.Exp), pt)
            B.free(b, ta)
            t_gates = Q.a(lambda e: e.activation(eg, gcu, ACT.Exp), t_g)

            if dump is not None:
                dbg("gcu", gcu, (Q.last("dve"),))
            u = wk[:, 0:1036].rearrange("p (k t) -> p k t", k=4)
            Q.v(lambda e: e.memset(u[:, :, 0:3], 0.0), Q.pe_done())
            for H in range(2):
                qT, z, kT, vT, K, kbg, V, knT, MT, qkT, T, TT, Y, BT, wT = (S(i) for i in range(15))
                St = wk[:, 1536:2048]
                d4 = lambda a: a.rearrange("p (k t) -> p k t", k=4)
                t4 = lambda a: a.rearrange("p (t f) -> p t f", t=2)
                for base, dst in ((0, qT), (8, kT), (16, vT)):
                    ufree = [Q.last("dve")]

                    def take(ps, j, n, pt, dst=dst, base=base):
                        ta = Q.a(lambda e: e.activation(u[:, j:j + n, 3:259], ps[:, 0:n * 256].rearrange("p (k t) -> p k t", k=n),
                                                        ACT.Copy), pt, ufree[0])
                        for i in range(j, j + n):
                            w = sm("od_conv", 4 * (base + 4 * H + i), 4 * (base + 4 * H + i) + 4)
                            y = d4(dst)[:, i, :]
                            Q.v(lambda e, i=i, y=y, w=w: e.tensor_scalar(y, u[:, i, 0:256], w[:, 0:1], None, ALU.mult), ta, Q.last("pe"))
                            for s in range(1, 4):
                                tv = Q.v(lambda e, i=i, y=y, w=w, s=s: e.scalar_tensor_tensor(
                                    y, u[:, i, s:s + 256], w[:, s:s + 1], y, ALU.mult, ALU.add))
                        Q.a(lambda e, dst=dst, j=j, n=n: e.activation(d4(dst)[:, j:j + n, :], d4(dst)[:, j:j + n, :], ACT.Silu), tv)
                        return ta
                    dense("od_in", (), [base + 4 * H + i for i in range(4)], 8, xH, xL, tn, take)
                by_token("od_in", (), 24 + 4 * H, yH, yL, [(0,), (1,)], tn,
                         lambda ps, pt, t: Q.a(lambda e: e.activation(z[:, t * 512:(t + 1) * 512], ps[:, :], ACT.Silu), pt))
                t_c = Q.last("act")
                if dump is not None and H == 0:
                    dbg("oqT", qT, (Q.last("act"),)); dbg("ovT", vT, (Q.last("act"),))
                for t in range(2):
                    transpose4([d4(kT)[:, h, t * 128:(t + 1) * 128] for h in range(4)],
                               K[:, t * 512:(t + 1) * 512].rearrange("p (k t) -> p k t", k=4), (t_c,))
                    transpose4([d4(vT)[:, h, t * 128:(t + 1) * 128] for h in range(4)],
                               V[:, t * 512:(t + 1) * 512].rearrange("p (k t) -> p k t", k=4), (t_c,))
                t_kv = Q.last("act")
                sq = Y
                tv = Q.v(lambda e: e.tensor_tensor(sq, qT, qT, ALU.mult), t_kv)
                b, ps, bt = B.take()
                for t in range(2):
                    for h in range(4):
                        Q.mm(ps[:, t * 4 + h:t * 4 + h + 1], d4(sq)[:, h, t * 128:(t + 1) * 128], ones[:, 0:1], True, True, (bt, tv))
                Q.v(lambda e, ps=ps: e.tensor_scalar(rq, ps[:, 0:8], EPS, None, ALU.add), Q.pe_done())
                B.free(b, Q.last("dve"))
                tp = power(rq)
                Q.v(lambda e: e.tensor_scalar(rq, rq, float(128 ** -0.5), None, ALU.mult), tp)
                gs = lambda a: a.rearrange("p (t h) -> p t h", t=2)[:, :, 4 * H:4 * H + 4]
                Q.v(lambda e: e.tensor_tensor(rq2.rearrange("p (t h) -> p t h", t=2), rq.rearrange("p (t h) -> p t h", t=2),
                                              gs(eg), ALU.mult), t_gates)
                k3 = K.rearrange("p (h d) -> p h d", h=8)
                head_norm(k3, BT.rearrange("p (h d) -> p h d", h=8), 8, 128, 1.0)
                t_kn = Q.last("dve")
                for t in range(2):
                    transpose4([K[:, t * 512 + h * 128:t * 512 + (h + 1) * 128] for h in range(4)],
                               d4(knT)[:, :, t * 128:(t + 1) * 128], (t_kn,))
                t_knT = Q.last("act")
                for t in range(2):
                    col = lambda a, t=t: bc(a[:, 8 * t + 4 * H:8 * t + 4 * H + 4].unsqueeze(2), [128, 4, 128])
                    hv = lambda a, t=t: a[:, t * 512:(t + 1) * 512].rearrange("p (h d) -> p h d", h=4)
                    Q.v(lambda e, col=col, hv=hv: e.tensor_tensor(hv(V), hv(V), col(beta), ALU.mult))
                    Q.v(lambda e, col=col, hv=hv: e.tensor_tensor(hv(kbg), hv(K), col(beta), ALU.mult))
                    Q.v(lambda e, col=col, hv=hv: e.tensor_tensor(hv(kbg), hv(kbg), col(eg), ALU.mult))
                    for h in range(4):
                        tv = Q.v(lambda e, t=t, h=h: e.tensor_scalar(Y[:, h * 128:(h + 1) * 128], ident,
                                                                     gcu[:, 8 * t + 4 * H + h:8 * t + 4 * H + h + 1], None, ALU.mult),
                                 Q.last("pe"))
                    b, ps, bt = B.take()
                    Q.mm(ps[:, :], ones, Y[:, 0:512], True, False, (bt, tv))
                    Q.mm(ps[:, :].rearrange("p (h t) -> p h t", h=4), ident, bc(sm("dmask").unsqueeze(1), [128, 4, 128]), False, True)
                    pt = Q.pe_done()
                    for h in range(4):
                        ta = Q.a(lambda e, ps=ps, h=h, t=t: e.activation(
                            kT[:, t * 512 + h * 128:t * 512 + (h + 1) * 128], ps[:, h * 128:(h + 1) * 128], ACT.Exp,
                            bias=gcu[:, 8 * t + 4 * H + h:8 * t + 4 * H + h + 1], scale=-1.0), pt)
                    B.free(b, ta)
                    for kind in range(2):
                        b, ps, bt = B.take()
                        L = knT if kind == 0 else qT
                        for h in range(4):
                            Q.mm(ps[:, h * 128:(h + 1) * 128], d4(L)[:, h, t * 128:(t + 1) * 128],
                                 d4(knT)[:, h, t * 128:(t + 1) * 128], True, True, (bt, t_knT))
                        pt = Q.pe_done()
                        for h in range(4):
                            s_ = (beta[:, 8 * t + 4 * H + h:8 * t + 4 * H + h + 1] if kind == 0 else rq[:, 4 * t + h:4 * t + h + 1])
                            tv = Q.v(lambda e, ps=ps, h=h, t=t, s_=s_: e.scalar_tensor_tensor(
                                vT[:, h * 128:(h + 1) * 128], ps[:, h * 128:(h + 1) * 128], s_,
                                kT[:, t * 512 + h * 128:t * 512 + (h + 1) * 128], ALU.mult, ALU.mult), pt, ta, Q.last("pe"))
                        B.free(b, tv)
                        dst = MT if kind == 0 else qkT
                        transpose4([vT[:, h * 128:(h + 1) * 128] for h in range(4)],
                                   dst[:, t * 512:(t + 1) * 512].rearrange("p (k t) -> p k t", k=4), (tv,))
                    Q.v(lambda e, col=col, hv=hv: e.tensor_tensor(hv(K), hv(K), col(kd), ALU.mult), t_knT)
                t_MT = Q.last("act")
                if dump is not None and H == 0:
                    dbg("MT", MT, (Q.last("act"), Q.last("dve"))); dbg("knT", knT, (Q.last("act"), Q.last("dve")))
                    dbg("qkT", qkT, (Q.last("act"), Q.last("dve")))
                p8 = lambda a: a.rearrange("p (i t) -> p i t", i=8)
                lv = lambda l: bc(sm("levels", 128 * l, 128 * l + 128).unsqueeze(1), [128, 8, 128])
                Q.v(lambda e: e.tensor_tensor(p8(BT), p8(MT), lv(0), ALU.mult), t_MT)
                tv = Q.v(lambda e: e.tensor_tensor(p8(TT), bc(ident.unsqueeze(1), [128, 8, 128]), p8(BT), ALU.subtract))
                for t in range(2):
                    transpose4([TT[:, t * 512 + h * 128:t * 512 + (h + 1) * 128] for h in range(4)],
                               T[:, t * 512:(t + 1) * 512].rearrange("p (k t) -> p k t", k=4), (tv,))
                t_T = Q.last("act")
                for l in range(1, 6):
                    fill(1)
                    tb = Q.v(lambda e, l=l: e.tensor_tensor(p8(BT), p8(MT), lv(l), ALU.mult), Q.last("pe"))
                    for t in range(2):
                        b, ps, bt = B.take()
                        for h in range(4):
                            i = t * 4 + h
                            Q.mm(ps[:, h * 128:(h + 1) * 128], p8(BT)[:, i, :], p8(T)[:, i, :], True, True, (bt, tb, t_T))
                        ta = Q.a(lambda e, ps=ps, t=t: e.activation(Y[:, t * 512:(t + 1) * 512], ps[:, :], ACT.Copy), Q.pe_done())
                        B.free(b, ta)
                    for t in range(2):
                        for kind in range(2):
                            if kind == 0 and l == 5:
                                continue
                            b, ps, bt = B.take()
                            for h in range(4):
                                i = t * 4 + h
                                if kind == 0:
                                    Q.mm(ps[:, h * 128:(h + 1) * 128], p8(TT)[:, i, :], p8(Y)[:, i, :], True, True, (bt, ta))
                                else:
                                    Q.mm(ps[:, h * 128:(h + 1) * 128], p8(Y)[:, i, :], p8(TT)[:, i, :], True, True, (bt, ta))
                            dst = (T if kind == 0 else TT)[:, t * 512:(t + 1) * 512]
                            tv = Q.v(lambda e, ps=ps, dst=dst: e.tensor_tensor(dst, dst, ps[:, :], ALU.subtract), Q.pe_done())
                            B.free(b, tv)
                    t_T = tv
                if dump is not None and H == 0:
                    dbg("TT", TT, (Q.last("act"), Q.last("dve")))
                U = vT
                for t in range(2):
                    b, ps, bt = B.take()
                    for h in range(4):
                        i = t * 4 + h
                        Q.mm(ps[:, h * 128:(h + 1) * 128], p8(TT)[:, i, :], p8(V)[:, i, :], True, True, (bt, t_T))
                    ta = Q.a(lambda e, ps=ps, t=t: e.activation(U[:, t * 512:(t + 1) * 512], ps[:, :], ACT.Copy), Q.pe_done())
                    B.free(b, ta)
                    b, ps, bt = B.take()
                    for h in range(4):
                        i = t * 4 + h
                        Q.mm(ps[:, h * 128:(h + 1) * 128], p8(kbg)[:, i, :], p8(TT)[:, i, :], True, True, (bt, t_T))
                    ta = Q.a(lambda e, ps=ps, t=t: e.activation(wT[:, t * 512:(t + 1) * 512], ps[:, :], ACT.Copy), Q.pe_done())
                    B.free(b, ta)
                t_uw = ta
                O = T
                vn = Y
                t_s = None
                for n in range(4):
                    if n < 3:
                        fill(1)
                    t, o = n // 2, 64 * (n % 2)
                    r = slice(o, o + 64)
                    vs = vn[r, t * 512:(t + 1) * 512]
                    us = U[r, t * 512:(t + 1) * 512]
                    if n == 0:
                        tvn = Q.v(lambda e, vs=vs, us=us: e.tensor_copy(vs, us), t_uw, Q.last("pe"))
                    else:
                        b, ps, bt = B.take()
                        for h in range(4):
                            i = t * 4 + h
                            Q.mm(ps[r, h * 128:(h + 1) * 128], p8(wT)[:, i, o:o + 64], St[:, h * 128:(h + 1) * 128], True, True,
                                 (bt, t_s, t_uw))
                        tvn = Q.v(lambda e, vs=vs, us=us, ps=ps, r=r: e.tensor_tensor(vs, us, ps[r, :], ALU.subtract), Q.pe_done())
                        B.free(b, tvn)
                    b, ps, bt = B.take()
                    for h in range(4):
                        i = t * 4 + h
                        Q.mm(ps[r, h * 128:(h + 1) * 128], p8(qkT)[r, i, o:o + 64], vn[r, t * 512 + h * 128:t * 512 + (h + 1) * 128],
                             True, True, (bt, tvn))
                    Os = O[r, t * 512:(t + 1) * 512]
                    ta = Q.a(lambda e, ps=ps, r=r, Os=Os: e.activation(Os, ps[r, :], ACT.Copy), Q.pe_done())
                    B.free(b, ta)
                    if n:
                        b, ps, bt = B.take()
                        for h in range(4):
                            Q.mm(ps[r, h * 128:(h + 1) * 128], d4(qT)[:, h, t * 128 + o:t * 128 + o + 64],
                                 St[:, h * 128:(h + 1) * 128], True, True, (bt, t_s))
                        pt = Q.pe_done()
                        for h in range(4):
                            tv = Q.v(lambda e, ps=ps, r=r, h=h, t=t: e.scalar_tensor_tensor(
                                O[r, t * 512 + h * 128:t * 512 + (h + 1) * 128], ps[r, h * 128:(h + 1) * 128],
                                rq2[r, 4 * t + h:4 * t + h + 1], O[r, t * 512 + h * 128:t * 512 + (h + 1) * 128],
                                ALU.mult, ALU.add), pt, ta)
                        B.free(b, tv)
                    if n < 3:
                        b, ps, bt = B.take()
                        for h in range(4):
                            i = t * 4 + h
                            Q.mm(ps[:, h * 128:(h + 1) * 128], p8(K)[r, i, :], vn[r, t * 512 + h * 128:t * 512 + (h + 1) * 128],
                                 True, True, (bt, tvn))
                        pt = Q.pe_done()
                        if n == 0:
                            t_s = Q.v(lambda e, ps=ps: e.tensor_copy(St, ps[:, :]), pt)
                        else:
                            for h in range(4):
                                el = EL[:, 16 * (n % 2) + 8 * t + 4 * H + h:16 * (n % 2) + 8 * t + 4 * H + h + 1]
                                t_s = Q.v(lambda e, ps=ps, h=h, el=el: e.scalar_tensor_tensor(
                                    St[:, h * 128:(h + 1) * 128], St[:, h * 128:(h + 1) * 128], el,
                                    ps[:, h * 128:(h + 1) * 128], ALU.mult, ALU.add), pt)
                        B.free(b, t_s)
                if dump is not None and H == 0:
                    dbg("O", O, (Q.last("act"), Q.last("dve")))
                o3 = O.rearrange("p (h d) -> p h d", h=8)
                head_norm(o3, BT.rearrange("p (h d) -> p h d", h=8), 8, 128, tok=(Q.last("act"),))
                Q.v(lambda e: e.tensor_tensor(o3, o3, bc(sm("o_g").unsqueeze(1), [128, 8, 128]), ALU.mult))
                tv = Q.v(lambda e: e.tensor_tensor(O, O, z, ALU.mult))
                for t in range(2):
                    b, ps, bt = B.take()
                    for h in range(4):
                        Q.tr(ps[:, h * 128:(h + 1) * 128], O[:, t * 512 + h * 128:t * 512 + (h + 1) * 128], ident, (bt, tv))
                    t_o = parts(oH[:, 4 * H:4 * H + 4, t * 128:(t + 1) * 128], oL[:, 4 * H:4 * H + 4, t * 128:(t + 1) * 128],
                                ps[:, :].rearrange("p (k t) -> p k t", k=4), (Q.pe_done(),))
                    B.free(b, t_o[1])
            dense("od_out", (), list(range(8)), 8, lambda q: oH[:, q, :], lambda q: oL[:, q, :], t_o, add_x)

        mods = [mi(96), mi(96)]
        s1 = mi(32)

        c2 = mi(256).rearrange("p (k n) -> p k n", k=8)
        ada_n = [0]
        ada_late = []

        def ada_step():
            i = ada_n[0]
            if i >= 24:
                if ada_late:
                    ada_late.pop()()
                return
            ada_n[0] += 1
            if i == 0:
                Q.v(lambda e: e.memset(c2, 0.0))
                ada_t.append(Q.a(lambda e: e.activation(c2[:, :, 0:2], sm("c2").rearrange("p (k s) -> p k s", k=8), ACT.Silu),
                                 Q.last("dve"), t_in))
            l, c4 = i // 12, i % 12
            c = W.ask("ada", (l,), 4 * c4, 4, 8, "raw")
            ap, tok = c.raw()
            w = ap.rearrange("p (j k n) -> p j k n", j=4, k=8)
            b, ps, bt = B.take()
            for k in range(2):
                for g in range(4):
                    Q.mm(ps[32 * g:32 * g + 32, :].rearrange("p (j n) -> p j n", j=4), c2[:, 2 * g + k, :], w[:, :, 2 * g + k, :],
                         k == 0, k == 1, (tok, bt, ada_t[0]))
            pt = Q.pe_done()
            c.done(pt)
            if ada_late:
                ada_late.pop()()
            ta = Q.a(lambda e: e.activation(adaT[:, :], ps[:, :], ACT.Copy), pt, Q.last("pe"))
            B.free(b, ta)

            def late():
                b, ps, bt = B.take()
                for j in range(4):
                    Q.tr(ps[:, j * 128:(j + 1) * 128], adaT[:, j * 128:(j + 1) * 128], ident, (bt, ta))
                m = mods[l].rearrange("p (j s) -> p j s", j=48)[:, 4 * c4:4 * c4 + 4, :]
                for s in range(2):
                    v = ps[:, :].rearrange("p (j g n) -> p j g n", j=4, g=4)[:, :, :, s]
                    Q.v(lambda e: e.tensor_reduce(m[:, :, s], v, AX.X, ALU.add), Q.pe_done())
                B.free(b, Q.last("dve"))
                Q.v(lambda e: e.tensor_tensor(m, m, bc(sm("ada_b", 48 * l + 4 * c4, 48 * l + 4 * c4 + 4).unsqueeze(2), [128, 4, 2]), ALU.add))
            ada_late.append(late)
        ada_t = []

        def fill(n):
            for _ in range(n):
                ada_step()

        def mod(l, which, side):
            return mods[l].rearrange("p (w k s) -> p w s k", w=6, k=8)[:, which, side, :]

        s_c = Q.new_sem("s_c")
        s_k = Q.new_sem("s_k")

        def load_consts():
            after = (Q.last("dve"), Q.last("act"), Q.pe_done())
            return Q.dma("pool", cT[:, :], dr["ctxT"], s_c, after)

        def scales(l, which_g, which_m, side):
            g = sm(which_g, 8 * l, 8 * l + 8)
            dst = s1[:, 8 * side:8 * side + 8]
            Q.v(lambda e: e.tensor_scalar(dst, mod(l, which_m, side), 1.0, None, ALU.add))
            Q.v(lambda e: e.tensor_tensor(dst, dst, g, ALU.mult))
            return dst

        def mixer2(ph, l):
            open_area(ph, "sc", 13568)
            nH, nL = hl(ph, 8, 2)
            CS = sc(0, 1024).rearrange("p (k t) -> p k t", k=2)
            BD = sc(1024, 256)
            fp = sc(1280, 2048).rearrange("p (s t f) -> p s t f", s=2, t=2)
            kv = sc(3328, 2048).rearrange("p (s t f) -> p s t f", s=2, t=2)
            qq = sc(5376, 2048).rearrange("p (s f) -> p s f", s=2)
            qTt = sc(7424, 1024).rearrange("p (h t) -> p h t", h=4)
            kTt = sc(8448, 1024).rearrange("p (h t) -> p h t", h=2)
            PT = [sc(9472, 1024), sc(10496, 1024)]
            P = [sc(11520, 512), sc(12032, 512)]
            tmp = sc(12544, 1024)
            tmp2 = tmp[:, 0:512]
            fH = open_area(ph, "fH", 512, F32R)
            fL = open_area(ph, "fL", 512, F32R)
            src = [x8, c8]
            nside = 2 if l == 0 else 1
            t_const = Q.dma("pool", sc(0, 1280), dr["dft"], s_c, lasts() + [t_ctx])
            for side in range(2):
                dst = scales(l, "n1", 1, side)
                tn = norm(src[side], dst, mod(l, 0, side), (t_ctx,) + tuple(lasts()),
                          lambda k: nH[:, k, side, :], lambda k: nL[:, k, side, :])
            t_pool = Q.dma("pool", wk[:, :], dr["poolA"], s_k, lasts())
            PA = wk[:, :].rearrange("p (g k t) -> p g k t", g=4, k=2)
            yH = lambda q, s, t: nH[:, q, s, t * 128:(t + 1) * 128]
            yL = lambda q, s, t: nL[:, q, s, t * 128:(t + 1) * 128]
            some = [(s, t) for s in range(nside) for t in range(2)]
            both = [(s, t) for s in range(2) for t in range(2)]
            by_token("w_in", (l,), 8, yH, yL, both, tn,
                     lambda ps, pt, s, t: Q.a(lambda e: e.activation(kv[:, s, t, :], ps[:, :], ACT.Copy), pt))
            t_kv = Q.last("act")
            by_token("w_in", (l,), 4, yH, yL, some, tn,
                     lambda ps, pt, s, t: Q.a(lambda e: e.activation(qq[:, s, t * 512:(t + 1) * 512], ps[:, :], ACT.Copy), pt))
            t_qq = Q.last("act")
            by_token("w_in", (l,), 0, yH, yL, some, tn,
                     lambda ps, pt, s, t: Q.a(lambda e: e.activation(fp[:, s, t, :], ps[:, :], ACT.Copy), pt))
            t_fp = Q.last("act")
            mH, mL = nH, nL
            t_n = Q.pe_done()

            def rope2(z, t, heads):
                zz = z.rearrange("p (h a x f) -> p h a x f", h=heads, a=2, x=2)
                n = heads * 64
                t1 = tmp[:, 0:n].rearrange("p (h a f) -> p h a f", h=heads, a=2)
                t2 = tmp[:, n:2 * n].rearrange("p (h a f) -> p h a f", h=heads, a=2)
                cb = bc(sm("rcos", 64 * t, 64 * t + 64).rearrange("p (a f) -> p a f", a=2).unsqueeze(1), [128, heads, 2, 32])
                sb_ = bc(sm("rsin", 64 * t, 64 * t + 64).rearrange("p (a f) -> p a f", a=2).unsqueeze(1), [128, heads, 2, 32])
                return rope(zz[:, :, :, 0, :], zz[:, :, :, 1, :], zz[:, :, :, 0, :], zz[:, :, :, 1, :], cb, sb_, t1, t2)

            for s in range(2):
                for t in range(2):
                    z = kv[:, s, t, 0:256]
                    z3 = z.rearrange("p (h d) -> p h d", h=2)
                    head_norm(z3, tmp[:, 0:256].rearrange("p (h d) -> p h d", h=2), 2, 128, tok=(t_kv,))
                    tv = Q.v(lambda e, z3=z3: e.tensor_tensor(z3, z3, bc(sm("kg", 128 * l, 128 * l + 128).unsqueeze(1), [128, 2, 128]), ALU.mult))
                    if s == 0:
                        tv = rope2(z, t, 2)
                    t_kT = transpose4([z[:, h * 128:(h + 1) * 128] for h in range(2)],
                                      kTt[:, :, s * 256 + t * 128:s * 256 + (t + 1) * 128], (tv,))
            for s in range(nside):
                for f in range(2):
                    b, ps, bt = B.take()
                    for t in range(2):
                        Q.mm(ps[:, :], fp[:, s, t, f * 128:(f + 1) * 128], CS[:, t, :], t == 0, t == 1, (bt, t_fp, t_const))
                    pq = P[f]
                    ta = Q.a(lambda e, ps=ps, pq=pq: e.activation(pq, ps[:, :], ACT.Copy), Q.pe_done())
                    B.free(b, ta)
                fr = [x[:, :].rearrange("p (k t) -> p k t", k=2) for x in (fH, fL)]
                b, ps, bt = B.take()
                for f in range(2):
                    for k in range(2):
                        Q.mm(ps[:, f * 256:(f + 1) * 256], BD[:, k * 128:(k + 1) * 128], P[f][:, k * 256:(k + 1) * 256], k == 0, k == 1,
                             (bt, ta))
                t_fr = parts(fH[:, :], fL[:, :], ps[:, :], (Q.pe_done(),))
                B.free(b, t_fr[1])
                b, ps, bt = B.take()
                for g in range(4):
                    o = 64 * (g % 2)
                    for t in range(2):
                        Q.mm(ps[o:o + 64, (g // 2) * 256:(g // 2 + 1) * 256], fp[:, s, t, 256 + g * 64:256 + (g + 1) * 64],
                             PA[:, g, t, :], t == 0, t == 1, (bt, t_pool, t_fp))
                dp = tmp[:, 512:1024]
                tv = Q.v(lambda e: e.tensor_copy(dp, ps[:, :]), Q.pe_done())
                B.free(b, tv)
                b, ps, bt = B.take()
                for g in range(4):
                    o = 64 * (g % 2)
                    wp = sm("w_pool", 128 * l + 64 * (g // 2), 128 * l + 64 * (g // 2) + 64)
                    Q.mm(ps[o:o + 64, (g // 2) * 256:(g // 2 + 1) * 256], wp[o:o + 64, :], dp[o:o + 64, (g // 2) * 256:(g // 2 + 1) * 256],
                         True, True, (bt, tv))
                pt = Q.pe_done()
                for k in range(2):
                    tv = Q.v(lambda e: e.tensor_scalar(tmp2[:, k * 256:(k + 1) * 256], ps[:, k * 256:(k + 1) * 256],
                                                       sm("pool_scale", 2 * l + k, 2 * l + k + 1), None, ALU.mult), pt)
                B.free(b, tv)
                parts(mH[:, 2:4, s, :], mL[:, 2:4, s, :], tmp2.rearrange("p (k t) -> p k t", k=2), (tv, t_n))

                def take_f(ps, j, n, pt):
                    return parts(mH[:, 0:2, s, :], mL[:, 0:2, s, :], ps[:, :].rearrange("p (k t) -> p k t", k=2), (pt,))[1]
                dense("w_four", (l,), [0, 1], 2, lambda q: fr[0][:, q, :], lambda q: fr[1][:, q, :], t_fr, take_f)
                for t in range(2):
                    z = qq[:, s, t * 512:(t + 1) * 512]
                    z3 = z.rearrange("p (h d) -> p h d", h=4)
                    head_norm(z3, tmp[:, 0:512].rearrange("p (h d) -> p h d", h=4), 4, 128, tok=(t_qq,))
                    tv = Q.v(lambda e: e.tensor_tensor(z3, z3, bc(sm("qg", 128 * l, 128 * l + 128).unsqueeze(1), [128, 4, 128]), ALU.mult))
                    if s == 0:
                        tv = rope2(z, t, 4)
                    t_qT = transpose4([z[:, h * 128:(h + 1) * 128] for h in range(4)],
                                      qTt[:, :, t * 128:(t + 1) * 128], (tv,))
                k0, nk = (0, 512) if s == 0 else (256, 256)
                kn = nk // 128
                free = [None, None]
                for h in range(4):
                    pt_ = PT[h % 2].rearrange("p (k t) -> p k t", k=4)
                    for t in range(2):
                        b, ps, bt = B.take()
                        Q.mm(ps[:, 0:nk], qTt[:, h, t * 128:(t + 1) * 128], kTt[:, h // 2, k0:k0 + nk], True, True, (bt, t_qT, t_kT))
                        pt = Q.pe_done()
                        m_ = rr[:, 8 + t:9 + t]
                        z_ = rr[:, 10 + t:11 + t]
                        Q.v(lambda e, ps=ps, m_=m_, nk=nk: e.tensor_reduce(m_, ps[:, 0:nk], AX.X, ALU.max), pt)
                        tv = Q.v(lambda e, m_=m_: e.tensor_scalar(m_, m_, -float(128 ** -0.5), None, ALU.mult))
                        p = P[t][:, 0:nk]
                        ta = Q.a(lambda e, p=p, ps=ps, nk=nk, m_=m_, z_=z_: e.activation(p, ps[:, 0:nk], ACT.Exp, bias=m_,
                                                                                         scale=float(128 ** -0.5), accum_out=z_), tv, pt, Q.last("pe"))
                        B.free(b, ta)
                        Q.v(lambda e, z_=z_: e.reciprocal(z_, z_), ta)
                        tv = Q.v(lambda e, p=p, z_=z_: e.tensor_scalar(p, p, z_, None, ALU.mult))
                        b, ps, bt = B.take()
                        for k in range(kn):
                            Q.tr(ps[:, k * 128:(k + 1) * 128], p[:, k * 128:(k + 1) * 128], ident, (bt, tv))
                        ta = Q.a(lambda e, ps=ps, t=t, pt_=pt_, nk=nk, kn=kn: e.activation(
                            pt_[:, 0:kn, t * 128:(t + 1) * 128], ps[:, 0:nk].rearrange("p (k t) -> p k t", k=kn), ACT.Copy),
                            Q.pe_done(), free[h % 2])
                        B.free(b, ta)
                    b, ps, bt = B.take()
                    g = h // 2
                    for k in range(kn):
                        kt = k0 // 128 + k
                        Q.mm(ps[:, 0:256], kv[:, kt // 2, kt % 2, 256 + g * 128:256 + (g + 1) * 128], pt_[:, k, :], k == 0, k == kn - 1,
                             (bt, ta, t_kv))
                    free[h % 2] = Q.pe_done()
                    _, tv = parts(mH[:, 4 + h, s, :], mL[:, 4 + h, s, :], ps[:, 0:256], (Q.pe_done(), t_n))
                    B.free(b, tv)

            def take(ps, j, n, pt):
                for s in range(nside):
                    t = Q.v(lambda e: e.scalar_tensor_tensor(src[s][:, j, :], ps[:, s * 256:(s + 1) * 256], mod(l, 2, s)[:, j:j + 1],
                                                             src[s][:, j, :], ALU.mult, ALU.add), pt, link=False)
                return t
            dense("w_out", (l,), list(range(8)), 8, lambda q: mH[:, q, 0:nside, :], lambda q: mL[:, q, 0:nside, :],
                  tuple(lasts()), take, width=256 * nside, per=1)

        def lasts():
            return [Q.last("dve"), Q.last("act"), Q.pe_done()]

        def moe(ph, l):
            open_area(ph, "sc", 12656)
            nT = open_area(ph, "nT", 4096)
            n2 = nT[:, :].rearrange("p (k s t) -> p k s t", k=8, s=2)
            more = open_area(ph, "more", MORE * SLOT)
            if not dry:
                for i in range(MORE):
                    W.idle.append(Slot(more[:, i * SLOT:(i + 1) * SLOT], f"slot{RING + i}", tuple(lasts())))
            nside = 2 if l == 0 else 1
            src = [x8, c8]
            w = 32 * nside
            xs = sc(0, 128 * w).rearrange("p (k e s n) -> p k e s n", k=8, e=16, s=nside)
            PgT = sc(8192, 2048).rearrange("p (s i t) -> p s i t", s=2, i=4)
            P = sc(10240, 1024)
            Pg = sc(11264, 1024)
            Y = sc(10240, 2048).rearrange("p (s n) -> p s n", s=2)
            aff = sc(12288, 32)
            affT = adaT[:, 0:256]
            msk = adaT[:, 256:512]
            cs = sc(12320, 256)
            sl = sc(12576, 32)
            lg = sc(12608, 32)
            st = sc(12640, 16)
            gat = [nT[:, 0:512], nT[:, 512:1024]]
            hid = [nT[:, 1024:1536], nT[:, 1536:2048]]
            aT = [nT[:, 2048:2560], nT[:, 2560:3072]]
            for side in range(nside):
                dst = scales(l, "n2", 4, side)
                tn = norm(src[side], dst, mod(l, 3, side), tuple(lasts()), out=lambda k: n2[:, k, side, :])
                wr = sm("w_router", 128 * l, 128 * l + 128).rearrange("p (k n) -> p k n", k=8)
                for t in range(2):
                    b, ps, bt = B.take()
                    for q in range(8):
                        Q.mm(ps[:, 0:16], n2[:, q, side, t * 128:(t + 1) * 128], wr[:, q, :], q == 0, q == 7, (bt,) + tn)
                    L = lg[:, 16 * t:16 * t + 16]
                    A = aff[:, 16 * t:16 * t + 16]
                    Q.v(lambda e, ps=ps, L=L: e.tensor_copy(L, ps[:, 0:16]), Q.pe_done())
                    B.free(b, Q.last("dve"))
                    Q.v(lambda e, L=L, t=t: e.tensor_reduce(st[:, t:t + 1], L, AX.X, ALU.max))
                    tv = Q.v(lambda e, t=t: e.tensor_scalar(st[:, t:t + 1], st[:, t:t + 1], -1.0, None, ALU.mult))
                    ta = Q.a(lambda e, A=A, L=L, t=t: e.activation(A, L, ACT.Exp, bias=st[:, t:t + 1], accum_out=st[:, 2 + t:3 + t]), tv)
                    Q.v(lambda e, t=t: e.reciprocal(st[:, 2 + t:3 + t], st[:, 2 + t:3 + t]), ta)
                    tv = Q.v(lambda e, A=A, t=t: e.tensor_scalar(A, A, st[:, 2 + t:3 + t], None, ALU.mult))
                if dump is not None:
                    dbg(f"aff{l}{side}", aff, tuple(lasts()))
                b, ps, bt = B.take()
                for t in range(2):
                    Q.tr(ps[0:16, t * 128:(t + 1) * 128], aff[:, 16 * t:16 * t + 16], ident, (bt, tv))
                Q.v(lambda e, ps=ps: e.tensor_copy(affT[0:16, :], ps[0:16, 0:256]), Q.pe_done())
                B.free(b, Q.last("dve"))
                for _ in range(CAP // 8):
                    Q.v(lambda e: e.max(st[0:16, 8:16], affT[0:16, :]))
                    Q.v(lambda e: e.match_replace(affT[0:16, :], st[0:16, 8:16], affT[0:16, :], -1.0))
                Q.v(lambda e: e.tensor_scalar(msk[0:16, :], affT[0:16, :], -1.0, None, ALU.is_equal))
                Q.v(lambda e: e.tensor_tensor_scan(cs[0:16, :], bc(ones[0:16, 0:1], [16, 256]), msk[0:16, :], 0.0, ALU.mult, ALU.add))
                Q.v(lambda e: e.tensor_tensor(cs[0:16, :], cs[0:16, :], msk[0:16, :], ALU.mult))
                tv = Q.v(lambda e: e.tensor_scalar(cs[0:16, :], cs[0:16, :], -1.0, None, ALU.add))
                b, ps, bt = B.take()
                for t in range(2):
                    Q.tr(ps[:, t * 16:(t + 1) * 16], cs[0:16, t * 128:(t + 1) * 128], ident[0:16, 0:16], (bt, tv))
                Q.v(lambda e, ps=ps: e.tensor_copy(sl, ps[:, 0:32]), Q.pe_done())
                B.free(b, Q.last("dve"))
                for t in range(2):
                    pv = P[:, t * 512:(t + 1) * 512].rearrange("p (e j) -> p e j", e=16)
                    pg = Pg[:, t * 512:(t + 1) * 512].rearrange("p (e j) -> p e j", e=16)
                    Q.v(lambda e, pv=pv, t=t: e.tensor_tensor(pv, bc(sm("iota").unsqueeze(1), [128, 16, 32]),
                                                              bc(sl[:, 16 * t:16 * t + 16].unsqueeze(2), [128, 16, 32]), ALU.is_equal), Q.last("pe"))
                    tv = Q.v(lambda e, pv=pv, pg=pg, t=t: e.tensor_tensor(pg, pv, bc(aff[:, 16 * t:16 * t + 16].unsqueeze(2), [128, 16, 32]), ALU.mult))
                for t in range(2):
                    transpose4([Pg[:, t * 512 + i * 128:t * 512 + (i + 1) * 128] for i in range(4)],
                               PgT[:, side, :, t * 128:(t + 1) * 128], (tv,))
                hk = wk[:, :].rearrange("p (t f) -> p t f", t=2)
                for t in range(2):
                    for hf in range(2):
                        t_h = transpose4([n2[:, hf * 4 + i, side, t * 128:(t + 1) * 128] for i in range(4)],
                                         hk[:, t, hf * 512:(hf + 1) * 512].rearrange("p (i t) -> p i t", i=4), tn + (tv,))
                for k in range(8):
                    b, ps, bt = B.take()
                    for t in range(2):
                        Q.mm(ps[:, :], hk[:, t, k * 128:(k + 1) * 128], P[:, t * 512:(t + 1) * 512], t == 0, t == 1, (bt, t_h, tv))
                    xv = ps[:, :].rearrange("p (e n) -> p e n", e=16)
                    if k % 2:
                        tx = Q.a(lambda e: e.activation(xs[:, k, :, side, :], xv, ACT.Copy), Q.pe_done())
                    else:
                        tx = Q.v(lambda e: e.tensor_copy(xs[:, k, :, side, :], xv), Q.pe_done())
                    B.free(b, tx)
            tx = tuple(lasts())
            free_a = [None, None]
            for e_ in range(NE):
                i2, i4 = e_ % 2, e_ % 4
                cs_ = [W.ask(n, (l, e_), j, 4, 8, "raw") for n in ("moe_gate", "moe_up") for j in (0, 4)]
                view = lambda c: c.raw()[0].rearrange("p (j k n) -> p j k n", j=4, k=8)
                X = lambda k: xs[:, k, e_, :, :]
                if nside == 2:
                    bg, psg, tg = B.take()
                    bu, psu, tu = B.take()
                    for ps, bt, cc in ((psg, tg, cs_[0:2]), (psu, tu, cs_[2:4])):
                        vs = [view(c) for c in cc]
                        for k in range(8):
                            for h in range(2):
                                Q.mm(ps[64 * h:64 * h + 64, :].rearrange("p (j n) -> p j n", j=4), X(k), vs[h][:, :, k, :],
                                     k == 0, k == 7, (cc[h].raw()[1], bt) + tx)
                        pt = Q.pe_done()
                        for c in cc:
                            c.done(pt)
                        if ps is psg:
                            ta = Q.a(lambda e: e.activation(gat[i2], psg[:, :], ACT.Silu), pt)
                            B.free(bg, ta)
                    tv = Q.v(lambda e: e.tensor_tensor(hid[i2], psu[:, :], gat[i2], ALU.mult), pt, ta)
                    B.free(bu, tv)
                    rows = slice(0, 128)
                else:
                    b, ps, bt = B.take()
                    vs = [view(c) for c in cs_]
                    for k in range(8):
                        for h in range(4):
                            Q.mm(ps[32 * h:32 * h + 32, :].rearrange("p (j n) -> p j n", j=4), X(k), vs[h][:, :, k, :],
                                 k == 0, k == 7, (cs_[h].raw()[1], bt) + tx)
                    pt = Q.pe_done()
                    for c in cs_:
                        c.done(pt)
                    ta = Q.a(lambda e: e.activation(gat[i2][64:128, :], ps[0:64, :], ACT.Silu), pt)
                    tv = Q.v(lambda e: e.tensor_tensor(hid[i2][64:128, :], ps[64:128, :], gat[i2][64:128, :], ALU.mult), pt, ta)
                    B.free(b, tv)
                    rows = slice(64, 128)
                r = 2 * w
                b, ps, bt = B.take()
                for j in range(4):
                    Q.tr(ps[:, j * r:(j + 1) * r], hid[i2][rows, j * 128:(j + 1) * 128], ident[rows, rows], (bt, tv))
                t_aT = Q.a(lambda e: e.activation(aT[i2][:, 0:4 * r], ps[:, 0:4 * r], ACT.Copy), Q.pe_done(), free_a[i2])
                B.free(b, t_aT)
                cd = [W.ask("moe_down", (l, e_), j, 4, 8, "raw") for j in (0, 4)]
                vs = [view(c) for c in cd]
                b, ps, bt = B.take()
                for k in range(8):
                    lhs = aT[i2][:, (k % 4) * r + (k // 4) * w:(k % 4) * r + (k // 4) * w + w]
                    for h in range(2):
                        Q.mm(ps[w * h:w * h + w, :].rearrange("p (j n) -> p j n", j=4), lhs, vs[h][:, :, k, :],
                             k == 0, k == 7, (cd[h].raw()[1], bt, t_aT))
                pt = Q.pe_done()
                free_a[i2] = pt
                for c in cd:
                    c.done(pt)
                yo = slice(32 * i4, 32 * i4 + 32)
                for h in range(2):
                    for s in range(nside):
                        o = w * h + 32 * s
                        if h:
                            t1 = Q.a(lambda e: e.activation(Y[yo, s, h * 512:(h + 1) * 512], ps[o:o + 32, :], ACT.Copy), pt, y_free[0], link=False)
                        else:
                            t2 = Q.v(lambda e: e.tensor_copy(Y[yo, s, h * 512:(h + 1) * 512], ps[o:o + 32, :]), pt, y_free[0], link=False)
                y_tok[0] = (t1, t2)
                Q.v(lambda e: e.memset(dummy, 0.0), t1)
                B.free(b, Q.last("dve"))
                if i4 == 3:
                    eg = e_ // 4
                    for s in range(nside):
                        for k in range(8):
                            if k % 2 == 0:
                                b, ps, bt = B.take()
                            o = (k % 2) * 256
                            Q.mm(ps[:, o:o + 256], Y[:, s, k * 128:(k + 1) * 128], PgT[:, s, eg, :], True, True, (bt, t1, t2))
                            if k % 2:
                                pt = Q.pe_done()
                                for kk in (k - 1, k):
                                    tv = Q.v(lambda e: e.scalar_tensor_tensor(
                                        src[s][:, kk, :], ps[:, (kk % 2) * 256:(kk % 2) * 256 + 256], mod(l, 5, s)[:, kk:kk + 1],
                                        src[s][:, kk, :], ALU.mult, ALU.add), pt)
                                B.free(b, tv)
                    y_free[0] = Q.pe_done()
            if not dry:
                W.idle = [s for s in W.idle if s.sem not in [f"slot{RING + i}" for i in range(MORE)]]
        y_free, y_tok = [None], [None]

        def open_parts(ph):
            W.WH = open_area(ph, "WH", NB * 1024, F32R)[:, :].rearrange("p (b f) -> p b f", b=NB)
            W.WL = open_area(ph, "WL", NB * 1024, F32R)[:, :].rearrange("p (b f) -> p b f", b=NB)
            W.part_free = [t for t in (lasts() * NB)[0:NB]]
            W.part_free = [tuple(lasts())] * NB

        def shown(i):
            if dump is not None:
                dbg(f"x{i}", xT[:, :], (Q.last("dve"),))

        steps = [even, lambda *a: ffn(*a, 0), lambda *a: ple(*a, 0), odd, lambda *a: ffn(*a, 1), lambda *a: ple(*a, 1)]
        with ExitStack() as first:
            open_parts(first)
            nH, nL = hl(first, 8)
            for i, st_ in enumerate(steps):
                if i < upto:
                    with ExitStack() as ph:
                        st_(ph, nH, nL)
                    shown(i)
            while ada_n[0] < 24 or ada_late:
                fill(1)
        if upto > 6:
            t_ctx = load_consts()
            with ExitStack() as ph:
                open_parts(ph)
                mixer2(ph, 0)
            shown(6)
            with ExitStack() as ph:
                moe(ph, 0)
            shown(7)
        if upto > 8:
            with ExitStack() as ph:
                open_parts(ph)
                mixer2(ph, 1)
            with ExitStack() as ph:
                moe(ph, 1)
        if dry:
            return W.asked

        t_o = Q.dma("sp", out_dram, xT[:, :], s_out, (Q.last("dve"),))
        nc.sync.wait_ge(Q.sem[t_o[0]], t_o[1])


def constants():
    f = np.float32
    i = np.arange(128)
    c = {}
    c["ident"] = np.eye(128, dtype=f)
    c["ones"] = np.ones((128, 128), f)
    inv = []
    for dim in (64, 32):
        e = np.arange(0, dim, 2, dtype=f) / f(dim)
        inv.append((1.0 / np.power(f(10000.0), e)).astype(f))
    c["invf"] = np.tile(np.concatenate(inv)[None, :], (128, 1))
    c["tri"] = np.where(i[None, :] <= i[:, None], 0.0, -BIG).astype(f)
    c["iota"] = np.tile(np.arange(32, dtype=f)[None, :], (128, 1))
    t = np.arange(256)
    inv2 = 10000.0 ** (-np.arange(0, 64, 2, dtype=np.float64) / 64)
    ang = np.stack([(t // 64)[:, None] * inv2, (t % 64)[:, None] * inv2], 1).reshape(2, 128, 64)
    c["rcos"] = np.cos(ang).transpose(1, 0, 2).reshape(128, 128).astype(f)
    c["rsin"] = np.sin(ang).transpose(1, 0, 2).reshape(128, 128).astype(f)
    lv = []
    for l in range(6):
        b = 1 << l
        same = (i[:, None] // (2 * b)) == (i[None, :] // (2 * b))
        lv.append((same & ((i[:, None] // b) % 2 == 0) & ((i[None, :] // b) % 2 == 1)).astype(f))
    c["levels"] = np.concatenate(lv, 1)
    same = (i[:, None] // 64) == (i[None, :] // 64)
    c["cumT"] = (same & (i[:, None] <= i[None, :])).astype(f)
    c["lastT"] = (same & (i[:, None] % 64 == 63)).astype(f)
    c["sel"] = np.concatenate([np.tile((i == 63 + 64 * j).astype(f)[:, None], (1, 128)) for j in range(2)], 1)
    c["dmask"] = np.where(same & (i[None, :] <= i[:, None]), 0.0, BIG).astype(f)
    n = np.arange(256)
    a = 2 * np.pi * ((n[:, None] * n[None, :]) % 256) / 256
    cs = np.concatenate([np.cos(a), np.sin(a)], 1) / 16.0
    cs = cs.reshape(2, 128, 512).transpose(1, 0, 2).reshape(128, 1024)
    d = np.arange(64)
    b = 2 * np.pi * ((d[:, None] * d[None, :]) % 64) / 64
    bd = np.zeros((128, 256))
    for k in range(2):
        bd[64 * k:64 * k + 64, 64 * k:64 * k + 64] = np.cos(b) / 8.0
        bd[64 * k:64 * k + 64, 128 + 64 * k:128 + 64 * k + 64] = -np.sin(b) / 8.0
    dft = np.concatenate([cs, bd], 1).astype(f)
    pa = []
    for win in (2, 4, 8, 16):
        lo = np.clip(n - win // 2, 0, 256)
        hi = np.clip(n + win // 2, 0, 256)
        s = n[:, None]
        m = ((s >= lo[None, :]) & (s < hi[None, :])) / (hi - lo)[None, :].astype(np.float64) - np.eye(256)
        pa.append(m.reshape(2, 128, 256).transpose(1, 0, 2).reshape(128, 512))
    return c, dft, np.concatenate(pa, 1).astype(f)


def layout(a):
    cat, asc = np.concatenate, np.ascontiguousarray

    def blocks(w):
        lead = w.shape[:-2]
        k, n = w.shape[-2:]
        w = w.reshape(*lead, k // 128, 128, n // 128, 128)
        r = len(lead)
        w = w.transpose(*range(r), r + 2, r + 1, r, r + 3)
        return asc(w.reshape(*lead, n // 128, 128, k))

    def pad(w):
        return cat([w, np.zeros((w.shape[0], -w.shape[1] % 128), w.dtype)], 1)

    def featT(x):
        t, k = x.shape
        return asc(x.T.reshape(k // 128, 128, t).transpose(1, 0, 2).reshape(128, -1))

    def cols(v):
        v = v.reshape(-1, 128)
        return v.T

    def rows(v):
        return np.broadcast_to(v.reshape(1, -1), (128, v.size))

    const, dft, poolA = constants()
    s = dict(const)
    s["xtiny"] = rows(a["od_a_log"][0][0:2])
    s["norm_mix"] = cols(a["norm_mix_g"])
    s["norm_ffn"] = cols(a["norm_ffn_g"])
    s["ple_post"] = cols(a["ple_post_norm_g"])
    s["ple_norm"] = cols(a["ple_norm_g"])
    s["ev_conv"] = a["ev_conv_w"][0].reshape(3, 4, 128).transpose(2, 1, 0).reshape(128, 12)
    s["od_conv"] = a["od_conv_w"][0].reshape(4, 24, 128).transpose(2, 1, 0).reshape(128, 96)
    s["ev_qg"] = rows(a["ev_q_norm_g"])
    s["ev_kg"] = rows(a["ev_k_norm_g"])
    s["ln_g"] = rows(a["ev_ik_ln_g"])
    s["ln_b"] = rows(a["ev_ik_ln_b"])
    s["o_g"] = rows(a["od_o_norm_g"])
    s["a_log"] = rows(a["od_a_log"])
    s["dt_bias"] = rows(a["od_dt_bias"])
    s["c2"] = np.stack([cols(a["c_2"]), cols(a["c_ctx_2"])], 2).reshape(128, 16)
    s["ada_b"] = cols(a["ada_b_2"])
    s["n1"] = cols(a["norm1_g_2"])
    s["n2"] = cols(a["norm2_g_2"])
    s["pool_scale"] = cols(a["pool_scale_2"])
    s["qg"] = rows(a["q_norm_g_2"])
    s["kg"] = rows(a["k_norm_g_2"])
    s["w_pool"] = a["w_pool_2"].reshape(2, 2, 128, 64).transpose(2, 0, 1, 3).reshape(128, 256)
    s["w_router"] = a["w_router_2"].reshape(2, 8, 128, 16).transpose(2, 0, 1, 3).reshape(128, 256)
    small = cat([np.asarray(s[n]).reshape(128, w) for n, w in SMALL], 1)
    ev, od = a["ev_w_in"][0], a["od_w_in"][0]
    return {
        "small": asc(small), "xT": featT(a["x"][0]), "ctxT": featT(a["ctx_2"][0]),
        "posT": asc(a["positions"].reshape(2, 128).T), "dft": dft, "poolA": poolA,
        "pT": asc(np.stack([featT(a["p"][l, 0]) for l in range(2)])),
        "ev_in": blocks(pad(ev)), "ev_out": blocks(a["ev_w_out"][0]),
        "od_in": blocks(pad(od)), "od_out": blocks(a["od_w_out"][0]),
        "ffn_gate": blocks(a["ffn_w_gate"]), "ffn_up": blocks(a["ffn_w_up"]), "ffn_down": blocks(a["ffn_w_down"]),
        "ple_proj": blocks(a["ple_w_proj"]), "ple_gate": blocks(a["ple_w_gate"]),
        "ada": blocks(a["ada_w_2"]), "w_in": blocks(a["w_in_2"]), "w_out": blocks(a["w_out_2"]),
        "w_four": blocks(a["w_fourier_2"]),
        "moe_gate": blocks(a["w_gate_2"]), "moe_up": blocks(a["w_up_2"]), "moe_down": blocks(a["w_down_2"]),
    }


def kernel(**inputs):
    import numpy as _np
    import concourse.bacc as _bacc
    from concourse import mybir as _mybir
    from concourse.bass_utils import run_bass_kernel_spmd as _run

    arrays = layout({k: _np.asarray(v) for k, v in inputs.items()})
    plan = None
    for dry in (True, False):
        nc = _bacc.Bacc("TRN2", target_bir_lowering=False, num_devices=1)
        dr = {n: nc.dram_tensor(n, v.shape, _mybir.dt.from_np(v.dtype), kind="ExternalInput").ap() for n, v in arrays.items()}
        out = nc.dram_tensor("out", (128, 2048), _mybir.dt.float32, kind="ExternalOutput").ap()
        plan = program(nc, dr, out, plan, dry)
    r = _run(nc, [arrays], core_ids=[0])
    o = r.results[0]["out"].reshape(128, 8, 256)
    return _np.ascontiguousarray(o.transpose(2, 1, 0).reshape(1, 256, 1024))
```

```python
from contextlib import ExitStack

import numpy as np
import concourse.bass as bass
from concourse import mybir

F32 = mybir.dt.float32
F32R = mybir.dt.float32r
I32 = mybir.dt.int32
ALU = mybir.AluOpType
ACT = mybir.ActivationFunctionType
AX = mybir.AxisListType

D = 1024
EPS = 1e-6
BIG = 1e30
TAKEN = -3e38
RING = 3
MORE = 3
NB = 3
AHEAD = 2
SLOT = 4096
NE = 16
CAP = 32
MAGIC = 12582912.0
TWO_PI_A = 6.28125
TWO_PI_B = 0.00193500518798828125
TWO_PI_C = float(2 * np.pi - 6.28125 - 0.00193500518798828125)

FIRST = 321
SMALL = [
    ("eps", 1), ("norm_mix", 16), ("ones", 128), ("ident", 128), ("invf", 48), ("norm_ffn", 16), ("ple_post", 16), ("ple_norm", 16),
    ("ev_conv", 12), ("od_conv", 96), ("ev_qg", 64), ("ev_kg", 64), ("ln_g", 64), ("ln_b", 64),
    ("o_g", 128), ("a_log", 8), ("dt_bias", 8),
    ("c2", 16), ("ada_b", 96), ("n1", 16), ("n2", 16), ("pool_scale", 4),
    ("qg", 256), ("kg", 256), ("w_pool", 256), ("w_router", 256),
    ("tri", 128), ("iota", 32),
    ("rcos", 256), ("rsin", 256), ("levels", 768), ("cumT", 128), ("lastT", 128),
    ("sel", 256), ("dmask", 128),
]
OFF = {}
_at = 0
for _n, _w in SMALL:
    OFF[_n] = (_at, _w)
    _at += _w
NSMALL = _at


class Queues:

    def __init__(self, nc, ctx, dry):
        self.nc, self.ctx, self.dry = nc, ctx, dry
        self.eng = {"pe": nc.tensor, "act": nc.scalar, "dve": nc.vector, "pool": nc.gpsimd, "sp": nc.sync}
        self.sem = {n: ctx.enter_context(nc.semaphore("s_" + n)) for n in self.eng}
        self.count = {n: 0 for n in self.sem}
        self.seen = {n: {} for n in self.eng}
        self.mm_last = None
        self.names = 0

    def count_names(self):
        self.names += 1
        return self.names

    def new_sem(self, name):
        self.sem[name] = self.ctx.enter_context(self.nc.semaphore(name))
        self.count[name] = 0
        return name

    def put(self, eng, fn, after=(), inc=None, by=1):
        if self.dry:
            return inc, 0
        e = self.eng[eng]
        flat = list(after)
        for t in flat:
            if t is None:
                continue
            if not isinstance(t[0], str):
                flat.extend(t)
                continue
            name, value = t
            if self.seen[eng].get(name, 0) < value:
                self.seen[eng][name] = value
                e.wait_ge(self.sem[name], value)
        ins = fn(e)
        if inc:
            ins.then_inc(self.sem[inc], by)
            self.count[inc] += by
            return inc, self.count[inc]
        self.mm_last = ins
        return None

    def mm(self, out, lhsT, rhs, start, stop, after=(), skip=False):
        self.put("pe", lambda e: e.matmul(out, lhsT, rhs, start=start, stop=stop, skip_group_check=skip), after)

    def tr(self, out, in_, ident, after=()):
        self.put("pe", lambda e: e.transpose(out, in_, ident), after)

    def pe_done(self):
        if self.mm_last is not None:
            self.mm_last.then_inc(self.sem["pe"], 1)
            self.mm_last = None
            self.count["pe"] += 1
        return "pe", self.count["pe"]

    def _one(self, eng, fn, after, link):
        prev = (eng, self.count[eng]) if link else None
        return self.put(eng, fn, (prev,) + tuple(after), eng)

    def v(self, fn, *after, link=True):
        return self._one("dve", fn, after, link)

    def a(self, fn, *after, link=True):
        return self._one("act", fn, after, link)

    def g(self, fn, *after, link=True):
        return self._one("pool", fn, after, link)

    def last(self, eng):
        return (eng, self.count[eng])

    def dma(self, eng, out, in_, sem, after=()):
        return self.put(eng, lambda e: e.dma_start(out, in_), after, sem, 16)


class Banks:

    def __init__(self, nc, ctx):
        self.bank = [ctx.enter_context(nc.psum_tensor(f"ps{i}", [128, 512], F32)) for i in range(8)]
        self.idle = [(i, None) for i in range(8)]

    def take(self):
        i, tok = self.idle.pop(0)
        return i, self.bank[i], tok

    def free(self, i, tok):
        self.idle.append((i, tok))


class Slot:

    def __init__(self, ap, sem, free=None):
        self.ap, self.sem, self.free = ap, sem, free


class Chunk:

    def __init__(self, ws, n, key):
        self.ws, self.n, self.key = ws, n, key

    def raw(self):
        return self.ws.load(self.n)

    def piece(self, i):
        return self.ws.split(self.n, i)

    def done(self, tok):
        self.ws.release(self.n, tok)


class Weights:

    def __init__(self, Q, dr, plan):
        self.Q, self.dr, self.plan = Q, dr, plan
        self.asked = []
        self.idle = []
        self.place = {}
        self.parts = {}
        self.used = {}
        self.units = []
        self.at = 0
        self.turn = 0
        self.part_free = [None] * NB
        if plan is not None:
            for n, key in enumerate(plan):
                if key[-1] == "raw":
                    self.units.append((n, None))
                else:
                    self.units += [(n, i) for i in range(self.pieces(key))]

    @staticmethod
    def pieces(key):
        _, _, _, m, kt, mode = key
        return kt // 2 if mode == "tok" else -(-m * kt // 8)

    def ask(self, name, idx, j0, m, kt, mode):
        key = (name, idx, j0, m, kt, mode)
        self.asked.append(key)
        n = len(self.asked) - 1
        assert self.plan is None or self.plan[n] == key
        return Chunk(self, n, key)

    def load(self, n):
        if self.Q.dry:
            return self.slots[0].ap, None
        if n not in self.place:
            assert n == len(self.place)
            slot = self.idle.pop(0)
            name, idx, j0, m, kt, _ = self.plan[n]
            w = self.dr[name]
            for i in idx:
                w = w[i]
            f = kt * 128
            dst = slot.ap[:, 0:m * f]
            tok = self.Q.dma("sp", dst.rearrange("p (j f) -> p j f", j=m), w[j0:j0 + m].rearrange("j p f -> p j f"),
                             slot.sem, (slot.free,))
            self.place[n] = (slot, tok)
        slot, tok = self.place[n]
        return slot.ap, tok

    def release(self, n, tok):
        if self.Q.dry:
            return
        slot = self.place[n][0]
        slot.free = tok
        self.idle.append(slot)

    def prime(self):
        while not self.Q.dry and len(self.parts) < 2 and self.emit():
            pass

    def emit(self):
        while self.at < len(self.units) and self.units[self.at][1] is None and self.units[self.at][0] in self.place:
            self.at += 1
        if self.at >= len(self.units):
            return False
        n, i = self.units[self.at]
        if i is None or (n not in self.place and not self.idle):
            return False
        if len(self.parts) + self.held >= NB:
            return False
        ap, tok = self.load(n)
        _, _, _, m, kt, mode = self.plan[n]
        b = self.at_part % NB
        self.at_part += 1
        if mode == "tok":
            src = ap[:, 0:m * kt * 128].rearrange("p (j f) -> p j f", j=m)[:, :, i * 256:(i + 1) * 256]
            width = m * 256
            view = lambda x: x[:, 0:width].rearrange("p (j f) -> p j f", j=m)
        else:
            width = min(1024, m * kt * 128 - i * 1024)
            src = ap[:, i * 1024:i * 1024 + width]
            view = lambda x: x[:, 0:width]
        H, L = self.WH[:, b, :], self.WL[:, b, :]
        free = self.part_free[b]
        tH = self.Q.a(lambda e: e.activation(view(H), src, ACT.Copy), tok, free, link=False)
        tL = self.Q.v(lambda e: e.tensor_tensor(view(L), src, view(H).bitcast(F32), ALU.subtract), tok, tH, free, link=False)
        self.parts[(n, i)] = (H, L, tH, tL, b)
        self.at += 1
        if self.at == len(self.units) or self.units[self.at][0] != n:
            self.release(n, tL)
        return True

    at_part = 0
    held = 0

    def split(self, n, i):
        if self.Q.dry:
            return self.WH[:, 0, :], self.WL[:, 0, :], None, None, 0
        while (n, i) not in self.parts:
            while self.units[self.at][1] is None:
                self.at += 1
            assert self.emit()
        p = self.parts.pop((n, i))
        self.held += 1
        for _ in range(AHEAD - (len(self.parts))):
            if not self.emit():
                break
        return p

    def free_part(self, p, tok):
        self.part_free[p[4]] = tok
        self.held -= not self.Q.dry


def bc(ap, shape):
    return ap.to_broadcast(shape)


def program(nc, dr, out_dram, plan=None, dry=False):
    with ExitStack() as ctx:
        Q = Queues(nc, ctx, dry)
        B = Banks(nc, ctx)
        W = Weights(Q, dr, plan)

        def sb(name, n):
            return ctx.enter_context(nc.sbuf_tensor("m_" + name, [128, n], F32))

        small = sb("small", NSMALL)
        xT = sb("xT", 2048)
        cT = sb("cT", 2048)
        wk = sb("wk", 2048)
        misc = sb("misc", 1152)
        adaT = sb("adaT", 512)
        ring = ctx.enter_context(nc.sbuf_tensor("ring", [128, RING, SLOT], F32))
        for i in range(RING + MORE):
            Q.new_sem(f"slot{i}")
        W.slots = [Slot(ring[:, i, :], f"slot{i}") for i in range(RING)]
        W.idle = list(W.slots)
        posi = ctx.enter_context(nc.sbuf_tensor("posi", [128, 2], I32))

        def sm(name, a=0, b=None):
            o, w = OFF[name]
            return small[:, o + a:o + (w if b is None else b)]

        area = {}

        def open_area(ph, name, n, dt=F32):
            area[name] = ph.enter_context(nc.sbuf_tensor(f"{name}_{Q.count_names()}", [128, n], dt))
            return area[name]

        def sc(off, n):
            assert off + n <= area["sc"].shape[1]
            return area["sc"][:, off:off + n]

        x8 = xT[:, :].rearrange("p (k t) -> p k t", k=8)
        c8 = cT[:, :].rearrange("p (k t) -> p k t", k=8)
        wk8 = wk[:, :].rearrange("p (k t) -> p k t", k=8)
        ident = sm("ident")
        ones = sm("ones")

        mo = [0]

        def mi(n):
            mo[0] += n
            assert mo[0] <= 1152
            return misc[:, mo[0] - n:mo[0]]

        s_out = Q.new_sem("s_out")
        dummy = misc[:, 1150:1152]

        s_x, s_in, s_pos = Q.new_sem("s_x"), Q.new_sem("s_in"), Q.new_sem("s_pos")
        Q.dma("sp", small[:, 0:FIRST], dr["small"][:, 0:FIRST], s_pos)
        t_pos = Q.dma("act", posi[:, :], dr["posT"], s_pos)
        t_x = Q.dma("sp", xT[:, :], dr["xT"], s_x)
        t_in = Q.dma("act", small[:, FIRST:NSMALL], dr["small"][:, FIRST:NSMALL], s_in)

        def dense(*args, **kw):
            for _ in dense_steps(*args, **kw):
                pass

        def by_token(*args):
            for _ in by_token_steps(*args):
                pass

        background = []

        def fill(n):
            for _ in range(n):
                while background:
                    if next(background[0], "end") != "end":
                        break
                    background.pop(0)
                else:
                    ada_step()

        def finish():
            while background:
                for _ in background.pop(0):
                    pass

        def dense_steps(name, idx, tiles, kt, xH, xL, tok, consume, per=2, width=256):
            m = {8: 4, 4: 8, 2: 8}.get(kt, 1)
            i = 0
            held = None
            while i < len(tiles):
                k = min(m, len(tiles) - i)
                c = W.ask(name, idx, tiles[i], k, kt, "T")
                nb = k * kt
                for p0 in range(0, nb, 8):
                    part = c.piece(p0 // 8)
                    H, L, tH, tL, _ = part
                    blocks = list(range(p0, min(p0 + 8, nb)))
                    while blocks:
                        j = blocks[0] // kt
                        mine = [n for n in blocks if n // kt == j]
                        blocks = blocks[len(mine):]
                        g = (i + j) % per
                        first, last = mine[0] % kt == 0, mine[-1] % kt == kt - 1
                        if g == 0 and first:
                            held = B.take()
                        b, ps, bt = held
                        o = ps[:, g * width:(g + 1) * width]
                        for n in mine:
                            w = H[:, (n - p0) * 128:(n - p0 + 1) * 128]
                            Q.mm(o, w, xH(n % kt), first and n == mine[0], False, (tH, bt) + tok)
                            Q.mm(o, w, xL(n % kt), False, False)
                        for n in mine:
                            w = L[:, (n - p0) * 128:(n - p0 + 1) * 128]
                            Q.mm(o, w, xH(n % kt), False, last and n == mine[-1], (tL,))
                        if last and (g == per - 1 or i + j == len(tiles) - 1):
                            pt = Q.pe_done()
                            B.free(b, consume(ps, i + j - g, g + 1, pt))
                    W.free_part(part, Q.pe_done())
                    yield
                i += k

        def by_token_steps(name, idx, j0, xH, xL, which, tok, consume):
            c = W.ask(name, idx, j0, 4, 8, "tok")
            held = [B.take() for _ in which]
            for i in range(4):
                part = c.piece(i)
                H, L, tH, tL, _ = part
                H4 = H.rearrange("p (j k n) -> p j k n", j=4, k=2)
                L4 = L.rearrange("p (j k n) -> p j k n", j=4, k=2)
                for (b, ps, bt), st in zip(held, which):
                    o = ps[:, :].rearrange("p (j n) -> p j n", j=4)
                    for k in range(2):
                        q = 2 * i + k
                        Q.mm(o, xH(q, *st), H4[:, :, k, :], q == 0, False, (tH, bt) + tok)
                        Q.mm(o, xL(q, *st), H4[:, :, k, :], False, False)
                    for k in range(2):
                        q = 2 * i + k
                        Q.mm(o, xH(q, *st), L4[:, :, k, :], False, q == 7, (tL,))
                W.free_part(part, Q.pe_done())
                if i < 3:
                    yield
            pt = Q.pe_done()
            for (b, ps, bt), st in zip(held, which):
                B.free(b, consume(ps, pt, *st))
            yield

        rr = mi(256)

        def power(ap):
            t = Q.v(lambda e: e.reciprocal(ap, ap))
            return Q.a(lambda e: e.activation(ap, ap, ACT.Sqrt), t)

        def rstd(ps, n, dim, eps, tok):
            Q.v(lambda e: e.tensor_scalar(rr[:, 0:n], ps, 1.0 / dim, eps, ALU.mult, ALU.add), tok)
            return power(rr[:, 0:n])

        acc = [wk[:, 0:512], sm("levels", 0, 512)]
        sq = [wk[:, 512:1024], wk[:, 1024:1536]]
        sq_free = [None, None]
        late = []
        summed = [None, None]

        def square(src, j, n, tok, side=0):
            o = 256 * (j % 2)
            v = lambda a: a[:, o:o + n * 256].rearrange("p (k t) -> p k t", k=n)
            if j < 2:
                summed[side] = (summed[side] if j else None, Q.a(lambda e: e.activation(v(acc[side]), src[:, j:j + n, :], ACT.Square), tok, link=False))
                return
            i = (j // 2) % 2
            settle()
            ta = Q.a(lambda e: e.activation(v(sq[i]), src[:, j:j + n, :], ACT.Square), tok, sq_free[i], link=False)

            def add():
                sq_free[i] = summed[side] = Q.v(lambda e: e.tensor_tensor(v(acc[side]), v(acc[side]), v(sq[i]), ALU.add),
                                                ta, summed[side])
            late.append(add)

        def settle():
            while late:
                late.pop(0)()

        def norm_stats(src, tok, side, r):
            settle()
            b, ps, bt = B.take()
            if side is None:
                ta = Q.a(lambda e: e.activation(wk8[:, 0:4, :], src[:, 0:4, :], ACT.Square), *tok)
                Q.v(lambda e: e.tensor_tensor(wk8[:, 4:8, :], src[:, 4:8, :], src[:, 4:8, :], ALU.mult), *tok)
                Q.v(lambda e: e.tensor_tensor(wk8[:, 4:6, :], wk8[:, 4:6, :], wk8[:, 6:8, :], ALU.add))
                Q.v(lambda e: e.tensor_tensor(wk8[:, 0:2, :], wk8[:, 0:2, :], wk8[:, 2:4, :], ALU.add), ta, link=False)
                t = Q.v(lambda e: e.tensor_tensor(wk8[:, 0:2, :], wk8[:, 0:2, :], wk8[:, 4:6, :], ALU.add))
                a = wk[:, 0:512]
            else:
                t, a = summed[side], acc[side]
            if side is not None:
                W.prime()
            Q.a(lambda e: e.activation(r[:, 0:1], sm("eps"), ACT.Sqrt), *tok, link=False)
            Q.mm(ps[:, 0:256], ones, a[:, 0:256], True, False, (t, bt))
            Q.mm(ps[:, 0:256], ones, a[:, 256:512], False, True)
            pt = Q.pe_done()
            t = Q.a(lambda e: e.activation(r, ps[:, 0:256], ACT.Sqrt, bias=sm("eps"), scale=1.0 / D), pt)
            B.free(b, t)
            t = Q.v(lambda e: e.reciprocal(r, r), t)
            return t, r

        def norm(src, gain, shift, tok, outH=None, outL=None, out=None, side=None, room=wk8, fills=0, stats=None):
            tok = tuple(tok)
            if stats is None:
                stats = norm_stats(src, tok, side, rr[:, 0:256])
            t, r = stats
            first = tok + (t, Q.last("act"))
            todo = []
            for k in range(8):
                y = room[:, k, :] if out is None else out(k)
                t = Q.v(lambda e: e.scalar_tensor_tensor(y, src[:, k, :], gain[:, k:k + 1], r,
                                                         ALU.mult, ALU.mult), *first, link=False)
                if out is not None:
                    if shift is not None:
                        t = Q.a(lambda e: e.activation(y, y, ACT.Identity, bias=shift[:, k:k + 1]), t, link=False)
                    continue
                if shift is None:
                    ta = Q.a(lambda e: e.activation(outH(k), y, ACT.Copy), t, *first, link=False)
                    todo.append(lambda k=k, y=y, ta=ta: Q.v(lambda e: e.tensor_tensor(
                        outL(k), y, outH(k).bitcast(F32), ALU.subtract), ta, link=False))
                else:
                    ta = Q.a(lambda e: e.activation(outH(k), y, ACT.Identity, bias=shift[:, k:k + 1]), t, *first, link=False)
                    todo.append(lambda k=k, y=y, ta=ta: Q.v(lambda e: e.scalar_tensor_tensor(
                        outL(k), y, shift[:, k:k + 1], outH(k).bitcast(F32), ALU.add, ALU.subtract), ta, link=False))
                if len(todo) > 2:
                    todo.pop(0)()
            for f in todo:
                f()
            done = (Q.last("dve"), Q.last("act"))
            fill(fills)
            return done

        def parts(H, L, src, tok, rtok=()):
            ta = Q.a(lambda e: e.activation(H, src, ACT.Copy), *tok, *rtok)
            return ta, Q.v(lambda e: e.tensor_tensor(L, src, H.bitcast(F32), ALU.subtract), ta, *rtok)

        def transpose4(parts, dst, tok, eng="act"):
            b, ps, bt = B.take()
            for i, p in enumerate(parts):
                Q.tr(ps[:, i * 128:(i + 1) * 128], p, ident, (bt,) + tok)
            pt = Q.pe_done()
            n = len(parts)
            src = ps[:, 0:n * 128].rearrange("p (i t) -> p i t", i=dst.shape[1])
            if eng == "act":
                t = Q.a(lambda e: e.activation(dst, src, ACT.Copy), pt)
            else:
                t = Q.v(lambda e: e.tensor_copy(dst, src), pt)
            B.free(b, t)
            return t

        def head_norm(z, tmp, heads, dim, scale_to=None, tok=()):
            ta = Q.a(lambda e: e.activation(tmp, z, ACT.Square), Q.last("dve"), *tok)
            Q.v(lambda e: e.tensor_reduce(rr[:, 0:heads], tmp, AX.X, ALU.add), ta)
            Q.v(lambda e: e.tensor_scalar(rr[:, 0:heads], rr[:, 0:heads], 1.0 / (scale_to or dim), EPS, ALU.mult, ALU.add))
            tp = power(rr[:, 0:heads])
            return Q.v(lambda e: e.tensor_tensor(z, z, bc(rr[:, 0:heads].unsqueeze(2), [128, heads, dim]), ALU.mult), tp)

        def rope(o1, o2, x1, x2, c, s, t1, t2):
            Q.v(lambda e: e.tensor_tensor(t1, x1, c, ALU.mult))
            Q.v(lambda e: e.tensor_tensor(t2, x2, s, ALU.mult))
            Q.v(lambda e: e.tensor_tensor(t1, t1, t2, ALU.subtract))
            Q.v(lambda e: e.tensor_tensor(t2, x1, s, ALU.mult))
            Q.v(lambda e: e.tensor_tensor(o2, x2, c, ALU.mult))
            Q.v(lambda e: e.tensor_tensor(o2, o2, t2, ALU.add))
            return Q.v(lambda e: e.tensor_copy(o1, t1))

        def hl(ph, k, s=1):
            H = open_area(ph, "H", k * s * 256, F32R)
            L = open_area(ph, "L", k * s * 256, F32R)
            if s == 1:
                return [x[:, :].rearrange("p (k t) -> p k t", k=k) for x in (H, L)]
            return [x[:, :].rearrange("p (k s t) -> p k s t", k=k, s=s) for x in (H, L)]

        def add_x(ps, j, n, pt):
            t = Q.v(lambda e: e.tensor_tensor(x8[:, j:j + n, :], x8[:, j:j + n, :],
                                              ps[:, 0:n * 256].rearrange("p (k t) -> p k t", k=n), ALU.add), pt, link=False)
            square(x8, j, n, t)
            return t

        def turn(x, tmp, c, s, view, halves):
            tmp1, tmp2 = halves(tmp)
            x1, x2 = halves(x)
            Q.v(lambda e: e.tensor_tensor(view(tmp), view(x), s, ALU.mult))
            Q.v(lambda e: e.tensor_tensor(view(x), view(x), c, ALU.mult), link=False)
            Q.v(lambda e: e.tensor_tensor(x1, x1, tmp2, ALU.subtract))
            return Q.v(lambda e: e.tensor_tensor(x2, x2, tmp1, ALU.add), link=False)

        def head_rstd(z, tmp, out, dim, tok, factor=None):
            ta = Q.a(lambda e: e.activation(tmp, z, ACT.Square), *tok)
            Q.v(lambda e: e.tensor_reduce(out, tmp, AX.X, ALU.add), ta)
            Q.v(lambda e: e.tensor_scalar(out, out, 1.0 / dim, EPS, ALU.mult, ALU.add))
            t = power(out)
            if factor is not None:
                t = Q.v(lambda e: e.tensor_scalar(out, out, factor, None, ALU.mult), t)
            return t

        def even(ph, nH, nL):
            open_area(ph, "sc", 14216)
            mH, mL = hl(ph, 8)
            at = [0]

            def place(n):
                at[0] += n
                return sc(at[0] - n, n)

            q, k, vv, qi = (place(1024) for _ in range(4))
            kid, kiT = place(256), place(256)
            qTt, kTt, qiT = (place(1024).rearrange("p (k t) -> p k t", k=4) for _ in range(3))
            score, bias = place(384), place(384)
            P = [place(768) for _ in range(2)]
            PT = [place(768) for _ in range(2)]
            tmp = place(1024)
            u = place(1032).rearrange("p (k t) -> p k t", k=4)
            cqs = [place(128) for _ in range(4)]
            cI, sI = place(64), place(64)
            zc = cT[:, 0:1024]
            zz = cT[:, 1024:2048]
            wi = mi(16)
            posf = mi(2)
            st = mi(96)
            rq = st[:, 0:16]
            rk = st[:, 16:32]
            mu = st[:, 32:34]
            ri = st[:, 34:36]
            best = [st[:, 40:48], st[:, 48:56]]
            soft = [st[:, 56:64], st[:, 64:72]]

            Q.v(lambda e: e.tensor_copy(posf, posi[:, :]), t_pos)
            ang = tmp[:, 0:96]
            r1 = tmp[:, 96:192]
            r2 = tmp[:, 192:288]
            cosA, sinA = tmp[:, 288:416], tmp[:, 416:544]
            for t in range(2):
                Q.v(lambda e: e.tensor_scalar(ang[:, 48 * t:48 * t + 48], sm("invf"), posf[:, t:t + 1], None, ALU.mult))
            for quarter in (0.25, 0.0):
                Q.v(lambda e: e.tensor_scalar(r1, ang, float(1 / (2 * np.pi)), quarter, ALU.mult, ALU.add), Q.last("act"))
                Q.v(lambda e: e.tensor_scalar(r1, r1, MAGIC, None, ALU.add))
                Q.v(lambda e: e.tensor_scalar(r1, r1, -MAGIC, None, ALU.add))
                Q.v(lambda e: e.scalar_tensor_tensor(r2, r1, -TWO_PI_A, ang, ALU.mult, ALU.add))
                Q.v(lambda e: e.scalar_tensor_tensor(r2, r1, -TWO_PI_B, r2, ALU.mult, ALU.add))
                Q.v(lambda e: e.scalar_tensor_tensor(r2, r1, -TWO_PI_C, r2, ALU.mult, ALU.add))
                if quarter:
                    Q.v(lambda e: e.tensor_scalar(r2, r2, float(np.pi / 2), None, ALU.add))
                Q.v(lambda e: e.tensor_scalar(r2, r2, 3.1415925, None, ALU.min))
                t_r = Q.v(lambda e: e.tensor_scalar(r2, r2, -3.1415925, None, ALU.max))
                v2 = r2.rearrange("p (t f) -> p t f", t=2)
                A_, I_ = (cosA, cI) if quarter else (sinA, sI)
                for x in range(2):
                    Q.a(lambda e: e.activation(A_.rearrange("p (t x f) -> p t x f", t=2, x=2)[:, :, x, :], v2[:, :, 0:32], ACT.Sin), t_r, link=False)
                    t_cs = Q.a(lambda e: e.activation(I_.rearrange("p (t x f) -> p t x f", t=2, x=2)[:, :, x, :], v2[:, :, 32:48], ACT.Sin), t_r, link=False)
            tn = norm(x8, sm("norm_mix", 0, 8), None, (t_x, t_pos), lambda k: nH[:, k, :], lambda k: nL[:, k, :])
            W.prime()
            for i, (tab, g) in enumerate(((cosA, "ev_qg"), (sinA, "ev_qg"), (cosA, "ev_kg"), (sinA, "ev_kg"))):
                t_tab = Q.v(lambda e: e.tensor_tensor(cqs[i].rearrange("p (t f) -> p t f", t=2), tab.rearrange("p (t f) -> p t f", t=2),
                                                      bc(sm(g).unsqueeze(1), [128, 2, 64]), ALU.mult), t_cs, t_in, link=False)

            xH = lambda q: nH[:, q, :]
            xL = lambda q: nL[:, q, :]
            yH = lambda q, t: nH[:, q, t * 128:(t + 1) * 128]
            yL = lambda q, t: nL[:, q, t * 128:(t + 1) * 128]
            th = lambda a: a.rearrange("p (t h d) -> p t h d", t=2, h=8)
            heads = lambda a: a.rearrange("p (n d) -> p n d", n=16)
            split64 = lambda a: [a.rearrange("p (n x f) -> p n x f", n=16, x=2)[:, :, i, :] for i in range(2)]

            def copy_to(dst):
                return lambda ps, pt, t: Q.a(lambda e: e.activation(dst[:, t * 512:(t + 1) * 512], ps[:, :], ACT.Copy), pt, link=False)

            kw = tmp[:, 544:800]
            dense("ev_in", (), [28], 8, xH, xL, tn,
                  lambda ps, j, n, pt: Q.a(lambda e: e.activation(kw, ps[:, 0:256], ACT.Copy), pt))
            t_kw = Q.last("act")
            by_token("ev_in", (), 24, yH, yL, [(0,), (1,)], tn, copy_to(qi))
            t_qi0 = Q.last("act")
            got = {}

            def tokens_of(name, j0, dst):
                yield from by_token_steps("ev_in", (), j0, yH, yL, [(0,), (1,)], tn, copy_to(dst))
                got[name] = Q.last("act")

            def conv():
                t0 = Q.v(lambda e: e.memset(u[:, :, 0:2], 0.0), link=False)
                t_zc = {}

                def take_zc(ps, j, n, pt):
                    t_zc[j] = Q.a(lambda e: e.activation(zc[:, j * 256:(j + n) * 256], ps[:, 0:n * 256], ACT.Copy), pt, link=False)
                    return t_zc[j]
                yield from dense_steps("ev_in", (), [4, 5, 6, 7], 8, xH, xL, tn, take_zc)

                def take_zh(ps, j, n, pt):
                    t = Q.v(lambda e: e.tensor_tensor(u[:, j:j + n, 2:258], ps[:, 0:n * 256].rearrange("p (k t) -> p k t", k=n),
                                                      zc[:, j * 256:(j + n) * 256].rearrange("p (k t) -> p k t", k=n), ALU.mult),
                            pt, t_zc[j], t0, link=False)
                    ys = [zz[:, i * 256:(i + 1) * 256] for i in range(j, j + n)]
                    ws = [sm("ev_conv", 3 * i, 3 * i + 3) for i in range(j, j + n)]
                    for i in range(n):
                        t1 = Q.a(lambda e: e.activation(ys[i], u[:, j + i, 0:256], ACT.Copy, scale=ws[i][:, 0:1]), t, link=False)
                    for tap in (1, 2):
                        for i in range(n):
                            Q.v(lambda e: e.scalar_tensor_tensor(ys[i], u[:, j + i, tap:tap + 256], ws[i][:, tap:tap + 1], ys[i],
                                                                 ALU.mult, ALU.add), t1)
                    return t
                yield from dense_steps("ev_in", (), [8, 9, 10, 11], 8, xH, xL, tn, take_zh)

                def take_zb(ps, j, n, pt):
                    z = zz[:, j * 256:(j + n) * 256].rearrange("p (k t) -> p k t", k=n)
                    t = Q.v(lambda e: e.tensor_tensor(z, ps[:, 0:n * 256].rearrange("p (k t) -> p k t", k=n), z, ALU.mult), pt)
                    got["conv"] = parts(mH[:, j:j + n, :], mL[:, j:j + n, :], z, (t,))
                    return t
                yield from dense_steps("ev_in", (), [0, 1, 2, 3], 8, xH, xL, tn, take_zb)

            jobs = [tokens_of("q", 12, q), tokens_of("k", 16, k), tokens_of("v", 20, vv), conv()]
            background.extend(jobs)

            def until(job):
                while job in background:
                    for _ in background.pop(0):
                        pass

            b, ps, bt = B.take()
            for t in range(2):
                Q.tr(ps[:, t * 128:(t + 1) * 128], kw[:, t * 128:(t + 1) * 128], ident, (bt, t_kw))
            pt = Q.pe_done()
            fill(1)
            key = ps[:, 0:256].rearrange("p (t n) -> p t n", t=2)
            kd2 = kid.rearrange("p (t n) -> p t n", t=2)
            kd = kd2[:, :, 0:64]
            two = lambda a, n: bc(a.unsqueeze(2), [128, 2, n])
            row = lambda name: bc(sm(name).unsqueeze(1), [128, 2, 64])
            Q.v(lambda e: e.tensor_reduce(mu, key[:, :, 0:64], AX.X, ALU.add), pt)
            Q.v(lambda e: e.tensor_scalar(wi.rearrange("p (t n) -> p t n", t=2), key[:, :, 64:72], float(8 ** -0.5 * 64 ** -0.5), None, ALU.mult), pt, link=False)
            Q.v(lambda e: e.tensor_scalar(mu, mu, 1.0 / 64, None, ALU.mult))
            tv = Q.v(lambda e: e.tensor_tensor(kd, key[:, :, 0:64], two(mu, 64), ALU.subtract))
            B.free(b, tv)
            t_ri = head_rstd(kd, tmp[:, 0:128].rearrange("p (t n) -> p t n", t=2), ri, 64, (tv,))
            Q.v(lambda e: e.tensor_tensor(kd, kd, two(ri, 64), ALU.mult), t_ri)
            Q.v(lambda e: e.tensor_tensor(kd, kd, row("ln_g"), ALU.mult))
            Q.v(lambda e: e.tensor_tensor(kd, kd, row("ln_b"), ALU.add))
            b2 = tmp[:, 128:192].rearrange("p (t f) -> p t f", t=2)
            turn(kd2[:, :, 0:32], b2, cI.rearrange("p (t f) -> p t f", t=2), sI.rearrange("p (t f) -> p t f", t=2),
                 lambda a: a, lambda a: (a[:, :, 0:16], a[:, :, 16:32]))
            tk = Q.v(lambda e: e.tensor_copy(kd2[:, :, 64:128], kd))
            z4 = th(qi)[:, :, :, 0:32]
            b4 = tmp[:, 0:512].rearrange("p (t h f) -> p t h f", t=2, h=8)
            wide = lambda a: bc(a.rearrange("p (t f) -> p t f", t=2).unsqueeze(2), [128, 2, 8, 32])
            Q.v(lambda e: e.memset(dummy, 0.0), t_qi0)
            tr_ = turn(z4, b4, wide(cI), wide(sI), lambda a: a, lambda a: (a[:, :, :, 0:16], a[:, :, :, 16:32]))
            fill(2)
            transpose4([kid[:, 0:128], kid[:, 128:256]], kiT.rearrange("p (i t) -> p i t", i=2), (tk,))
            t_ki = Q.last("act")
            fill(1)
            for t in range(2):
                t_qi = transpose4([qi[:, t * 512 + i * 128:t * 512 + (i + 1) * 128] for i in range(4)],
                                  qiT[:, :, t * 128:(t + 1) * 128], (tr_,))
            fill(1)

            t0 = Q.v(lambda e: e.memset(score, 0.0), link=False)
            relt = [t0, t0]
            cut = [slice(0, 128), slice(128, 384)]
            for h in range(8):
                b, ps, bt = B.take()
                o = (h % 2) * 64
                for t in range(2):
                    Q.mm(ps[:, cut[t]], qiT[o:o + 64, h // 2, t * 128:(t + 1) * 128], kiT[o:o + 64, 0:128 * (t + 1)], True, True,
                         (bt, t_qi, t_ki))
                rel = tmp[:, 512 * (h % 2):512 * (h % 2) + 384]
                ta = Q.a(lambda e: e.activation(rel, ps[:, 0:384], ACT.Relu), Q.pe_done(), relt[h % 2], link=False)
                B.free(b, ta)
                for t in range(2):
                    relt[h % 2] = Q.v(lambda e: e.scalar_tensor_tensor(
                        score[:, cut[t]], rel[:, cut[t]], wi[:, t * 8 + h:t * 8 + h + 1], score[:, cut[t]], ALU.mult, ALU.add), ta,
                        link=t == 0)
                if h % 3 == 2:
                    fill(1)
            mask_at = [slice(0, 128), slice(256, 384)]
            for t in range(2):
                Q.v(lambda e: e.tensor_tensor(score[:, mask_at[t]], score[:, mask_at[t]], sm("tri"), ALU.add), link=t == 0)

            def pick(n):
                for _ in range(n):
                    for t in range(2):
                        Q.v(lambda e: e.max(best[t], score[:, cut[t]]), link=t == 0)
                    for t in range(2):
                        Q.v(lambda e: e.match_replace(score[:, cut[t]], best[t], score[:, cut[t]], TAKEN), link=t == 0)

            pick(4)
            until(jobs[1])
            t_rq = head_rstd(heads(q), heads(tmp), rq, 64, (got["q"], Q.last("dve")), 0.125)
            wide2 = lambda a: bc(a.rearrange("p (t f) -> p t f", t=2).unsqueeze(2), [128, 2, 8, 64])
            t_q = turn(q, tmp, wide2(cqs[0]), wide2(cqs[1]), th, split64)
            t_rk = head_rstd(heads(k), heads(tmp), rk, 64, (got["k"], Q.last("dve")))
            fill(1)
            for t in range(2):
                t_qT = transpose4([q[:, t * 512 + i * 128:t * 512 + (i + 1) * 128] for i in range(4)],
                                  qTt[:, :, t * 128:(t + 1) * 128], (t_q,))
            Q.v(lambda e: e.tensor_tensor(heads(k), heads(k), bc(rk.unsqueeze(2), [128, 16, 64]), ALU.mult), t_rk)
            t_k = turn(k, tmp, wide2(cqs[2]), wide2(cqs[3]), th, split64)
            fill(2)
            for t in range(2):
                t_kT = transpose4([k[:, t * 512 + i * 128:t * 512 + (i + 1) * 128] for i in range(4)],
                                  kTt[:, :, t * 128:(t + 1) * 128], (t_k,))
            pick(4)
            Q.v(lambda e: e.tensor_scalar(bias, score, TAKEN, 1.0, ALU.is_equal, ALU.subtract))
            Q.v(lambda e: e.tensor_scalar(bias, bias, BIG, None, ALU.mult))
            for t in range(2):
                t_bias = Q.v(lambda e: e.tensor_tensor(bias[:, mask_at[t]], bias[:, mask_at[t]], sm("tri"), ALU.add), link=t == 0)

            p_free = [None, None]

            def weights(i):
                sv = soft[i % 2]
                pss = []
                for j in range(2):
                    b, ps, bt = B.take()
                    o = j * 64
                    for t in range(2):
                        Q.mm(ps[:, cut[t]], qTt[o:o + 64, i, t * 128:(t + 1) * 128], kTt[o:o + 64, i, 0:128 * (t + 1)], True, True,
                             (bt, t_qT, t_kT))
                    pss.append((b, ps, Q.pe_done()))
                pr = lambda j, t: P[i % 2][:, 384 * j + cut[t].start:384 * j + cut[t].stop]
                for j, (b, ps, pt) in enumerate(pss):
                    for t in range(2):
                        c = t * 8 + 2 * i + j
                        tv = Q.v(lambda e: e.scalar_tensor_tensor(pr(j, t), ps[:, cut[t]], rq[:, c:c + 1], bias[:, cut[t]], ALU.mult, ALU.add),
                                 pt, p_free[i % 2], t_rq, t_bias, link=False)
                    B.free(b, tv)
                for j in range(2):
                    for t in range(2):
                        Q.v(lambda e: e.tensor_reduce(sv[:, 2 * j + t:2 * j + t + 1], pr(j, t), AX.X, ALU.max), link=j + t == 0)
                tv = Q.v(lambda e: e.tensor_scalar(sv[:, 0:4], sv[:, 0:4], -1.0, None, ALU.mult))
                for j in range(2):
                    for t in range(2):
                        c = 2 * j + t
                        ta = Q.a(lambda e: e.activation(pr(j, t), pr(j, t), ACT.Exp, bias=sv[:, c:c + 1], accum_out=sv[:, 4 + c:5 + c]),
                                 tv, link=False)
                Q.v(lambda e: e.reciprocal(sv[:, 4:8], sv[:, 4:8]), ta)
                for j in range(2):
                    for t in range(2):
                        c = 4 + 2 * j + t
                        tv = Q.v(lambda e: e.tensor_scalar(pr(j, t), pr(j, t), sv[:, c:c + 1], None, ALU.mult), link=j + t == 0)
                return tv

            def values(i, tv):
                for j in range(2):
                    b, ps, bt = B.take()
                    for n in range(3):
                        Q.tr(ps[:, n * 128:(n + 1) * 128], P[i % 2][:, 384 * j + n * 128:384 * j + (n + 1) * 128], ident, (bt, tv))
                    p_free[i % 2] = Q.pe_done()
                    ta = Q.a(lambda e: e.activation(PT[i % 2][:, 384 * j:384 * (j + 1)], ps[:, 0:384], ACT.Copy), p_free[i % 2], link=False)
                    B.free(b, ta)
                fill(1)
                b, ps, bt = B.take()
                for n in range(2):
                    for j in range(2):
                        h = 2 * i + j
                        Q.mm(ps[64 * j:64 * j + 64, 128 * n:256], vv[:, n * 512 + h * 64:n * 512 + (h + 1) * 64],
                             PT[i % 2][:, 384 * j + 256 * n:384 * j + 256 + 128 * n], n == 0, n == 1, (bt, ta, got["v"]))
                _, tv = parts(mH[:, 4 + i, :], mL[:, 4 + i, :], ps[:, 0:256], (Q.pe_done(),))
                B.free(b, tv)

            fill(1)
            tv = weights(0)
            until(jobs[2])
            for i in range(4):
                fill(1)
                if i < 3:
                    after = weights(i + 1)
                    fill(1)
                values(i, tv)
                tv = after
            finish()
            dense("ev_out", (), list(range(8)), 8, lambda q: mH[:, q, :], lambda q: mL[:, q, :],
                  (Q.last("act"), Q.last("dve")), add_x)

        def ffn(ph, nH, nL, l):
            aH, aL = hl(ph, 22)
            sg = [open_area(ph, "sg", 512)[:, :] for _ in range(2)]
            at = [open_area(ph, "at", 512)[:, :] for _ in range(2)]
            tn = norm(x8, sm("norm_ffn", 8 * l, 8 * l + 8), None, tuple(lasts()), lambda k: nH[:, k, :], lambda k: nL[:, k, :], side=0, fills=1)
            xH = lambda q: nH[:, q, :]
            xL = lambda q: nL[:, q, :]
            n = [0, 0]
            gtok, utok = {}, {}

            def gate(ps, j, k, pt):
                s = sg[n[0] % 2]
                gtok[n[0]] = Q.a(lambda e: e.activation(s[:, 0:k * 256], ps[:, 0:k * 256], ACT.Silu), pt, utok.get(n[0] - 2))
                n[0] += 1
                return gtok[n[0] - 1]

            for j0 in range(0, 22, 4):
                js = list(range(j0, min(j0 + 4, 22)))
                dense("ffn_gate", (l,), js, 8, xH, xL, tn, gate)

                def up(ps, j, k, pt):
                    s = sg[n[1] % 2]
                    a = at[n[1] % 2][:, 0:k * 256]
                    t = Q.v(lambda e: e.tensor_tensor(a, ps[:, 0:k * 256], s[:, 0:k * 256], ALU.mult), pt, gtok[n[1]], utok.get(n[1] - 2))
                    a3 = a.rearrange("p (k t) -> p k t", k=k)
                    utok[n[1]] = parts(aH[:, j0 + j:j0 + j + k, :], aL[:, j0 + j:j0 + j + k, :], a3, (t,))[1]
                    n[1] += 1
                    return t
                dense("ffn_up", (l,), js, 8, xH, xL, tn, up)
            dense("ffn_down", (l,), list(range(8)), 22, lambda q: aH[:, q, :], lambda q: aL[:, q, :], tuple(lasts()), add_x)

        s_p = Q.new_sem("s_p")

        def ple(ph, nH, nL, l):
            er = open_area(ph, "er", 2048)[:, :].rearrange("p (k t) -> p k t", k=8)
            praw = open_area(ph, "praw", 512)
            pH, pL = hl(ph, 2)
            sg = [open_area(ph, "sg", 512)[:, :] for _ in range(2)]
            tp = Q.dma("pool", praw[:, :], dr["pT"][l], s_p, lasts())
            tp = parts(pH, pL, praw[:, :].rearrange("p (k t) -> p k t", k=2), (tp,) + tuple(lasts()))

            def take(ps, j, n, pt):
                return Q.a(lambda e: e.activation(er[:, j:j + n, :], ps[:, 0:n * 256].rearrange("p (k t) -> p k t", k=n), ACT.Copy), pt)
            background.append(dense_steps("ple_proj", (l,), list(range(8)), 2, lambda q: pH[:, q, :], lambda q: pL[:, q, :], tp, take))
            tn = norm(x8, sm("ple_norm", 8 * l, 8 * l + 8), None, tuple(lasts()), lambda k: nH[:, k, :], lambda k: nL[:, k, :], side=0, fills=2)
            finish()
            gate_steps = dense_steps("ple_gate", (l,), list(range(8)), 8, lambda q: nH[:, q, :], lambda q: nL[:, q, :], tn,
                                     lambda *a: take2(*a))
            next(gate_steps)
            norm(er, sm("ple_post", 8 * l, 8 * l + 8), None, tuple(lasts()), out=lambda k: er[:, k, :])
            i = [0]
            free = [None, None]

            def take2(ps, j, n, pt):
                k = i[0] % 2
                s = sg[k]
                i[0] += 1
                ta = Q.a(lambda e: e.activation(s, ps[:, 0:n * 256], ACT.Sigmoid), pt, free[k])
                sv = s.rearrange("p (k t) -> p k t", k=n)
                Q.v(lambda e: e.tensor_tensor(sv, sv, er[:, j:j + n, :], ALU.mult), ta)
                free[k] = Q.v(lambda e: e.tensor_tensor(x8[:, j:j + n, :], x8[:, j:j + n, :], sv, ALU.add))
                square(x8, j, n, free[k])
                return ta
            for _ in gate_steps:
                pass

        def odd(ph, nH, nL):
            open_area(ph, "sc", 14 * 1024)
            oH, oL = hl(ph, 8)
            S = lambda i: sc(i * 1024, 1024) if i < 14 else cT[:, (i - 14) * 1024:(i - 13) * 1024]
            gb = mi(16 * 3)
            gcu, beta, eg = gb[:, 0:16], gb[:, 16:32], gb[:, 32:48]
            gk = mi(32)
            glast, kd = gk[:, 0:16], gk[:, 16:32]
            EL = mi(32)
            ea = mi(8)
            gt = mi(48)
            rq = mi(8)
            rq2 = mi(8)
            be = mi(16)
            tn = norm(x8, sm("norm_mix", 8, 16), None, tuple(lasts()), lambda k: nH[:, k, :], lambda k: nL[:, k, :], side=0, fills=1)
            xH = lambda q: nH[:, q, :]
            xL = lambda q: nL[:, q, :]
            yH = lambda q, t: nH[:, q, t * 128:(t + 1) * 128]
            yL = lambda q, t: nL[:, q, t * 128:(t + 1) * 128]

            ab = S(12)[:, 0:256]
            dense("od_in", (), [32], 8, xH, xL, tn,
                  lambda ps, j, n, pt: Q.a(lambda e: e.activation(ab, ps[:, 0:256], ACT.Copy), pt))
            t_ab = Q.last("act")
            u = wk[:, 0:1036].rearrange("p (k t) -> p k t", k=4)
            Q.v(lambda e: e.memset(u[:, :, 0:3], 0.0), Q.pe_done())
            St = wk[:, 1536:2048]
            d4 = lambda a: a.rearrange("p (k t) -> p k t", k=4)
            places = [(0, 1, 2, 3, 7), (14, 15, 2, 3, 7)]
            def out_half(H, t_o):
                def add_half(ps, j, n, pt):
                    return Q.v(lambda e: e.tensor_tensor(x8[:, j:j + n, :], x8[:, j:j + n, :],
                                                         ps[:, 0:n * 256].rearrange("p (k t) -> p k t", k=n), ALU.add), pt, link=False)
                yield from dense_steps("od_out", (H,), list(range(8)), 4, lambda q: oH[:, 4 * H + q, :], lambda q: oL[:, 4 * H + q, :],
                                       t_o, add_x if H else add_half)

            t_z, t_cv = [None, None], [None, None]

            def project(H, what):
                qT, z, kT, vT = (S(i) for i in places[H][0:4])
                free = tuple(lasts())
                for base, dst in [((0, qT), (8, kT), (16, vT))[i] for i in what if i < 3]:
                    ufree = [Q.last("dve")]

                    def take(ps, j, n, pt, dst=dst, base=base):
                        ta = Q.a(lambda e: e.activation(u[:, j:j + n, 3:259], ps[:, 0:n * 256].rearrange("p (k t) -> p k t", k=n),
                                                        ACT.Copy), pt, ufree[0])
                        w = [sm("od_conv", 4 * (base + 4 * H + i), 4 * (base + 4 * H + i) + 4) for i in range(4)]
                        for i in range(j, j + n):
                            t0 = Q.a(lambda e: e.activation(d4(dst)[:, i, :], u[:, i, 0:256], ACT.Copy, scale=w[i][:, 0:1]), ta, *free)
                        for s in range(1, 4):
                            for i in range(j, j + n):
                                tv = Q.v(lambda e: e.scalar_tensor_tensor(
                                    d4(dst)[:, i, :], u[:, i, s:s + 256], w[i][:, s:s + 1], d4(dst)[:, i, :], ALU.mult, ALU.add), t0)
                        ufree[0] = tv
                        Q.a(lambda e, dst=dst, j=j, n=n: e.activation(d4(dst)[:, j:j + n, :], d4(dst)[:, j:j + n, :], ACT.Silu), tv)
                        return ta
                    yield from dense_steps("od_in", (), [base + 4 * H + i for i in range(4)], 8, xH, xL, tn, take)
                if 3 not in what:
                    t_cv[H] = Q.last("act")
                    return
                yield from by_token_steps("od_in", (), 24 + 4 * H, yH, yL, [(0,), (1,)], tn,
                                          lambda ps, pt, t: Q.a(lambda e: e.activation(z[:, t * 512:(t + 1) * 512], ps[:, :], ACT.Silu),
                                                                pt, *free))
                t_z[H] = Q.last("act")

            background.append(project(0, (0, 1, 2, 3)))
            t_ea = Q.a(lambda e: e.activation(ea, sm("a_log"), ACT.Exp))
            b, ps, bt = B.take()
            for t in range(2):
                Q.tr(ps[:, t * 128:(t + 1) * 128], ab[:, t * 128:(t + 1) * 128], ident, (bt, t_ab))
            pt = Q.pe_done()
            fill(1)
            g, a1, a2 = gt[:, 0:16], gt[:, 16:32], gt[:, 32:48]
            in2 = lambda a: a.rearrange("p (t n) -> p t n", t=2)
            gate = ps[:, 0:256].rearrange("p (t n) -> p t n", t=2)
            both = lambda a: bc(a.unsqueeze(1), [128, 2, 8])
            Q.v(lambda e: e.tensor_tensor(in2(g), gate[:, :, 0:8], both(sm("dt_bias")), ALU.add), pt)
            tb = Q.v(lambda e: e.tensor_scalar(in2(a2), gate[:, :, 8:16], -1.0, None, ALU.mult))
            B.free(b, tb)
            Q.v(lambda e: e.tensor_scalar(a1, g, -1.0, None, ALU.mult))
            tv = Q.v(lambda e: e.tensor_tensor(a1, a1, g, ALU.min))
            t_e = Q.a(lambda e: e.activation(a2, a2, ACT.Exp), tv)
            Q.a(lambda e: e.activation(a1, a1, ACT.Exp), tv)
            ta = Q.a(lambda e: e.activation(a1, a1, ACT.Ln, bias=1.0))
            Q.v(lambda e: e.tensor_scalar(a2, a2, 1.0, None, ALU.add), t_e)
            Q.v(lambda e: e.reciprocal(beta, a2))
            Q.v(lambda e: e.tensor_scalar(g, g, 0.0, None, ALU.max))
            Q.v(lambda e: e.tensor_tensor(g, g, a1, ALU.add), ta)
            Q.v(lambda e: e.tensor_scalar(g, g, -1.0, None, ALU.mult))
            t_g = Q.v(lambda e: e.tensor_tensor(in2(gcu), in2(g), both(ea), ALU.mult), t_ea)
            fill(1)
            b, ps, bt = B.take()
            Q.mm(ps[:, 0:16], sm("cumT"), gcu, True, True, (bt, t_g))
            t_g = Q.v(lambda e, ps=ps: e.tensor_copy(gcu, ps[:, 0:16]), Q.pe_done())
            B.free(b, t_g)
            fill(1)
            b, ps, bt = B.take()
            Q.mm(ps[:, 0:16], sm("lastT"), gcu, True, True, (bt, t_g))
            Q.mm(ps[:, 16:32], sm("sel", 0, 128), gcu, True, True)
            Q.mm(ps[:, 32:48], sm("sel", 128, 256), gcu, True, True)
            pt = Q.pe_done()
            t1 = Q.v(lambda e, ps=ps: e.tensor_tensor(kd, ps[:, 0:16], gcu, ALU.subtract), pt)
            Q.a(lambda e: e.activation(kd, kd, ACT.Exp), t1)
            ta = Q.a(lambda e, ps=ps: e.activation(EL, ps[:, 16:48], ACT.Exp), pt)
            B.free(b, ta)
            t_gates = Q.a(lambda e: e.activation(eg, gcu, ACT.Exp), t_g)
            Q.v(lambda e: e.tensor_tensor(be, beta, eg, ALU.mult), t_gates)

            def mix(H):
                qT, z, kT, vT, knT = (S(i) for i in places[H])
                rest = [i for i in range(16) if i not in places[H] and (H == 1 or i < 14)]
                K, kbg, V, MT, qkT, T, TT, Y, BT = (S(i) for i in rest[0:9])
                t_c = (t_z[H], t_cv[H])
                for t in range(2):
                    transpose4([d4(kT)[:, h, t * 128:(t + 1) * 128] for h in range(4)],
                               K[:, t * 512:(t + 1) * 512].rearrange("p (k t) -> p k t", k=4), (t_c,))
                    transpose4([d4(vT)[:, h, t * 128:(t + 1) * 128] for h in range(4)],
                               V[:, t * 512:(t + 1) * 512].rearrange("p (k t) -> p k t", k=4), (t_c,))
                fill(1)
                t_kv = Q.last("act")
                sq = Y
                tv = Q.a(lambda e: e.activation(sq, qT, ACT.Square), t_kv)
                b, ps, bt = B.take()
                for t in range(2):
                    for h in range(4):
                        Q.mm(ps[:, t * 4 + h:t * 4 + h + 1], d4(sq)[:, h, t * 128:(t + 1) * 128], ones[:, 0:1], True, True, (bt, tv))
                Q.v(lambda e, ps=ps: e.tensor_scalar(rq, ps[:, 0:8], EPS, None, ALU.add), Q.pe_done())
                B.free(b, Q.last("dve"))
                tp = power(rq)
                Q.v(lambda e: e.tensor_scalar(rq, rq, float(128 ** -0.5), None, ALU.mult), tp)
                gs = lambda a: a.rearrange("p (t h) -> p t h", t=2)[:, :, 4 * H:4 * H + 4]
                Q.v(lambda e: e.tensor_tensor(rq2.rearrange("p (t h) -> p t h", t=2), rq.rearrange("p (t h) -> p t h", t=2),
                                              gs(eg), ALU.mult), t_gates)
                k3 = K.rearrange("p (h d) -> p h d", h=8)
                head_norm(k3, BT.rearrange("p (h d) -> p h d", h=8), 8, 128, 1.0)
                t_kn = Q.last("dve")
                fill(1)
                for t in range(2):
                    transpose4([K[:, t * 512 + h * 128:t * 512 + (h + 1) * 128] for h in range(4)],
                               d4(knT)[:, :, t * 128:(t + 1) * 128], (t_kn,))
                t_knT = Q.last("act")
                for t in range(2):
                    for h in range(4):
                        tv = Q.v(lambda e, t=t, h=h: e.tensor_scalar(Y[:, h * 128:(h + 1) * 128], ident,
                                                                     gcu[:, 8 * t + 4 * H + h:8 * t + 4 * H + h + 1], None, ALU.mult),
                                 Q.last("pe"))
                    fill(1)
                    b, ps, bt = B.take()
                    Q.mm(ps[:, :], ones, Y[:, 0:512], True, False, (bt, tv))
                    Q.mm(ps[:, :].rearrange("p (h t) -> p h t", h=4), ident, bc(sm("dmask").unsqueeze(1), [128, 4, 128]), False, True)
                    pt = Q.pe_done()
                    for h in range(4):
                        ta = Q.a(lambda e, ps=ps, h=h, t=t: e.activation(
                            kT[:, t * 512 + h * 128:t * 512 + (h + 1) * 128], ps[:, h * 128:(h + 1) * 128], ACT.Exp,
                            bias=gcu[:, 8 * t + 4 * H + h:8 * t + 4 * H + h + 1], scale=-1.0), pt)
                    B.free(b, ta)
                    for kind in range(2):
                        b, ps, bt = B.take()
                        L = knT if kind == 0 else qT
                        for h in range(4):
                            Q.mm(ps[:, h * 128:(h + 1) * 128], d4(L)[:, h, t * 128:(t + 1) * 128],
                                 d4(knT)[:, h, t * 128:(t + 1) * 128], True, True, (bt, t_knT))
                        pt = Q.pe_done()
                        for h in range(4):
                            s_ = (beta[:, 8 * t + 4 * H + h:8 * t + 4 * H + h + 1] if kind == 0 else rq[:, 4 * t + h:4 * t + h + 1])
                            tv = Q.v(lambda e, ps=ps, h=h, t=t, s_=s_: e.scalar_tensor_tensor(
                                vT[:, h * 128:(h + 1) * 128], ps[:, h * 128:(h + 1) * 128], s_,
                                kT[:, t * 512 + h * 128:t * 512 + (h + 1) * 128], ALU.mult, ALU.mult), pt, ta, Q.last("pe"))
                        B.free(b, tv)
                        if kind == 0:
                            fill(1)
                        dst = MT if kind == 0 else qkT
                        transpose4([vT[:, h * 128:(h + 1) * 128] for h in range(4)],
                                   dst[:, t * 512:(t + 1) * 512].rearrange("p (k t) -> p k t", k=4), (tv,))
                t_MT = Q.last("act")
                if H == 0:
                    background.append(project(1, (1, 2)))
                fill(1)
                p8 = lambda a: a.rearrange("p (i t) -> p i t", i=8)
                lv = lambda l: bc(sm("levels", 128 * l, 128 * l + 128).unsqueeze(1), [128, 8, 128])
                Q.v(lambda e: e.tensor_tensor(p8(BT), p8(MT), lv(0), ALU.mult), t_MT)
                tv = Q.v(lambda e: e.tensor_tensor(p8(TT), bc(ident.unsqueeze(1), [128, 8, 128]), p8(BT), ALU.subtract))
                for t in range(2):
                    transpose4([TT[:, t * 512 + h * 128:t * 512 + (h + 1) * 128] for h in range(4)],
                               T[:, t * 512:(t + 1) * 512].rearrange("p (k t) -> p k t", k=4), (tv,))
                t_T = Q.last("act")
                scaled = []
                for dst, src, g in ((V, V, beta), (kbg, K, be), (K, K, kd)):
                    for t in range(2):
                        c = bc(g[:, 8 * t + 4 * H:8 * t + 4 * H + 4].unsqueeze(2), [128, 4, 128])
                        hv = lambda a, t=t: a[:, t * 512:(t + 1) * 512].rearrange("p (h d) -> p h d", h=4)
                        scaled.append(lambda hv=hv, c=c, dst=dst, src=src: Q.v(
                            lambda e: e.tensor_tensor(hv(dst), hv(src), c, ALU.mult), t_knT, t_gates))
                for l in range(1, 6):
                    tb = Q.v(lambda e, l=l: e.tensor_tensor(p8(BT), p8(MT), lv(l), ALU.mult), Q.last("pe"))
                    for t in range(2):
                        b, ps, bt = B.take()
                        for h in range(4):
                            i = t * 4 + h
                            Q.mm(ps[:, h * 128:(h + 1) * 128], p8(BT)[:, i, :], p8(T)[:, i, :], True, True, (bt, tb, t_T))
                        ta = Q.a(lambda e, ps=ps, t=t: e.activation(Y[:, t * 512:(t + 1) * 512], ps[:, :], ACT.Copy), Q.pe_done())
                        B.free(b, ta)
                    for f in scaled[0:2]:
                        f()
                    del scaled[0:2]
                    fill(1)
                    for t in range(2):
                        for kind in range(2):
                            if kind == 0 and l == 5:
                                continue
                            b, ps, bt = B.take()
                            for h in range(4):
                                i = t * 4 + h
                                if kind == 0:
                                    Q.mm(ps[:, h * 128:(h + 1) * 128], p8(TT)[:, i, :], p8(Y)[:, i, :], True, True, (bt, ta))
                                else:
                                    Q.mm(ps[:, h * 128:(h + 1) * 128], p8(Y)[:, i, :], p8(TT)[:, i, :], True, True, (bt, ta))
                            dst = (T if kind == 0 else TT)[:, t * 512:(t + 1) * 512]
                            tv = Q.v(lambda e, ps=ps, dst=dst: e.tensor_tensor(dst, dst, ps[:, :], ALU.subtract), Q.pe_done())
                            B.free(b, tv)
                    t_T = tv
                    fill(1)
                U, wT = V, kbg
                for t in range(2):
                    b, ps, bt = B.take()
                    for h in range(4):
                        i = t * 4 + h
                        Q.mm(ps[:, h * 128:(h + 1) * 128], p8(TT)[:, i, :], p8(V)[:, i, :], True, True, (bt, t_T))
                    ta = Q.a(lambda e, ps=ps, t=t: e.activation(U[:, t * 512:(t + 1) * 512], ps[:, :], ACT.Copy), Q.pe_done())
                    B.free(b, ta)
                    b, ps, bt = B.take()
                    for h in range(4):
                        i = t * 4 + h
                        Q.mm(ps[:, h * 128:(h + 1) * 128], p8(kbg)[:, i, :], p8(TT)[:, i, :], True, True, (bt, t_T))
                    ta = Q.a(lambda e, ps=ps, t=t: e.activation(wT[:, t * 512:(t + 1) * 512], ps[:, :], ACT.Copy), Q.pe_done())
                    B.free(b, ta)
                t_uw = ta
                O = T
                vn = Y
                t_s = None
                for n in range(4):
                    t, o = n // 2, 64 * (n % 2)
                    r = slice(o, o + 64)
                    vs = vn[r, t * 512:(t + 1) * 512]
                    us = U[r, t * 512:(t + 1) * 512]
                    if n == 0:
                        tvn = Q.v(lambda e, vs=vs, us=us: e.tensor_copy(vs, us), t_uw, Q.last("pe"))
                    else:
                        b, ps, bt = B.take()
                        for h in range(4):
                            i = t * 4 + h
                            Q.mm(ps[r, h * 128:(h + 1) * 128], p8(wT)[:, i, o:o + 64], St[:, h * 128:(h + 1) * 128], True, True,
                                 (bt, t_s, t_uw))
                        tvn = Q.v(lambda e, vs=vs, us=us, ps=ps, r=r: e.tensor_tensor(vs, us, ps[r, :], ALU.subtract), Q.pe_done())
                        B.free(b, tvn)
                    fill(1)
                    b, ps, bt = B.take()
                    for h in range(4):
                        i = t * 4 + h
                        Q.mm(ps[r, h * 128:(h + 1) * 128], p8(qkT)[r, i, o:o + 64], vn[r, t * 512 + h * 128:t * 512 + (h + 1) * 128],
                             True, True, (bt, tvn))
                    Os = O[r, t * 512:(t + 1) * 512]
                    ta = Q.a(lambda e, ps=ps, r=r, Os=Os: e.activation(Os, ps[r, :], ACT.Copy), Q.pe_done())
                    B.free(b, ta)
                    if n:
                        b, ps, bt = B.take()
                        for h in range(4):
                            Q.mm(ps[r, h * 128:(h + 1) * 128], d4(qT)[:, h, t * 128 + o:t * 128 + o + 64],
                                 St[:, h * 128:(h + 1) * 128], True, True, (bt, t_s))
                        pt = Q.pe_done()
                        for h in range(4):
                            tv = Q.v(lambda e, ps=ps, r=r, h=h, t=t: e.scalar_tensor_tensor(
                                O[r, t * 512 + h * 128:t * 512 + (h + 1) * 128], ps[r, h * 128:(h + 1) * 128],
                                rq2[r, 4 * t + h:4 * t + h + 1], O[r, t * 512 + h * 128:t * 512 + (h + 1) * 128],
                                ALU.mult, ALU.add), pt, ta)
                        B.free(b, tv)
                    if n < 3:
                        b, ps, bt = B.take()
                        for h in range(4):
                            i = t * 4 + h
                            Q.mm(ps[:, h * 128:(h + 1) * 128], p8(K)[r, i, :], vn[r, t * 512 + h * 128:t * 512 + (h + 1) * 128],
                                 True, True, (bt, tvn))
                        pt = Q.pe_done()
                        if n == 0:
                            t_s = Q.v(lambda e, ps=ps: e.tensor_copy(St, ps[:, :]), pt)
                        else:
                            for h in range(4):
                                el = EL[:, 16 * (n % 2) + 8 * t + 4 * H + h:16 * (n % 2) + 8 * t + 4 * H + h + 1]
                                t_s = Q.v(lambda e, ps=ps, h=h, el=el: e.scalar_tensor_tensor(
                                    St[:, h * 128:(h + 1) * 128], St[:, h * 128:(h + 1) * 128], el,
                                    ps[:, h * 128:(h + 1) * 128], ALU.mult, ALU.add), pt)
                        B.free(b, t_s)
                o3 = O.rearrange("p (h d) -> p h d", h=8)
                head_norm(o3, BT.rearrange("p (h d) -> p h d", h=8), 8, 128, tok=(Q.last("act"),))
                Q.v(lambda e: e.tensor_tensor(o3, o3, bc(sm("o_g").unsqueeze(1), [128, 8, 128]), ALU.mult))
                tv = Q.v(lambda e: e.tensor_tensor(O, O, z, ALU.mult))
                fill(2)
                for t in range(2):
                    b, ps, bt = B.take()
                    for h in range(4):
                        Q.tr(ps[:, h * 128:(h + 1) * 128], O[:, t * 512 + h * 128:t * 512 + (h + 1) * 128], ident, (bt, tv))
                    t_o = parts(oH[:, 4 * H:4 * H + 4, t * 128:(t + 1) * 128], oL[:, 4 * H:4 * H + 4, t * 128:(t + 1) * 128],
                                ps[:, :].rearrange("p (k t) -> p k t", k=4), (Q.pe_done(),))
                    B.free(b, t_o[1])
                return t_o

            finish()
            background.append(project(1, (0, 3)))
            t_o = mix(0)
            finish()
            background.append(out_half(0, t_o))
            t_o = mix(1)
            finish()
            for _ in out_half(1, t_o):
                pass

        mods = [mi(96), mi(96)]
        s1 = mi(32)

        c_pad = mi(256)
        c2 = c_pad.rearrange("p (k n) -> p k n", k=8)
        ada_n = [0]
        ada_late = []

        def ada_step():
            i = ada_n[0]
            if i >= 24:
                if ada_late:
                    ada_late.pop()()
                return
            ada_n[0] += 1
            if i == 0:
                Q.v(lambda e: e.memset(c2, 0.0))
                ada_t.append(Q.a(lambda e: e.activation(c2[:, :, 0:2], sm("c2").rearrange("p (k s) -> p k s", k=8), ACT.Silu),
                                 Q.last("dve"), t_in))
            l, c4 = i // 12, i % 12
            c = W.ask("ada", (l,), 4 * c4, 4, 8, "raw")
            ap, tok = c.raw()
            w = ap.rearrange("p (j k n) -> p j k n", j=4, k=8)
            b, ps, bt = B.take()
            for k in range(2):
                for g in range(4):
                    Q.mm(ps[32 * g:32 * g + 32, :].rearrange("p (j n) -> p j n", j=4), c2[:, 2 * g + k, :], w[:, :, 2 * g + k, :],
                         k == 0, k == 1, (tok, bt, ada_t[0]))
            pt = Q.pe_done()
            c.done(pt)
            if ada_late:
                ada_late.pop()()
            ta = Q.a(lambda e: e.activation(adaT[:, :], ps[:, :], ACT.Copy), pt, Q.last("pe"))
            B.free(b, ta)

            def late():
                b, ps, bt = B.take()
                for j in range(4):
                    Q.tr(ps[:, j * 128:(j + 1) * 128], adaT[:, j * 128:(j + 1) * 128], ident, (bt, ta))
                m = mods[l].rearrange("p (j s) -> p j s", j=48)[:, 4 * c4:4 * c4 + 4, :]
                for s in range(2):
                    v = ps[:, :].rearrange("p (j g n) -> p j g n", j=4, g=4)[:, :, :, s]
                    Q.v(lambda e: e.tensor_reduce(m[:, :, s], v, AX.X, ALU.add), Q.pe_done())
                B.free(b, Q.last("dve"))
                Q.v(lambda e: e.tensor_tensor(m, m, bc(sm("ada_b", 48 * l + 4 * c4, 48 * l + 4 * c4 + 4).unsqueeze(2), [128, 4, 2]), ALU.add))
            ada_late.append(late)
        ada_t = []

        def mod(l, which, side):
            return mods[l].rearrange("p (w k s) -> p w s k", w=6, k=8)[:, which, side, :]

        s_c = Q.new_sem("s_c")
        s_k = Q.new_sem("s_k")
        s_cT = Q.new_sem("s_cT")

        def scales(l, which_g, which_m, side):
            g = sm(which_g, 8 * l, 8 * l + 8)
            dst = s1[:, 8 * side:8 * side + 8]
            Q.v(lambda e: e.tensor_scalar(dst, mod(l, which_m, side), 1.0, None, ALU.add))
            Q.v(lambda e: e.tensor_tensor(dst, dst, g, ALU.mult))
            return dst

        def both_stats(order):
            room = [rr[:, 0:256], small[:, OFF["sel"][0]:OFF["sel"][0] + 256]]
            return {side: norm_stats([x8, c8][side], tuple(lasts()) + (t_ctx,), side, room[side]) for side in order}

        def mixer2(ph, l):
            open_area(ph, "sc", 13568)
            nH, nL = hl(ph, 8, 2)
            CS = sc(0, 1024).rearrange("p (k t) -> p k t", k=2)
            BD = sc(1024, 256)
            fp = sc(1280, 2048).rearrange("p (s t f) -> p s t f", s=2, t=2)
            kv = sc(3328, 2048).rearrange("p (s t f) -> p s t f", s=2, t=2)
            qq = sc(5376, 2048).rearrange("p (s f) -> p s f", s=2)
            kTt = sc(7424, 1024).rearrange("p (h t) -> p h t", h=2)
            PT = [sc(8448, 1024), sc(9472, 1024)]
            P = [sc(10496, 1024), sc(11520, 1024)]
            tmp = sc(12544, 1024)
            fH = open_area(ph, "fH", 512, F32R)
            fL = open_area(ph, "fL", 512, F32R)
            src = [x8, c8]
            nside = 2 if l == 0 else 1
            t_const = Q.dma("pool", sc(0, 1280), dr["dft"], s_c, lasts() + [t_ctx])
            st = c_pad
            rk, rq, soft = st[:, 0:8], [st[:, 8:16], st[:, 16:24]], [st[:, 24:28], st[:, 28:32]]
            rqn = [st[:, 32:40], st[:, 40:48]]
            tn = ()
            gains = [scales(l, "n1", 1, side) for side in range(2)]
            stats = both_stats((1, 0))
            for side in (1, 0):
                dst = gains[side]
                tn += norm(src[side], dst, mod(l, 0, side), (t_ctx,) + tuple(lasts()),
                           lambda k: nH[:, k, side, :], lambda k: nL[:, k, side, :], side=side, stats=stats[side],
                           room=sc(8448, 2048).rearrange("p (k t) -> p k t", k=8) if side else wk8)
            t_pool = Q.dma("pool", wk[:, :], dr["poolA"], s_k, lasts())
            PA = wk[:, :].rearrange("p (g k t) -> p g k t", g=4, k=2)
            tabs = [small[:, OFF["levels"][0] + 512:OFF["levels"][0] + 768], small[:, OFF["levels"][0] + 768:OFF["levels"][0] + 1024], adaT[:, 0:256], adaT[:, 256:512]]
            for i in range(4):
                g = sm("kg" if i > 1 else "qg", 128 * l, 128 * l + 128)
                two = lambda a: a.rearrange("p (t f) -> p t f", t=2)
                Q.v(lambda e: e.tensor_tensor(two(tabs[i]), two(sm("rsin" if i % 2 else "rcos")), bc(g.unsqueeze(1), [128, 2, 128]), ALU.mult),
                    Q.last("pe"), link=False)
            yH = lambda q, s, t: nH[:, q, s, t * 128:(t + 1) * 128]
            yL = lambda q, s, t: nL[:, q, s, t * 128:(t + 1) * 128]
            some = [(s, t) for s in range(nside) for t in range(2)]
            both = [(s, t) for s in range(2) for t in range(2)]
            got = {}
            by_token("w_in", (l,), 8, yH, yL, both, tn,
                     lambda ps, pt, s, t: Q.a(lambda e: e.activation(kv[:, s, t, :], ps[:, :], ACT.Copy), pt, link=False))
            t_kv = Q.last("act")

            def tokens_of(name, j0, view):
                yield from by_token_steps("w_in", (l,), j0, yH, yL, some, tn, lambda ps, pt, s, t: Q.a(
                    lambda e: e.activation(view(s, t), ps[:, :], ACT.Copy), pt, link=False))
                got[name] = Q.last("act")

            jobs = [tokens_of("q", 4, lambda s, t: qq[:, s, t * 512:(t + 1) * 512]), tokens_of("fp", 0, lambda s, t: fp[:, s, t, :])]
            background.extend(jobs)
            mH, mL = nH, nL
            halves = lambda a: [a.rearrange("p (n x f) -> p n x f", x=2, f=32)[:, :, i, :] for i in range(2)]

            def table(i, heads):
                return bc(tabs[i].rearrange("p (t f) -> p t f", t=2).unsqueeze(2), [128, 2, heads, 128])

            kk = kv.rearrange("p s t f -> p (s t) f")[:, :, 0:256]
            t4_ = tmp.rearrange("p (n f) -> p n f", n=4)
            ta = Q.a(lambda e: e.activation(t4_, kk, ACT.Square), t_kv)
            Q.v(lambda e: e.tensor_reduce(rk, tmp.rearrange("p (n f) -> p n f", n=8), AX.X, ALU.add), ta)
            Q.v(lambda e: e.tensor_scalar(rk, rk, 1.0 / 128, EPS, ALU.mult, ALU.add))
            t_rk = power(rk)
            fill(1)
            kh = lambda a, s: a[:, s * 512:(s + 1) * 512].rearrange("p (t h d) -> p t h d", t=2, h=2)
            for s in range(2):
                for h in range(2):
                    kin = kv[:, s, :, h * 128:(h + 1) * 128]
                    r_ = bc(rk[:, 4 * s:4 * s + 4].rearrange("p (t h) -> p t h", t=2)[:, :, h:h + 1], [128, 2, 128])
                    tv = Q.v(lambda e: e.tensor_tensor(kh(tmp, s)[:, :, h, :], kin, r_, ALU.mult), t_rk, link=False)
            rot = P[0][:, 0:512]
            turn(tmp[:, 0:512], rot, table(2, 2), table(3, 2), lambda a: a.rearrange("p (t h d) -> p t h d", t=2, h=2), halves)
            tv = Q.v(lambda e: e.tensor_tensor(kh(tmp, 1), kh(tmp, 1), bc(sm("kg", 128 * l, 128 * l + 128).unsqueeze(1).unsqueeze(1), [128, 2, 2, 128]), ALU.mult))
            fill(1)
            for s in range(2):
                t_kT = transpose4([tmp[:, s * 512 + t * 256 + h * 128:s * 512 + t * 256 + (h + 1) * 128] for h in range(2) for t in range(2)],
                                  kTt[:, :, s * 256:(s + 1) * 256], (tv,))
            while jobs[0] in background:
                fill(1)
            for s in range(nside):
                z = qq[:, s, :]
                z8 = z.rearrange("p (n d) -> p n d", n=8)
                z4 = lambda a: a.rearrange("p (t h d) -> p t h d", t=2, h=4)
                t_rq = head_rstd(z8, tmp.rearrange("p (n d) -> p n d", n=8), rq[s], 128, (got["q"], Q.last("dve"), Q.last("pe")), float(128 ** -0.5))
                t_rq = Q.v(lambda e: e.tensor_scalar(rqn[s], rq[s], -1.0, None, ALU.mult))
                if s == 0:
                    tv = turn(z, tmp, table(0, 4), table(1, 4), z4, halves)
                else:
                    tv = Q.v(lambda e: e.tensor_tensor(z8, z8, bc(sm("qg", 128 * l, 128 * l + 128).unsqueeze(1), [128, 8, 128]), ALU.mult))
                fill(1)
                held = []
                for t in range(2):
                    b, ps, bt = B.take()
                    for h in range(4):
                        Q.tr(ps[:, h * 128:(h + 1) * 128], z[:, t * 512 + h * 128:t * 512 + (h + 1) * 128], ident, (bt, tv))
                    held.append((b, ps))
                pt = Q.pe_done()
                for t, (b, ps) in enumerate(held):
                    t_qT = Q.a(lambda e: e.activation(z.rearrange("p (h t) -> p h t", h=4)[:, :, t * 128:(t + 1) * 128],
                                                      ps[:, :].rearrange("p (h t) -> p h t", h=4), ACT.Copy), pt, link=False)
                    B.free(b, t_qT)
            finish()
            t_n = Q.pe_done()
            t_fp = got["fp"]
            pq = [tmp[:, 0:512], tmp[:, 512:1024]]
            fr = [x[:, :].rearrange("p (k t) -> p k t", k=2) for x in (fH, fL)]

            def fourier_pool(s):
                free = tuple(lasts())
                for f in range(2):
                    b, ps, bt = B.take()
                    for t in range(2):
                        Q.mm(ps[:, :], fp[:, s, t, f * 128:(f + 1) * 128], CS[:, t, :], t == 0, t == 1, (bt, t_fp, t_const))
                    ta = Q.a(lambda e: e.activation(pq[f], ps[:, :], ACT.Copy), Q.pe_done(), *free, link=False)
                    B.free(b, ta)
                    yield
                b, ps, bt = B.take()
                for f in range(2):
                    for k in range(2):
                        Q.mm(ps[:, f * 256:(f + 1) * 256], BD[:, k * 128:(k + 1) * 128], pq[f][:, k * 256:(k + 1) * 256], k == 0, k == 1,
                             (bt, ta))
                t_fr = parts(fH[:, :], fL[:, :], ps[:, :], (Q.pe_done(),))
                t_pq = Q.pe_done()
                B.free(b, t_fr[1])
                yield
                b, ps, bt = B.take()
                for t in range(2):
                    for g in range(4):
                        o = 64 * (g % 2)
                        Q.mm(ps[o:o + 64, (g // 2) * 256:(g // 2 + 1) * 256], fp[:, s, t, 256 + g * 64:256 + (g + 1) * 64],
                             PA[:, g, t, :], t == 0 and g < 2, t == 1, (bt, t_pool, t_fp), True)
                dp = pq[0]
                tv = Q.v(lambda e: e.tensor_copy(dp, ps[:, :]), Q.pe_done(), t_pq)
                B.free(b, tv)
                yield

                def take_f(ps, j, n, pt):
                    return parts(mH[:, 0:2, s, :], mL[:, 0:2, s, :], ps[:, :].rearrange("p (k t) -> p k t", k=2), (pt, t_n))[1]
                yield from dense_steps("w_four", (l,), [0, 1], 2, lambda q: fr[0][:, q, :], lambda q: fr[1][:, q, :], t_fr, take_f)
                b, ps, bt = B.take()
                for g in range(4):
                    o = 64 * (g % 2)
                    wp = sm("w_pool", 128 * l + 64 * (g // 2), 128 * l + 64 * (g // 2) + 64)
                    Q.mm(ps[o:o + 64, (g // 2) * 256:(g // 2 + 1) * 256], wp[o:o + 64, :], dp[o:o + 64, (g // 2) * 256:(g // 2 + 1) * 256],
                         True, True, (bt, tv))
                pt = Q.pe_done()
                for k in range(2):
                    tv = Q.v(lambda e: e.tensor_scalar(pq[1][:, k * 256:(k + 1) * 256], ps[:, k * 256:(k + 1) * 256],
                                                       sm("pool_scale", 2 * l + k, 2 * l + k + 1), None, ALU.mult), pt, t_pq)
                B.free(b, tv)
                parts(mH[:, 2:4, s, :], mL[:, 2:4, s, :], pq[1].rearrange("p (k t) -> p k t", k=2), (tv, t_n))
                yield

            background.extend(fourier_pool(s) for s in range(nside))

            p_free, pt_free = [None, None], [None, None]

            def weights(n, s, h):
                nk = 512 if s == 0 else 256
                k0 = 512 - nk
                sv = soft[n % 2]
                ht = lambda a: a[s].rearrange("p (t h) -> p h t", t=2)[:, h, :]
                pss = []
                for t in range(2):
                    b, ps, bt = B.take()
                    Q.mm(ps[:, 0:nk], qq[:, s, h * 256 + t * 128:h * 256 + (t + 1) * 128], kTt[:, h // 2, k0:k0 + nk], True, True,
                         (bt, t_qT, t_kT))
                    pss.append((b, ps, Q.pe_done()))
                for t, (b, ps, pt) in enumerate(pss):
                    Q.v(lambda e: e.tensor_reduce(sv[:, t:t + 1], ps[:, 0:nk], AX.X, ALU.max), pt, link=t == 0)
                tv = Q.v(lambda e: e.tensor_tensor(sv[:, 0:2], sv[:, 0:2], ht(rqn), ALU.mult))
                for t, (b, ps, pt) in enumerate(pss):
                    p = P[n % 2][:, t * 512:t * 512 + nk]
                    ta = Q.a(lambda e: e.activation(p, ps[:, 0:nk], ACT.Exp, bias=sv[:, t:t + 1], scale=rq[s][:, t * 4 + h:t * 4 + h + 1],
                                                    accum_out=sv[:, 2 + t:3 + t]), tv, p_free[n % 2], link=False)
                    B.free(b, ta)
                Q.v(lambda e: e.reciprocal(sv[:, 2:4], sv[:, 2:4]), ta)
                for t in range(2):
                    p = P[n % 2][:, t * 512:t * 512 + nk]
                    tv = Q.v(lambda e: e.tensor_scalar(p, p, sv[:, 2 + t:3 + t], None, ALU.mult), link=t == 0)
                return tv

            def values(n, s, h, tv):
                nk = 512 if s == 0 else 256
                kn, k0 = nk // 128, 512 - nk
                pt_ = PT[n % 2].rearrange("p (k t) -> p k t", k=4)
                for t in range(2):
                    b, ps, bt = B.take()
                    for k in range(kn):
                        Q.tr(ps[:, k * 128:(k + 1) * 128], P[n % 2][:, t * 512 + k * 128:t * 512 + (k + 1) * 128], ident, (bt, tv))
                    p_free[n % 2] = Q.pe_done()
                    ta = Q.a(lambda e: e.activation(pt_[:, 0:kn, t * 128:(t + 1) * 128], ps[:, 0:nk].rearrange("p (k t) -> p k t", k=kn),
                                                    ACT.Copy), p_free[n % 2], pt_free[n % 2], link=False)
                    B.free(b, ta)
                fill(1)
                b, ps, bt = B.take()
                for k in range(kn):
                    kt = k0 // 128 + k
                    Q.mm(ps[:, 0:256], kv[:, kt // 2, kt % 2, 256 + (h // 2) * 128:256 + (h // 2 + 1) * 128], pt_[:, k, :],
                         k == 0, k == kn - 1, (bt, ta, t_kv))
                pt_free[n % 2] = Q.pe_done()
                _, tv = parts(mH[:, 4 + h, s, :], mL[:, 4 + h, s, :], ps[:, 0:256], (Q.pe_done(), t_n))
                B.free(b, tv)

            units = [(s, h) for h in range(4) for s in range(nside)]
            tv = weights(0, *units[0])
            fill(1)
            for n, (s, h) in enumerate(units):
                if n + 1 < len(units):
                    after = weights(n + 1, *units[n + 1])
                values(n, s, h, tv)
                tv = after
            finish()


            def take(ps, j, n, pt):
                for s in range(nside):
                    t = Q.v(lambda e: e.scalar_tensor_tensor(src[s][:, j, :], ps[:, s * 256:(s + 1) * 256], mod(l, 2, s)[:, j:j + 1],
                                                             src[s][:, j, :], ALU.mult, ALU.add), pt, link=False)
                    square(src[s], j, 1, t, s)
                return t
            dense("w_out", (l,), list(range(8)), 8, lambda q: mH[:, q, 0:nside, :], lambda q: mL[:, q, 0:nside, :],
                  tuple(lasts()), take, width=256 * nside, per=1)

        def lasts():
            return [Q.last("dve"), Q.last("act"), Q.pe_done()]

        def moe(ph, l):
            open_area(ph, "sc", 11376)
            nT = open_area(ph, "nT", 4096)
            n2 = nT[:, :].rearrange("p (k s t) -> p k s t", k=8, s=2)
            more = open_area(ph, "more", (MORE - 1) * SLOT)
            if not dry:
                for i in range(MORE - 1):
                    W.idle.append(Slot(more[:, i * SLOT:(i + 1) * SLOT], f"slot{RING + i}", tuple(lasts())))
            routing = ExitStack()
            rowsH = open_area(routing, "rowsH", 2048, F32R)[:, :].rearrange("p (t f) -> p t f", t=2)
            rowsL = open_area(routing, "rowsL", 2048, F32R)[:, :].rearrange("p (t f) -> p t f", t=2)
            P = open_area(routing, "P", 1024, F32R)[:, :]
            nside = 2 if l == 0 else 1
            src = [x8, c8]
            w = 32 * nside
            xs = sc(0, 128 * w).rearrange("p (k e s n) -> p k e s n", k=8, e=16, s=nside)
            PgT = sc(8192, 2048).rearrange("p (s i t) -> p s i t", s=2, i=4)
            Pg = sc(10240, 1024)
            aff = sc(11264, 32)
            affT = adaT[:, 0:256]
            msk = adaT[:, 256:512]
            cs = c_pad
            sl = sc(11296, 32)
            lg = sc(11328, 32)
            st = sc(11360, 16)
            gat = [nT[:, 0:512], nT[:, 512:1024]]
            hid = [nT[:, 1024:1536], nT[:, 1536:2048]]
            aT = [nT[:, 2048:2560], nT[:, 2560:3072]]
            tn = []
            gains = [scales(l, "n2", 4, side) for side in range(nside)]
            stats = both_stats(range(nside))
            for side in range(nside):
                dst = gains[side]
                tn.append(norm(src[side], dst, mod(l, 3, side), tuple(lasts()), out=lambda k: n2[:, k, side, :], side=side, stats=stats[side]))
            wr = sm("w_router", 128 * l, 128 * l + 128).rearrange("p (k n) -> p k n", k=8)
            own = small[:, OFF["levels"][0]:OFF["levels"][0] + 1024]
            sides = [(aff, affT, msk, cs, sl, lg, st), (own[:, 0:32], own[:, 256:512], own[:, 512:768], own[:, 768:1024],
                                                        own[:, 32:64], own[:, 64:96], own[:, 96:112])]
            chosen = {}

            def choose(side):
                aff, affT, msk, cs, sl, lg, st = sides[side]
                b, ps, bt = B.take()
                for k in range(2):
                    for g in range(4):
                        Q.mm(ps[32 * g:32 * g + 16, 0:256], wr[:, 2 * g + k, :], n2[:, 2 * g + k, side, :], k == 0, k == 1,
                             (bt,) + tn[side])
                L3, A3 = (a.rearrange("p (t n) -> p t n", t=2) for a in (lg, aff))
                pt = Q.pe_done()
                tz = Q.v(lambda e: e.memset(affT, 0.0), Q.last("act"))
                for g in range(4):
                    r = slice(32 * g, 32 * g + 16)
                    if g % 2:
                        t1 = Q.v(lambda e: e.tensor_copy(affT[r, :], ps[r, 0:256]), pt, tz, link=False)
                    else:
                        t0 = Q.a(lambda e: e.activation(affT[r, :], ps[r, 0:256], ACT.Copy), pt, tz, link=False)
                B.free(b, (t0, t1))
                yield
                b, ps, bt = B.take()
                for t in range(2):
                    Q.tr(ps[:, t * 128:(t + 1) * 128], affT[:, t * 128:(t + 1) * 128], ident, (bt, t0, t1))
                Q.v(lambda e: e.tensor_reduce(L3, ps[:, 0:256].rearrange("p (t g n) -> p t n g", t=2, g=4)[:, :, 0:16, :], AX.X, ALU.add),
                    Q.pe_done())
                B.free(b, Q.last("dve"))
                yield
                Q.v(lambda e: e.tensor_reduce(st[:, 0:2], L3, AX.X, ALU.max))
                tv = Q.v(lambda e: e.tensor_scalar(st[:, 0:2], st[:, 0:2], -1.0, None, ALU.mult))
                yield
                for t in range(2):
                    ta = Q.a(lambda e: e.activation(A3[:, t, :], L3[:, t, :], ACT.Exp, bias=st[:, t:t + 1], accum_out=st[:, 2 + t:3 + t]), tv, link=False)
                yield
                Q.v(lambda e: e.reciprocal(st[:, 2:4], st[:, 2:4]), ta)
                tv = Q.v(lambda e: e.tensor_tensor(A3, A3, bc(st[:, 2:4].unsqueeze(2), [128, 2, 16]), ALU.mult))
                yield
                b, ps, bt = B.take()
                for t in range(2):
                    Q.tr(ps[0:16, t * 128:(t + 1) * 128], aff[:, 16 * t:16 * t + 16], ident, (bt, tv))
                Q.v(lambda e: e.tensor_copy(affT[0:16, :], ps[0:16, 0:256]), Q.pe_done())
                B.free(b, Q.last("dve"))
                for _ in range(CAP // 8):
                    yield
                    Q.v(lambda e: e.max(st[0:16, 8:16], affT[0:16, :]))
                    yield
                    Q.v(lambda e: e.match_replace(affT[0:16, :], st[0:16, 8:16], affT[0:16, :], -1.0))
                yield
                Q.v(lambda e: e.tensor_scalar(msk[0:16, :], affT[0:16, :], -1.0, None, ALU.is_equal))
                yield
                Q.v(lambda e: e.tensor_tensor_scan(cs[0:16, :], bc(ones[0:16, 0:1], [16, 256]), msk[0:16, :], 0.0, ALU.mult, ALU.add))
                yield
                Q.v(lambda e: e.tensor_tensor(cs[0:16, :], cs[0:16, :], msk[0:16, :], ALU.mult))
                yield
                tv = Q.v(lambda e: e.tensor_scalar(cs[0:16, :], cs[0:16, :], -1.0, None, ALU.add))
                yield
                b, ps, bt = B.take()
                for t in range(2):
                    Q.tr(ps[:, t * 16:(t + 1) * 16], cs[0:16, t * 128:(t + 1) * 128], ident[0:16, 0:16], (bt, tv))
                chosen[side] = Q.v(lambda e: e.tensor_copy(sl, ps[:, 0:32]), Q.pe_done())
                B.free(b, chosen[side])

            def by_rows(side):
                held = []
                for t in range(2):
                    for hf in range(2):
                        b, ps, bt = B.take()
                        for i in range(4):
                            Q.tr(ps[:, i * 128:(i + 1) * 128], n2[:, hf * 4 + i, side, t * 128:(t + 1) * 128], ident, (bt,) + tn[side])
                        held.append((b, ps, Q.pe_done()))
                for n, (b, ps, pt) in enumerate(held):
                    t, hf = n // 2, n % 2
                    H, Lo = (a[:, t, hf * 512:(hf + 1) * 512] for a in (rowsH, rowsL))
                    ta = Q.a(lambda e: e.activation(H, ps[:, :], ACT.Copy), pt, rows_free[0], link=False)
                    tv = Q.v(lambda e: e.tensor_tensor(Lo, ps[:, :], H.bitcast(F32), ALU.subtract), ta, rows_free[0], link=False)
                    B.free(b, tv)
                return tv

            def one_hot(side):
                aff, sl = sides[side][0], sides[side][4]
                for t in range(2):
                    pv = P[:, t * 512:(t + 1) * 512].rearrange("p (e j) -> p e j", e=16)
                    Q.v(lambda e: e.tensor_tensor(pv, bc(sm("iota").unsqueeze(1), [128, 16, 32]),
                                                  bc(sl[:, 16 * t:16 * t + 16].unsqueeze(2), [128, 16, 32]), ALU.is_equal),
                        rows_free[0], chosen[side], link=False)
                t_P = Q.last("dve")
                for t in range(2):
                    pv = P[:, t * 512:(t + 1) * 512].rearrange("p (e j) -> p e j", e=16)
                    pg = Pg[:, t * 512:(t + 1) * 512].rearrange("p (e j) -> p e j", e=16)
                    tv = Q.v(lambda e: e.tensor_tensor(pg, pv.bitcast(F32), bc(aff[:, 16 * t:16 * t + 16].unsqueeze(2), [128, 16, 32]), ALU.mult),
                             rows_free[0], link=t == 0)
                return t_P, tv

            def gather(side, t_h, t_P):
                for k in range(8):
                    b, ps, bt = B.take()
                    for t in range(2):
                        p = P[:, t * 512:(t + 1) * 512]
                        Q.mm(ps[:, :], rowsH[:, t, k * 128:(k + 1) * 128], p, t == 0, False, (bt, t_h, t_P))
                        Q.mm(ps[:, :], rowsL[:, t, k * 128:(k + 1) * 128], p, False, t == 1)
                    xv = ps[:, :].rearrange("p (e n) -> p e n", e=16)
                    if k % 2:
                        tx = Q.a(lambda e: e.activation(xs[:, k, :, side, :], xv, ACT.Copy), Q.pe_done(), link=False)
                    else:
                        tx = Q.v(lambda e: e.tensor_copy(xs[:, k, :, side, :], xv), Q.pe_done(), link=False)
                    B.free(b, tx)

            rows_free = [None]
            steps_ = [choose(side) for side in range(nside)]
            for n in range(3):
                for c in steps_:
                    next(c)
            t_h = by_rows(0)
            while steps_:
                for c in list(steps_):
                    if next(c, "end") == "end":
                        steps_.remove(c)
            for side in range(nside):
                if side:
                    t_h = by_rows(side)
                t_P, tv = one_hot(side)
                for t in range(2):
                    transpose4([Pg[:, t * 512 + i * 128:t * 512 + (i + 1) * 128] for i in range(4)],
                               PgT[:, side, :, t * 128:(t + 1) * 128], (tv,))
                gather(side, t_h, t_P)
                rows_free[0] = Q.pe_done()
            routing.close()
            last_slot = open_area(ph, "last_slot", SLOT)[:, :]
            Y = [Pg, open_area(ph, "Y", 1024)[:, :]]
            if not dry:
                W.idle.append(Slot(last_slot, f"slot{RING + MORE - 1}", tuple(lasts())))
            y_free[0] = tuple(lasts())
            tx = tuple(lasts())
            free_a = [None, None]
            for e_ in range(NE):
                i2, i4 = e_ % 2, e_ % 4
                cs_ = [W.ask(n, (l, e_), j, 4, 8, "raw") for n in ("moe_gate", "moe_up") for j in (0, 4)]
                view = lambda c: c.raw()[0].rearrange("p (j k n) -> p j k n", j=4, k=8)
                X = lambda k: xs[:, k, e_, :, :]
                if nside == 2:
                    bg, psg, tg = B.take()
                    bu, psu, tu = B.take()
                    for ps, bt, cc in ((psg, tg, cs_[0:2]), (psu, tu, cs_[2:4])):
                        vs = [view(c) for c in cc]
                        for k in range(8):
                            for h in range(2):
                                Q.mm(ps[64 * h:64 * h + 64, :].rearrange("p (j n) -> p j n", j=4), X(k), vs[h][:, :, k, :],
                                     k == 0, k == 7, (cc[h].raw()[1], bt) + tx)
                        pt = Q.pe_done()
                        for c in cc:
                            c.done(pt)
                        if ps is psg:
                            ta = Q.a(lambda e: e.activation(gat[i2], psg[:, :], ACT.Silu), pt)
                            B.free(bg, ta)
                    tv = Q.v(lambda e: e.tensor_tensor(hid[i2], psu[:, :], gat[i2], ALU.mult), pt, ta)
                    B.free(bu, tv)
                    rows = slice(0, 128)
                else:
                    b, ps, bt = B.take()
                    vs = [view(c) for c in cs_]
                    for k in range(8):
                        for h in range(4):
                            Q.mm(ps[32 * h:32 * h + 32, :].rearrange("p (j n) -> p j n", j=4), X(k), vs[h][:, :, k, :],
                                 k == 0, k == 7, (cs_[h].raw()[1], bt) + tx)
                    pt = Q.pe_done()
                    for c in cs_:
                        c.done(pt)
                    ta = Q.a(lambda e: e.activation(gat[i2][64:128, :], ps[0:64, :], ACT.Silu), pt)
                    tv = Q.v(lambda e: e.tensor_tensor(hid[i2][64:128, :], ps[64:128, :], gat[i2][64:128, :], ALU.mult), pt, ta)
                    B.free(b, tv)
                    rows = slice(64, 128)
                r = 2 * w
                b, ps, bt = B.take()
                for j in range(4):
                    Q.tr(ps[:, j * r:(j + 1) * r], hid[i2][rows, j * 128:(j + 1) * 128], ident[rows, rows], (bt, tv))
                t_aT = Q.a(lambda e: e.activation(aT[i2][:, 0:4 * r], ps[:, 0:4 * r], ACT.Copy), Q.pe_done(), free_a[i2])
                B.free(b, t_aT)
                cd = [W.ask("moe_down", (l, e_), j, 4, 8, "raw") for j in (0, 4)]
                vs = [view(c) for c in cd]
                b, ps, bt = B.take()
                for k in range(8):
                    lhs = aT[i2][:, (k % 4) * r + (k // 4) * w:(k % 4) * r + (k // 4) * w + w]
                    for h in range(2):
                        Q.mm(ps[w * h:w * h + w, :].rearrange("p (j n) -> p j n", j=4), lhs, vs[h][:, :, k, :],
                             k == 0, k == 7, (cd[h].raw()[1], bt, t_aT))
                pt = Q.pe_done()
                free_a[i2] = pt
                for c in cd:
                    c.done(pt)
                yo = slice(32 * i4, 32 * i4 + 32)
                for h in range(2):
                    for s in range(nside):
                        o = w * h + 32 * s
                        if h:
                            t1 = Q.a(lambda e: e.activation(Y[s][yo, h * 512:(h + 1) * 512], ps[o:o + 32, :], ACT.Copy), pt, y_free[0], link=False)
                        else:
                            t2 = Q.v(lambda e: e.tensor_copy(Y[s][yo, h * 512:(h + 1) * 512], ps[o:o + 32, :]), pt, y_free[0], link=False)
                y_tok[0] = (t1, t2)
                Q.v(lambda e: e.memset(dummy, 0.0), t1)
                B.free(b, Q.last("dve"))
                if i4 == 3:
                    eg = e_ // 4
                    for s in range(nside):
                        for k in range(8):
                            if k % 2 == 0:
                                b, ps, bt = B.take()
                            o = (k % 2) * 256
                            Q.mm(ps[:, o:o + 256], Y[s][:, k * 128:(k + 1) * 128], PgT[:, s, eg, :], True, True, (bt, t1, t2))
                            if k % 2:
                                pt = Q.pe_done()
                                for kk in (k - 1, k):
                                    tv = Q.v(lambda e: e.scalar_tensor_tensor(
                                        src[s][:, kk, :], ps[:, (kk % 2) * 256:(kk % 2) * 256 + 256], mod(l, 5, s)[:, kk:kk + 1],
                                        src[s][:, kk, :], ALU.mult, ALU.add), pt, link=False)
                                if e_ == NE - 1 and l == 0:
                                    square(src[s], k - 1, 2, tv, s)
                                elif e_ == NE - 1:
                                    o = slice((k - 1) * 256, (k + 1) * 256)
                                    Q.dma("sp", out_dram[:, o], xT[:, o], s_out, (tv,))
                                B.free(b, tv)
                    y_free[0] = Q.pe_done()
            if not dry:
                W.idle = [s for s in W.idle if s.sem not in [f"slot{RING + i}" for i in range(MORE)]]
        t_ctx = None
        y_free, y_tok = [None], [None]

        def open_parts(ph):
            W.WH = open_area(ph, "WH", NB * 1024, F32R)[:, :].rearrange("p (b f) -> p b f", b=NB)
            W.WL = open_area(ph, "WL", NB * 1024, F32R)[:, :].rearrange("p (b f) -> p b f", b=NB)
            W.part_free = [tuple(lasts())] * NB

        steps = [even, lambda *a: ffn(*a, 0), lambda *a: ple(*a, 0), odd, lambda *a: ffn(*a, 1), lambda *a: ple(*a, 1)]
        with ExitStack() as first:
            open_parts(first)
            nH, nL = hl(first, 8)
            for i, st_ in enumerate(steps):
                if i == 4:
                    t_ctx = Q.dma("pool", cT[:, :], dr["ctxT"], s_cT, tuple(lasts()))
                if i == 5:
                    for j in range(0, 8, 2):
                        square(c8, j, 2, t_ctx, 1)
                with ExitStack() as ph:
                    st_(ph, nH, nL)
            while ada_n[0] < 24 or ada_late:
                fill(1)
        for l in range(2):
            with ExitStack() as ph:
                open_parts(ph)
                mixer2(ph, l)
            with ExitStack() as ph:
                moe(ph, l)
        if dry:
            return W.asked

        nc.sync.wait_ge(Q.sem[s_out], Q.count[s_out])


def constants():
    f = np.float32
    i = np.arange(128)
    c = {}
    c["ident"] = np.eye(128, dtype=f)
    c["eps"] = np.full((128, 1), EPS, f)
    c["ones"] = np.ones((128, 128), f)
    inv = []
    for dim in (64, 32):
        e = np.arange(0, dim, 2, dtype=f) / f(dim)
        inv.append((1.0 / np.power(f(10000.0), e)).astype(f))
    c["invf"] = np.tile(np.concatenate(inv)[None, :], (128, 1))
    c["tri"] = np.where(i[None, :] <= i[:, None], 0.0, -BIG).astype(f)
    c["iota"] = np.tile(np.arange(32, dtype=f)[None, :], (128, 1))
    t = np.arange(256)
    inv2 = 10000.0 ** (-np.arange(0, 64, 2, dtype=np.float64) / 64)
    ang = np.stack([(t // 64)[:, None] * inv2, (t % 64)[:, None] * inv2], 1)
    ang = np.repeat(ang[:, :, None, :], 2, 2).reshape(2, 128, 128)
    c["rcos"] = np.cos(ang).transpose(1, 0, 2).reshape(128, 256).astype(f)
    c["rsin"] = np.sin(ang).transpose(1, 0, 2).reshape(128, 256).astype(f)
    lv = []
    for l in range(6):
        b = 1 << l
        same = (i[:, None] // (2 * b)) == (i[None, :] // (2 * b))
        lv.append((same & ((i[:, None] // b) % 2 == 0) & ((i[None, :] // b) % 2 == 1)).astype(f))
    c["levels"] = np.concatenate(lv, 1)
    same = (i[:, None] // 64) == (i[None, :] // 64)
    c["cumT"] = (same & (i[:, None] <= i[None, :])).astype(f)
    c["lastT"] = (same & (i[:, None] % 64 == 63)).astype(f)
    c["sel"] = np.concatenate([np.tile((i == 63 + 64 * j).astype(f)[:, None], (1, 128)) for j in range(2)], 1)
    c["dmask"] = np.where(same & (i[None, :] <= i[:, None]), 0.0, BIG).astype(f)
    n = np.arange(256)
    a = 2 * np.pi * ((n[:, None] * n[None, :]) % 256) / 256
    cs = np.concatenate([np.cos(a), np.sin(a)], 1) / 16.0
    cs = cs.reshape(2, 128, 512).transpose(1, 0, 2).reshape(128, 1024)
    d = np.arange(64)
    b = 2 * np.pi * ((d[:, None] * d[None, :]) % 64) / 64
    bd = np.zeros((128, 256))
    for k in range(2):
        bd[64 * k:64 * k + 64, 64 * k:64 * k + 64] = np.cos(b) / 8.0
        bd[64 * k:64 * k + 64, 128 + 64 * k:128 + 64 * k + 64] = -np.sin(b) / 8.0
    dft = np.concatenate([cs, bd], 1).astype(f)
    pa = []
    for win in (2, 4, 8, 16):
        lo = np.clip(n - win // 2, 0, 256)
        hi = np.clip(n + win // 2, 0, 256)
        s = n[:, None]
        m = ((s >= lo[None, :]) & (s < hi[None, :])) / (hi - lo)[None, :].astype(np.float64) - np.eye(256)
        pa.append(m.reshape(2, 128, 256).transpose(1, 0, 2).reshape(128, 512))
    return c, dft, np.concatenate(pa, 1).astype(f)


def layout(a):
    cat, asc = np.concatenate, np.ascontiguousarray

    def blocks(w):
        lead = w.shape[:-2]
        k, n = w.shape[-2:]
        w = w.reshape(*lead, k // 128, 128, n // 128, 128)
        r = len(lead)
        w = w.transpose(*range(r), r + 2, r + 1, r, r + 3)
        return asc(w.reshape(*lead, n // 128, 128, k))

    def pad(w):
        return cat([w, np.zeros((w.shape[0], -w.shape[1] % 128), w.dtype)], 1)

    def featT(x):
        t, k = x.shape
        return asc(x.T.reshape(k // 128, 128, t).transpose(1, 0, 2).reshape(128, -1))

    def cols(v):
        v = v.reshape(-1, 128)
        return v.T

    def rows(v):
        return np.broadcast_to(v.reshape(1, -1), (128, v.size))

    const, dft, poolA = constants()
    s = dict(const)
    s["norm_mix"] = cols(a["norm_mix_g"])
    s["norm_ffn"] = cols(a["norm_ffn_g"])
    s["ple_post"] = cols(a["ple_post_norm_g"])
    s["ple_norm"] = cols(a["ple_norm_g"])
    s["ev_conv"] = a["ev_conv_w"][0].reshape(3, 4, 128).transpose(2, 1, 0).reshape(128, 12)
    s["od_conv"] = a["od_conv_w"][0].reshape(4, 24, 128).transpose(2, 1, 0).reshape(128, 96)
    s["ev_qg"] = rows(a["ev_q_norm_g"])
    s["ev_kg"] = rows(a["ev_k_norm_g"])
    s["ln_g"] = rows(a["ev_ik_ln_g"])
    s["ln_b"] = rows(a["ev_ik_ln_b"])
    s["o_g"] = rows(a["od_o_norm_g"])
    s["a_log"] = rows(a["od_a_log"])
    s["dt_bias"] = rows(a["od_dt_bias"])
    s["c2"] = np.stack([cols(a["c_2"]), cols(a["c_ctx_2"])], 2).reshape(128, 16)
    s["ada_b"] = cols(a["ada_b_2"])
    s["n1"] = cols(a["norm1_g_2"])
    s["n2"] = cols(a["norm2_g_2"])
    s["pool_scale"] = cols(a["pool_scale_2"])
    s["qg"] = rows(a["q_norm_g_2"])
    s["kg"] = rows(a["k_norm_g_2"])
    s["w_pool"] = a["w_pool_2"].reshape(2, 2, 128, 64).transpose(2, 0, 1, 3).reshape(128, 256)
    s["w_router"] = a["w_router_2"].reshape(2, 8, 128, 16).transpose(2, 0, 1, 3).reshape(128, 256)
    small = cat([np.asarray(s[n]).reshape(128, w) for n, w in SMALL], 1)
    ev, od = a["ev_w_in"][0], a["od_w_in"][0]
    return {
        "small": asc(small), "xT": featT(a["x"][0]), "ctxT": featT(a["ctx_2"][0]),
        "posT": asc(a["positions"].reshape(2, 128).T), "dft": dft, "poolA": poolA,
        "pT": asc(np.stack([featT(a["p"][l, 0]) for l in range(2)])),
        "ev_in": blocks(pad(ev)), "ev_out": blocks(a["ev_w_out"][0]),
        "od_in": blocks(pad(od)), "od_out": blocks(a["od_w_out"][0].reshape(2, 512, 1024)),
        "ffn_gate": blocks(a["ffn_w_gate"]), "ffn_up": blocks(a["ffn_w_up"]), "ffn_down": blocks(a["ffn_w_down"]),
        "ple_proj": blocks(a["ple_w_proj"]), "ple_gate": blocks(a["ple_w_gate"]),
        "ada": blocks(a["ada_w_2"]), "w_in": blocks(a["w_in_2"]), "w_out": blocks(a["w_out_2"]),
        "w_four": blocks(a["w_fourier_2"]),
        "moe_gate": blocks(a["w_gate_2"]), "moe_up": blocks(a["w_up_2"]), "moe_down": blocks(a["w_down_2"]),
    }


def kernel(**inputs):
    import numpy as _np
    import concourse.bacc as _bacc
    from concourse import mybir as _mybir
    from concourse.bass_utils import run_bass_kernel_spmd as _run

    arrays = layout({k: _np.asarray(v) for k, v in inputs.items()})
    plan = None
    for dry in (True, False):
        nc = _bacc.Bacc("TRN2", target_bir_lowering=False, num_devices=1)
        dr = {n: nc.dram_tensor(n, v.shape, _mybir.dt.from_np(v.dtype), kind="ExternalInput").ap() for n, v in arrays.items()}
        out = nc.dram_tensor("out", (128, 2048), _mybir.dt.float32, kind="ExternalOutput").ap()
        plan = program(nc, dr, out, plan, dry)
    r = _run(nc, [arrays], core_ids=[0])
    o = r.results[0]["out"].reshape(128, 8, 256)
    return _np.ascontiguousarray(o.transpose(2, 1, 0).reshape(1, 256, 1024))
```
